# Optimizing a Trainium2 kernel written in Bass

```python
import math
import jax, jax.numpy as jnp
from jax import lax
import numpy as np

D_MODEL = 1024
BATCH = 1
SEQ = 512
DEPTH = 1
DEC_BATCH = 8
DEC_SEQ = 8
PAST_LEN = 1024
PAGE_SIZE = 128

HEAD_DIM = 64
ATT_WIDTH = D_MODEL // 2
RWKV_WIDTH = D_MODEL - ATT_WIDTH
N_Q_HEADS = ATT_WIDTH // HEAD_DIM
N_KV_HEADS = 2
Q_PER_KV = N_Q_HEADS // N_KV_HEADS
KV_WIDTH = N_KV_HEADS * HEAD_DIM
WINDOW = 128
ATT_BLOCK = WINDOW
ATT_SCALE = HEAD_DIM ** -0.5
N_RWKV_HEADS = RWKV_WIDTH // HEAD_DIM
D_DECAY_LORA = 64
D_AAA_LORA = 64
D_GATE_LORA = 128
D_MV_LORA = 32
RWKV_SIZES = (RWKV_WIDTH, D_DECAY_LORA, RWKV_WIDTH, RWKV_WIDTH, D_AAA_LORA, D_GATE_LORA)
N_ATT_COLS = ATT_WIDTH + 2 * KV_WIDTH
N_RWKV_COLS = sum(RWKV_SIZES)
N_IN_COLS = N_ATT_COLS + N_RWKV_COLS
DECAY_SCALE = math.exp(-0.5)
GN_EPS = 64e-5
LN_EPS = 1e-5
N_EXPERTS = 16
N_EXPERT_GROUPS = 4
EXPERTS_PER_GROUP = N_EXPERTS // N_EXPERT_GROUPS
TOP_K = 2
EXPERT_FF = D_MODEL // 2
ALPHA = (2 * DEPTH) ** 0.25
BETA = (8 * DEPTH) ** -0.25

kernel_name = "hymba_swa_sink_rwkv7_grouped_moe_step"

F32 = jnp.float32

def _split(t, sizes):
    out, off = [], 0
    for s in sizes:
        out.append(t[..., off:off + s])
        off += s
    return out

def layer_norm(x, g, b):
    xf = x.astype(F32)
    mu = xf.mean(-1, keepdims=True)
    var = jnp.mean(jnp.square(xf - mu), -1, keepdims=True)
    return ((xf - mu) * lax.rsqrt(var + LN_EPS) * g + b).astype(x.dtype)

def sink_softmax(s, mask, sink):
    s = jnp.where(mask, s, -jnp.inf)
    sink = sink.astype(F32)
    m = jnp.maximum(s.max(-1, keepdims=True), sink)
    e = jnp.exp(s - m)
    return e / (e.sum(-1, keepdims=True) + jnp.exp(sink - m))

def window_attention_banded(q, k, v, sinks):
    B, T, H, G, Dh = q.shape
    L = ATT_BLOCK
    nb = T // L
    qb = q.reshape(B, nb, L, H, G, Dh)
    kb = k.reshape(B, nb, L, H, Dh)
    vb = v.reshape(B, nb, L, H, Dh)
    pad = jnp.zeros_like(kb[:, :1])
    kw = jnp.concatenate([jnp.concatenate([pad, kb[:, :-1]], 1), kb], axis=2)
    vw = jnp.concatenate([jnp.concatenate([pad, vb[:, :-1]], 1), vb], axis=2)
    s = jnp.einsum("bnqhgd,bnkhd->bnhgqk", qb, kw).astype(F32) * ATT_SCALE
    qi = jnp.arange(L)[:, None]
    kj = jnp.arange(2 * L)[None, :]
    diff = qi + L - kj
    band = (diff >= 0) & (diff < WINDOW)
    exists = (jnp.arange(nb)[:, None, None] * L + kj[None] - L) >= 0
    mask = band[None] & exists
    p = sink_softmax(s, mask[None, :, None, None], sinks[:, :, None, None])
    o = jnp.einsum("bnhgqk,bnkhd->bnqhgd", p.astype(v.dtype), vw)
    return o.reshape(B, T, H * G * Dh)

def window_attention_cached(q, k, v, ck, cv, sinks):
    B, S, H, G, Dh = q.shape
    W = ck.shape[1]
    kall = jnp.concatenate([ck.astype(k.dtype), k], axis=1)
    vall = jnp.concatenate([cv.astype(v.dtype), v], axis=1)
    s = jnp.einsum("bqhgd,bkhd->bhgqk", q, kall).astype(F32) * ATT_SCALE
    kpos = jnp.concatenate([jnp.arange(W) - W, jnp.arange(S)])
    qpos = jnp.arange(S)
    diff = qpos[:, None] - kpos[None, :]
    mask = (diff >= 0) & (diff < WINDOW)
    p = sink_softmax(s, mask, sinks[:, :, None, None])
    o = jnp.einsum("bhgqk,bkhd->bqhgd", p.astype(v.dtype), vall)
    return o.reshape(B, S, H * G * Dh)

def wkv7_scan(state, r, w, k, v, a, b):
    def step(S, inp):
        r_t, w_t, k_t, v_t, a_t, b_t = inp
        sa = jnp.einsum("bhij,bhj->bhi", S, a_t)
        S = S * w_t[:, :, None, :] + sa[..., None] * b_t[:, :, None, :] + v_t[..., None] * k_t[:, :, None, :]
        return S, jnp.einsum("bhij,bhj->bhi", S, r_t)
    xs = tuple(jnp.moveaxis(t.astype(F32), 1, 0) for t in (r, w, k, v, a, b))
    S, ys = lax.scan(step, state.astype(F32), xs)
    return S, jnp.moveaxis(ys, 0, 1)

def rwkv7_time_mix(rw, state, v_first, wt, l):
    B, T, _ = rw.shape
    sizes = RWKV_SIZES + ((D_MV_LORA,) if l > 0 else ())
    parts = [p.astype(F32) for p in _split(rw, sizes)]
    r, wl, k, v, al, gl = parts[:6]
    decay = jnp.exp(-DECAY_SCALE * jax.nn.sigmoid(wt["decay_w0"][l] + jnp.tanh(wl) @ wt["decay_w2"][l]))
    a = jax.nn.sigmoid(wt["aaa_a0"][l] + al @ wt["aaa_a2"][l])
    g = jax.nn.sigmoid(gl) @ wt["gate_g2"][l]
    if l == 0:
        v_first = v
    else:
        v = v + (v_first - v) * jax.nn.sigmoid(wt["vres_v0"][l - 1] + parts[6] @ wt["vres_v2"][l - 1])
    heads = lambda t: t.reshape(B, T, N_RWKV_HEADS, HEAD_DIM)
    kk = heads(k * wt["k_k"][l])
    kk = kk / jnp.maximum(jnp.sqrt(jnp.sum(kk * kk, -1, keepdims=True)), 1e-12)
    k = k * (1.0 + (a - 1.0) * wt["k_a"][l])
    rh, wh, kh, vh, ah = heads(r), heads(decay), heads(k), heads(v), heads(a)
    new_state, y = wkv7_scan(state, rh, wh, kh, vh, -kk, kk * ah)
    mu = y.mean(-1, keepdims=True)
    var = jnp.mean(jnp.square(y - mu), -1, keepdims=True)
    y = ((y - mu) * lax.rsqrt(var + GN_EPS)).reshape(B, T, RWKV_WIDTH) * wt["gn_g"][l] + wt["gn_b"][l]
    bonus = jnp.sum(rh * kh * wt["r_k"][l], -1, keepdims=True) * vh
    out = (y + bonus.reshape(B, T, RWKV_WIDTH)) * g
    return out, new_state, v_first

def routed_moe(x, w_router, router_bias, w_gate, w_up, w_down):
    logits = jnp.einsum("btd,de->bte", x, w_router).astype(F32)
    probs = jax.nn.softmax(logits, -1)
    sel = (probs + router_bias.astype(F32)).reshape(*probs.shape[:-1], N_EXPERT_GROUPS, EXPERTS_PER_GROUP)
    group_score = lax.top_k(sel, TOP_K)[0].sum(-1)
    best = jnp.argmax(group_score, -1)
    in_group = jnp.sum(sel * jax.nn.one_hot(best, N_EXPERT_GROUPS, dtype=F32)[..., None], -2)
    _, local = lax.top_k(in_group, TOP_K)
    idx = best[..., None] * EXPERTS_PER_GROUP + local
    w_sel = jnp.take_along_axis(probs, idx, -1)
    w_sel = w_sel / w_sel.sum(-1, keepdims=True)
    gates = jnp.sum(jax.nn.one_hot(idx, N_EXPERTS, dtype=F32) * w_sel[..., None], -2)
    h = jax.nn.silu(jnp.einsum("btd,edf->btef", x, w_gate)) * jnp.einsum("btd,edf->btef", x, w_up)
    h = h * gates[..., None].astype(h.dtype)
    return jnp.einsum("btef,efd->btd", h, w_down).astype(x.dtype)

def _trunk(x, shift_prev, cache_k, cache_v, wkv_prev, wt):
    decode = cache_k is not None
    B, T, _ = x.shape
    new_k, new_v, new_wkv, new_shift = [], [], [], []
    v_first = None
    for l in range(DEPTH):
        if l == 0:
            w_cat, mu = wt["w_in"][0], wt["mu_rwkv"][0]
        else:
            w_cat = jnp.concatenate([wt["w_in"][l], wt["w_vres_in"][l - 1]], axis=1)
            mu = jnp.concatenate([wt["mu_rwkv"][l], wt["mu_vres"][l - 1]])
        x_ext = jnp.concatenate([shift_prev[l][:, None].astype(x.dtype), x], axis=1)
        proj = jnp.einsum("btd,dc->btc", x_ext, w_cat)
        att_in = proj[:, 1:, :N_ATT_COLS]
        rw_cur = proj[:, 1:, N_ATT_COLS:]
        rw_prev = proj[:, :-1, N_ATT_COLS:]
        rw = rw_cur + (rw_prev - rw_cur) * mu
        new_shift.append(x[:, -1])
        q, k, v = _split(att_in, (ATT_WIDTH, KV_WIDTH, KV_WIDTH))
        q = q.reshape(B, T, N_KV_HEADS, Q_PER_KV, HEAD_DIM)
        k = k.reshape(B, T, N_KV_HEADS, HEAD_DIM)
        v = v.reshape(B, T, N_KV_HEADS, HEAD_DIM)
        sinks = wt["sinks"][l].reshape(N_KV_HEADS, Q_PER_KV)
        if decode:
            att = window_attention_cached(q, k, v, cache_k[l], cache_v[l], sinks)
            new_k.append(k)
            new_v.append(v)
        else:
            att = window_attention_banded(q, k, v, sinks)
            new_k.append(k[:, -WINDOW:])
            new_v.append(v[:, -WINDOW:])
        rw_out, wkv_l, v_first = rwkv7_time_mix(rw, wkv_prev[l], v_first, wt, l)
        new_wkv.append(wkv_l)
        mixed = jnp.concatenate([att.astype(x.dtype), rw_out.astype(x.dtype)], -1) @ wt["w_o"][l]
        x = layer_norm(ALPHA * x + mixed, wt["ln1_g"][l], wt["ln1_b"][l])
        ffn = routed_moe(x, wt["w_router"], wt["router_bias"], wt["w_gate"][l], wt["w_up"][l], wt["w_down"][l])
        x = layer_norm(ALPHA * x + ffn, wt["ln2_g"][l], wt["ln2_b"][l])
    return (x, jnp.stack(new_k), jnp.stack(new_v), jnp.stack(new_wkv), jnp.stack(new_shift))

def setup_inputs(seed: int = 0) -> dict:
    key = jax.random.key(seed)
    ks = iter(jax.random.split(key, 48))
    nrm = lambda shape, scale: jax.random.normal(next(ks), shape, F32) * scale
    unif = lambda shape, lo, hi: jax.random.uniform(next(ks), shape, F32, lo, hi)
    win_buf = min(WINDOW, PAST_LEN)
    D = D_MODEL
    return {
        "x_prompt": nrm((BATCH, SEQ, D), 1.0),
        "x_sample": nrm((DEC_BATCH, DEC_SEQ, D), 1.0),
        "cache_k": nrm((DEPTH, DEC_BATCH, win_buf, N_KV_HEADS, HEAD_DIM), 1.0),
        "cache_v": nrm((DEPTH, DEC_BATCH, win_buf, N_KV_HEADS, HEAD_DIM), 1.0),
        "state_wkv": nrm((DEPTH, DEC_BATCH, N_RWKV_HEADS, HEAD_DIM, HEAD_DIM), 0.3),
        "state_shift": nrm((DEPTH, DEC_BATCH, D), 1.0),
        "w_in": nrm((DEPTH, D, N_IN_COLS), D ** -0.5),
        "w_vres_in": nrm((DEPTH - 1, D, D_MV_LORA), D ** -0.5),
        "mu_rwkv": unif((DEPTH, N_RWKV_COLS), 0.1, 0.9),
        "mu_vres": unif((DEPTH - 1, D_MV_LORA), 0.1, 0.9),
        "sinks": nrm((DEPTH, N_Q_HEADS), 0.5),
        "decay_w0": unif((DEPTH, RWKV_WIDTH), -4.0, 2.0),
        "decay_w2": nrm((DEPTH, D_DECAY_LORA, RWKV_WIDTH), D_DECAY_LORA ** -0.5),
        "aaa_a0": nrm((DEPTH, RWKV_WIDTH), 0.5),
        "aaa_a2": nrm((DEPTH, D_AAA_LORA, RWKV_WIDTH), D_AAA_LORA ** -0.5),
        "vres_v0": nrm((DEPTH - 1, RWKV_WIDTH), 0.5),
        "vres_v2": nrm((DEPTH - 1, D_MV_LORA, RWKV_WIDTH), D_MV_LORA ** -0.5),
        "gate_g2": nrm((DEPTH, D_GATE_LORA, RWKV_WIDTH), D_GATE_LORA ** -0.5),
        "k_k": 0.85 + nrm((DEPTH, RWKV_WIDTH), 0.05),
        "k_a": 1.0 + nrm((DEPTH, RWKV_WIDTH), 0.05),
        "r_k": nrm((DEPTH, N_RWKV_HEADS, HEAD_DIM), 0.1),
        "gn_g": 1.0 + nrm((DEPTH, RWKV_WIDTH), 0.05),
        "gn_b": nrm((DEPTH, RWKV_WIDTH), 0.02),
        "w_o": nrm((DEPTH, D, D), BETA * D ** -0.5),
        "ln1_g": 1.0 + nrm((DEPTH, D), 0.05),
        "ln1_b": nrm((DEPTH, D), 0.02),
        "w_router": nrm((D, N_EXPERTS), D ** -0.5),
        "router_bias": nrm((N_EXPERTS,), 0.01),
        "w_gate": nrm((DEPTH, N_EXPERTS, D, EXPERT_FF), D ** -0.5),
        "w_up": nrm((DEPTH, N_EXPERTS, D, EXPERT_FF), D ** -0.5),
        "w_down": nrm((DEPTH, N_EXPERTS, EXPERT_FF, D), BETA * EXPERT_FF ** -0.5),
        "ln2_g": 1.0 + nrm((DEPTH, D), 0.05),
        "ln2_b": nrm((DEPTH, D), 0.02),
    }

def reference(x_prompt, x_sample, cache_k, cache_v, state_wkv, state_shift,
              w_in, w_vres_in, mu_rwkv, mu_vres, sinks, decay_w0, decay_w2,
              aaa_a0, aaa_a2, vres_v0, vres_v2, gate_g2, k_k, k_a, r_k, gn_g, gn_b,
              w_o, ln1_g, ln1_b, w_router, router_bias, w_gate, w_up, w_down, ln2_g, ln2_b):
    wt = dict(w_in=w_in, w_vres_in=w_vres_in, mu_rwkv=mu_rwkv, mu_vres=mu_vres, sinks=sinks,
              decay_w0=decay_w0, decay_w2=decay_w2, aaa_a0=aaa_a0, aaa_a2=aaa_a2,
              vres_v0=vres_v0, vres_v2=vres_v2, gate_g2=gate_g2, k_k=k_k, k_a=k_a, r_k=r_k,
              gn_g=gn_g, gn_b=gn_b, w_o=w_o, ln1_g=ln1_g, ln1_b=ln1_b, w_router=w_router,
              router_bias=router_bias, w_gate=w_gate, w_up=w_up, w_down=w_down,
              ln2_g=ln2_g, ln2_b=ln2_b)
    b_p = x_prompt.shape[0]
    zero_shift = jnp.zeros((DEPTH, b_p, D_MODEL), x_prompt.dtype)
    zero_wkv = jnp.zeros((DEPTH, b_p, N_RWKV_HEADS, HEAD_DIM, HEAD_DIM), F32)
    y_prompt, k_prompt, v_prompt, wkv_prompt, shift_prompt = _trunk(
        x_prompt, zero_shift, None, None, zero_wkv, wt)
    y_sample, k_sample, v_sample, wkv_sample, shift_sample = _trunk(
        x_sample, state_shift, cache_k, cache_v, state_wkv, wt)
    return (y_prompt, y_sample, k_prompt, v_prompt, wkv_prompt, shift_prompt,
            k_sample, v_sample, wkv_sample, shift_sample)


_drawn_inputs = setup_inputs


def setup_inputs(seed=0):
    import zlib

    import numpy as np

    out = dict(_drawn_inputs(seed))
    spreads = {}
    factors = {'sinks': 8.0, 'gn_b': 5.409, 'ln2_b': 2.746}
    for name, (base, spread) in spreads.items():
        noise = np.random.default_rng([zlib.crc32(name.encode()), seed]).standard_normal(out[name].shape)
        drawn = base * np.exp(spread * noise) if base else spread * noise
        out[name] = __import__('jax').numpy.asarray(drawn.astype(out[name].dtype))
    for name, factor in factors.items():
        out[name] = (out[name] * factor).astype(out[name].dtype)
    return out
```

```python
from contextlib import ExitStack
import math

import numpy as np

import concourse.bass as bass
from concourse import mybir

ALU = mybir.AluOpType
ACT = mybir.ActivationFunctionType
AX = mybir.AxisListType.X
F32 = mybir.dt.float32
I32 = mybir.dt.int32

P = 128
D = 1024
KT = D // P
NP_ = 512
NS = 64
NB = 8
TS = NS // NB
NT = NP_ + NS
TILES = NP_ // P
PAIRS = 4
HD = 64
CHUNK = 64
CHUNKS = NP_ // CHUNK
WIN = 128
E = 16
FF = 512
FT = FF // P
CAP = 128
OVER = 2 * NT // (CAP + 1)
BLOCKS = E + OVER
SLOTS = BLOCKS * CAP
COLT = 20
RING = 6
RANKB = 1
ALPHA = 2.0 ** 0.25
DECAY_SCALE = math.exp(-0.5)
GN_EPS = 64e-5
LN_EPS = 1e-5
NEG = -1e30
DEBUG = 1
ATT_SCALE = HD ** -0.5

MU, OMU, W0, A0, KK_, KA, RK, GNG, GNB, SINK, SINKD, RB, NPV = (
    0, 14, 28, 32, 36, 40, 44, 48, 52, 56, 64, 66, 82)


def constant_table():
    i = np.arange(P)
    s, t = i[:, None], i[None, :]
    t_ = {}
    t_["ident"] = np.eye(P)
    for tag, n, c in (("", P, CHUNK), ("_s", NS, TS)):
        same = (s // c == t // c)[:, :n]
        up = np.concatenate([(same & (s <= t[:, :n])), (same & (s < t[:, :n]))] * 2, 1).astype(float)
        t_["upper" + tag] = up
        t_["lower" + tag] = (same & (t[:, :n] < s)).astype(float)
    lev = []
    for m in (1, 2, 4, 8, 16, 32):
        lev.append(((s // (2 * m) == t // (2 * m)) & (s // m % 2 == 1) & (t // m % 2 == 0)).astype(float))
    t_["level"] = np.concatenate(lev, 1)
    kj = np.arange(2 * P)[None, :]
    diff = s + P - kj
    band = (diff >= 0) & (diff < WIN)
    t_["band"] = np.where(np.concatenate([band & (kj >= P), band], 1), 0.0, NEG)
    row = np.arange(P)
    rb, rt = row // 32, row % 8
    dm = np.full((P, 2, 192), NEG)
    w = np.arange(WIN)
    for b2 in range(2):
        dm[:, b2, :WIN] = np.where(w[None, :] > rt[:, None], 0.0, NEG)
        c = np.arange(NS)
        ok = (c[None, :] // TS == (b2 * 4 + rb)[:, None]) & (c[None, :] % TS <= rt[:, None])
        dm[:, b2, WIN:] = np.where(ok, 0.0, NEG)
    t_["bandd"] = dm.reshape(P, 384)
    t_["ident2"] = (s % HD == np.arange(HD)[None, :]).astype(float)
    t_["blk"] = (s // HD == t // HD).astype(float)
    t_["before"] = (s < t).astype(float)
    t_["ones"] = np.ones((P, P))
    t_["reset"] = np.ones((P, NT))
    t_["reset"][:, 0:NP_:CHUNK] = 0
    t_["reset"][:, NP_::TS] = 0
    t_["batch"] = (s // TS == np.arange(NB)[None, :]).astype(float)
    t_["rank"] = np.tile(np.arange(float(P)), (P, 1))
    t_["tokf"] = (np.arange(5)[None, :] * P + i[:, None]).astype(float)
    t_["iota4"] = np.tile(np.arange(4.0), (P, 1))
    t_["slot0"] = np.tile(np.arange(E) * float(CAP), (P, 1))
    t_["item"] = np.tile(np.arange(float(OVER)), (P, 1))
    t_["tri"] = np.tile((np.arange(E)[None, :] < np.arange(E)[:, None]).astype(float).reshape(1, -1), (P, 1))
    tok = np.arange(5)[None, :] * P + i[:, None]
    t_["valid"] = (tok < NT).astype(float)
    t_["spare"] = (tok >= NT).astype(float)
    return {k: np.ascontiguousarray(v, dtype=np.float32) for k, v in t_.items()}


def constant_layout():
    off, at = 0, {}
    for k, v in constant_table().items():
        at[k] = (off, v.shape[1])
        off += v.shape[1]
    return at, off


CAT, NCONST = constant_layout()

OUTS = [("y_prompt", (1, NP_, D)), ("y_sample", (NB, TS, D)), ("k_prompt", (1, 1, WIN, 2, HD)),
        ("v_prompt", (1, 1, WIN, 2, HD)), ("wkv_prompt", (1, 1, 8, HD, HD)), ("shift_prompt", (1, 1, D)),
        ("k_sample", (1, NB, TS, 2, HD)), ("v_sample", (1, NB, TS, 2, HD)),
        ("wkv_sample", (1, NB, 8, HD, HD)), ("shift_sample", (1, NB, D))]


def hymba_step(nc, i_, o_):
    with ExitStack() as ctx:
        sems = {}

        def sem(name):
            if name not in sems:
                sems[name] = ctx.enter_context(nc.semaphore(name))
            return sems[name]

        top = [0]

        def take(n):
            top[0] += n
            return top[0] - n

        o_const, o_par = take(NCONST), take(NPV)
        o_xt, o_mixa, o_ring = take(KT * 584), take(4 * NT), take(8192)
        o_rwkv, o_u = take(7 * 4 * NT), take(12288)
        o_temp = take(6 * NT)
        o_mixtmp = take(2 * 592)
        arena = ctx.enter_context(nc.sbuf_tensor("arena", [P, top[0]], F32))

        def v2(off, n):
            return arena[:, off:off + n]

        def v3(off, a, b):
            return v2(off, a * b).rearrange("p (a b) -> p a b", b=b)

        def v4(off, a, b, c):
            return v2(off, a * b * c).rearrange("p (a b c) -> p a b c", b=b, c=c)

        def C(name):
            o, w = CAT[name]
            return v2(o_const + o, w)

        ident = C("ident")
        consts, par = v2(o_const, NCONST), v2(o_par, NPV)
        xT = v3(o_xt, KT, 584)
        mixA = v3(o_mixa, 4, NT)
        ring = v4(o_ring, RING, KT, P)
        xst = v3(o_ring + RING * KT * P, 2, D)
        R4, K4, V4, A4, B4, SG4, G4 = (v3(o_rwkv + n * 4 * NT, 4, NT) for n in range(7))
        WA, GL = A4[:, 0, :], A4[:, 1, :]
        u = o_u
        qT = v3(u, 4, NP_); u += 4 * NP_
        qTs = v4(u, NB, 4, TS); u += 4 * NS
        kT = v2(u, P + NP_); u += P + NP_
        kTs = v2(u, NS); u += NS
        vT = v2(u, NT); u += NT
        Vt = v3(u, 5, P); u += 5 * P
        Vs = v2(u, P); u += P
        Kt3 = v2(u, P); u += P
        Ks = v2(u, P); u += P
        kc = v3(u, NB, P); u += NB * P
        vc = v3(u, NB, P); u += NB * P
        kcT = v3(u, NB, P); u += NB * P
        Sb = v3(u, 2, 1024); u += 2048
        PT = v3(u, 2, 512); u += 1024
        LW = v2(u, 512); u += 512
        GW = v2(u, 512); u += 512
        assert u <= o_u + 12288
        PM, PI, SQ = (v3(o_temp + 2 * n * NT, 2, NT) for n in range(3))
        mixtmp = v3(o_mixtmp, 2, 592)
        u = o_u
        TOK = [v3(u + n * 512, 4, P) for n in range(4)]; u += 2048
        BG = [v2(u + n * 1024, 1024) for n in range(2)]; u += 2048
        KG = [v2(u + n * 1024, 1024) for n in range(2)]; u += 2048
        NM, X, XT, W1, RHS, GH = ([v2(u + (2 * k + n) * 512, 512) for n in range(2)] for k in range(6))
        rwkv7 = v3(o_rwkv, 7, 4 * NT)
        Z0 = v4(o_temp, 4, NB, HD)
        stage = [v2(o_temp + 2048, 1024), v2(o_mixtmp, 1024)]
        Zp = v4(o_xt + 4 * NT, 8, 4, HD)
        mixR = v3(o_xt, 4, NT)
        GTs = RHS[0][:, 0:256]
        wo = v3(o_ring, KT, D)
        ln1 = v3(o_xt + 4 * NT, 2, D)
        x1 = v3(o_rwkv + 24576, 5, D)
        xres = v3(o_rwkv + 24576 + 5 * D, 2, D)
        x1T = v3(o_mixtmp, KT, P)
        WG = [v3(o_rwkv + n * 4096, KT, FF) for n in range(2)]
        WU = [v3(o_rwkv + (2 + n) * 4096, KT, FF) for n in range(2)]
        WD = [v3(o_rwkv + (4 + n) * 4096, FT, D) for n in range(2)]
        u = o_xt
        xg = v3(u, 2, D); u += 2 * D
        xgT = [v3(u + n * D, KT, P) for n in range(2)]; u += 2 * D
        sg = v3(u, 2, FF); u += 2 * FF
        hh = v3(u, 2, FF); u += 2 * FF
        hT = [v3(u + n * FF, FT, P) for n in range(2)]; u += 2 * FF
        yst = v3(u, 2, D); u += 2 * D
        yab = v4(o_rwkv, 5, 2, D)
        ln2 = v3(u, 2, D); u += 2 * D

        def small(*dims):
            nonlocal u
            n = 1
            for d_ in dims:
                n *= d_
            u += n
            assert u <= o_ring + 8192 + 0
            return v2(u - n, n) if len(dims) == 1 else v3(u - n, *dims) if len(dims) == 2 else v4(u - n, *dims)

        wr = ctx.enter_context(nc.sbuf_tensor("wr", [P, KT, E], F32))[:, :, :]
        rt = ctx.enter_context(nc.sbuf_tensor("rt", [P, 5, E], F32))
        lnst = ctx.enter_context(nc.sbuf_tensor("lnst", [P, 2, 20], F32))
        ln_eps = ctx.enter_context(nc.sbuf_tensor("ln_eps", [P, 1], F32))[:, :]
        tokid = ctx.enter_context(nc.sbuf_tensor("tokid", [P, 5], I32))
        zidx = ctx.enter_context(nc.sbuf_tensor("zidx", [P, BLOCKS], I32))
        PR, SEL, CN, O1, O2, EQ, M1, M2, PO = (small(5, E) for _ in range(9))
        G1, G2, C1, SC, BGR, CNB = (small(5, 4) for _ in range(6))
        S5 = small(12, 5)
        NV, ST, B2, CT = (small(E) for _ in range(4))
        TR = small(E, E)
        IT = small(OVER, E)
        IV = small(2, 32)
        OH = [small(5, P) for _ in range(2)]
        TI = [small(5, E) for _ in range(2)]
        smalli = ctx.enter_context(nc.sbuf_tensor("smalli", [P, 10 + BLOCKS + 1 + OVER], I32))
        slot_i = smalli[:, 0:10].rearrange("p (a b) -> p a b", b=2)
        idx_i = smalli[:, 10:10 + BLOCKS]
        flag_i = smalli[:, 10 + BLOCKS:11 + BLOCKS]
        eid_i = smalli[:, 11 + BLOCKS:11 + BLOCKS + OVER]
        x1d = nc.dram_tensor("x1_rows", [NT, D], F32).ap()
        ysd = nc.dram_tensor("expert_rows", [SLOTS, D], F32).ap()
        idxd = nc.dram_tensor("slot_token", [SLOTS, 1], I32).ap()

        def trows(i):
            return P if i < 4 else NS
        att_st = ctx.enter_context(nc.sbuf_tensor("att_st", [P, 2, 8, 4], F32))
        gn_eps = ctx.enter_context(nc.sbuf_tensor("gn_eps", [P, 1], F32))[:, :]
        PL = ctx.enter_context(nc.sbuf_tensor("PL", [P, 4, 16], F32))

        ps = ctx.enter_context(nc.psum_tensor("ps", [P, 8, 512], F32))

        block = ctx.enter_context(nc.Block())

        ATT0, RW0 = 2, 8

        def mix_index(ct):
            return ct if ct < 2 else ct - 6

        def mix_dst(m):
            if m == 0:
                return WA
            if m == 1:
                return GL
            return (R4, K4, V4)[(m - 2) % 3][:, (m - 2) // 3, :]

        souts = [BG[0][:, 0:512], BG[0][:, 512:1024], BG[1][:, 0:512], BG[1][:, 512:1024],
                 KG[0][:, 0:512], KG[0][:, 512:1024], KG[1][:, 0:512], KG[1][:, 512:1024]]

        def rows(q):
            return P if q < 4 else NS

        def levels(q):
            return 5 if q < 4 else 2

        def unit(T4, q, u, r=slice(0, P)):
            return T4[r, q, u * P:(u + 1) * P] if q < 4 else T4[r, u, NP_:NT]

        def units(T4, q):
            return T4[:, q, 0:NP_].rearrange("p (u t) -> p u t", u=4) if q < 4 else T4[:, :, NP_:NT]

        def par_rows(p):
            return slice(64 * p, 64 * p + 64)

        class Tally:

            def __init__(self, eng):
                self.eng, self.n = eng, {}

            def up(self, ins, name):
                ins.then_inc(sem(name), 1)
                self.n[name] = self.n.get(name, 0) + 1

            def link(self, ins, name):
                self.up(ins, name)
                self.eng.wait_ge(sem(name), self.n[name])

        def wait_read(eng, p):
            if p < 0:
                return
            if ATT0 <= p < RW0:
                eng.wait_ge(sem("att_evac"), p - ATT0 + 1)
            else:
                eng.wait_ge(sem("mixed"), mix_index(p) + 1)

        @block.sync
        def _(sp):
            sp.dma_start(ident, i_["consts"][:, 0:P]).then_inc(sem("ld_first"), 16)
            sp.dma_start(par, i_["params"][:, :]).then_inc(sem("ld_first"), 16)

            def load_win(ct):
                if ct >= RING:
                    sp.wait_ge(sem("proj"), ct - RING + 1)
                sp.dma_start(ring[:, ct % RING, :, :], i_["win"][ct].rearrange("p (k c) -> p k c", c=P)) \
                  .then_inc(sem(f"win{ct % RING}"), 16)

            load_win(0)
            load_win(1)
            sp.wait_ge(sem("xt_ps"), 4)
            load_win(2)
            load_win(3)
            sp.wait_ge(sem("xt_ps"), 8)
            sp.dma_start(wr, i_["w_router"].rearrange("(k p) e -> p k e", p=P)).then_inc(sem("ld_lora"), 16)
            sp.dma_start(LW[0:64, :], i_["decay_w2"][0]).then_inc(sem("ld_lora"), 16)
            sp.dma_start(LW[64:128, :], i_["aaa_a2"][0]).then_inc(sem("ld_lora"), 16)
            sp.dma_start(GW, i_["gate_g2"][0]).then_inc(sem("ld_lora"), 16)
            load_win(4)
            load_win(5)
            sp.dma_start(v2(o_const + P, NCONST - P), i_["consts"][:, P:NCONST]).then_inc(sem("ld_const"), 16)
            sp.dma_start(kc, i_["cache_k"][0].rearrange("b w h d -> w b (h d)")).then_inc(sem("ld_cache"), 16)
            sp.dma_start(vc, i_["cache_v"][0].rearrange("b w h d -> w b (h d)")).then_inc(sem("ld_cache"), 16)
            for ct in range(RING, COLT):
                load_win(ct)
            sp.wait_ge(sem("proj"), COLT)
            sp.dma_start(wo.rearrange("p k c -> p (k c)"), i_["wo"][:, :]).then_inc(sem("ld_wo"), 16)
            sp.dma_start(o_["shift_prompt"][0], i_["x_prompt"][0, NP_ - 1:NP_, :]).then_inc(sem("out"), 16)
            sp.dma_start(o_["shift_sample"][0], i_["x_sample"][:, TS - 1, :]).then_inc(sem("out"), 16)
            sp.wait_ge(sem("kv_tok"), 2)
            sp.dma_start(o_["k_prompt"].rearrange("l b w h d -> (l b w) (h d)"), Kt3).then_inc(sem("kv_out"), 16)
            sp.dma_start(o_["v_prompt"].rearrange("l b w h d -> (l b w) (h d)"), Vt[:, 4, :]).then_inc(sem("kv_out"), 16)
            sp.dma_start(o_["k_sample"].rearrange("l b w h d -> (l b w) (h d)"), Ks[0:NS, :]).then_inc(sem("kv_out"), 16)
            sp.dma_start(o_["v_sample"].rearrange("l b w h d -> (l b w) (h d)"), Vs[0:NS, :]).then_inc(sem("kv_out"), 16)
            sp.wait_ge(sem("kv_out"), 64)
            for h in range(4):
                if h < 2:
                    sp.wait_ge(sem("bonus_read"), 4)
                    sp.wait_ge(sem("prep"), 4)
                else:
                    sp.wait_ge(sem("st_ps"), h - 1)
                sp.dma_start(stage[h % 2][0:HD, :].rearrange("v (b h k) -> v b h k", b=2, k=HD),
                             i_["state_wkv"][0, 2 * h:2 * h + 2].rearrange("b h v k -> v b h k")) \
                  .then_inc(sem(f"ld_st{h % 2}"), 16)
            sp.wait_ge(sem("so_ev"), 8)
            for b in range(NB):
                sp.dma_start(o_["wkv_sample"][0, b].rearrange("h v k -> v h k"),
                             souts[b][0:HD, :].rearrange("v (h k) -> v h k", k=HD)).then_inc(sem("st_out"), 16)
            sp.wait_ge(sem("so_ev"), NB + 1)
            sp.dma_start(o_["wkv_prompt"][0, 0].rearrange("h v k -> v h k"),
                         GH[1][0:HD, :].rearrange("v (h k) -> v h k", k=HD)).then_inc(sem("st_out"), 16)
            sp.wait_ge(sem("st_out"), 16 * (NB + 1))
            sp.wait_ge(sem("gn_out"), 4)
            for r_ in range(2):
                sp.dma_start(ln1[:, r_, :], i_[("ln1_g", "ln1_b")[r_]][0:1, :].to_broadcast([P, D])) \
                  .then_inc(sem("ld_ln1"), 16)
            for i in range(2):
                sp.dma_start(xres[0:P, i, :], i_["x_prompt"][0, i * P:(i + 1) * P, :]).then_inc(sem(f"ld_rows{i}"), 16)

            def load_expert(e, s, ahead=True):
                for nm, W, src in (("gate", WG, i_["w_gate"]), ("up", WU, i_["w_up"]), ("down", WD, i_["w_down"])):
                    if ahead:
                        sp.wait_ge(sem(nm + "_ps"), e - 1)
                    w = src[0, bass.ds(e, 1)] if ahead else src[0, e:e + 1]
                    sp.dma_start(W[s], w.rearrange("a (k p) n -> p (a k) n", p=P)).then_inc(sem(f"w{nm}{s}"), 16)

            load_expert(0, 0, False)
            for i in range(5):
                if i == 1:
                    load_expert(1, 1, False)
                r = trows(i)
                sp.wait_ge(sem("x1_ready"), i + 1)
                sp.dma_start(x1d[i * P:i * P + r, :], x1[0:r, i, :]).then_inc(sem("x1_st"), 16)
                if i + 2 < 5:
                    n = i + 2
                    src = i_["x_prompt"][0, n * P:(n + 1) * P, :] if n < 4 else i_["x_sample"].rearrange("b t d -> (b t) d")
                    sp.dma_start(xres[0:trows(n), n % 2, :], src).then_inc(sem(f"ld_rows{n % 2}"), 16)
            sp.wait_ge(sem("logit_ps"), 5)
            for r_ in range(2):
                sp.dma_start(ln2[:, r_, :], i_[("ln2_g", "ln2_b")[r_]][0:1, :].to_broadcast([P, D])) \
                  .then_inc(sem("ld_ln2"), 16)
            with sp.Fori(1, E // 2) as it:
                for s in range(2):
                    load_expert(2 * it + s, s)

            sp.wait_ge(sem("slots"), 1)
            more = sp.value_load(flag_i[0:1, :], min_val=0, max_val=OVER)
            with sp.If(more > 0):
                sp.wait_ge(sem("down_ps"), E)
                sp.wait_ge(sem("up_ps"), E)

                def load_more(o):
                    e = sp.value_load(eid_i[0:1, bass.ds(o, 1)], min_val=0, max_val=E - 1)
                    for W, src in ((WG, i_["w_gate"]), (WU, i_["w_up"]), (WD, i_["w_down"])):
                        sp.dma_start(W[0], src[0, bass.ds(e, 1)].rearrange("a (k p) n -> p (a k) n", p=P)) \
                          .then_inc(sem("o_w"), 16)

                load_more(0)
                with sp.Fori(1, OVER) as it:
                    sp.wait_ge(sem("over_pe"), 4 * it)
                    load_more(it)
            for i in range(5):
                sp.wait_ge(sem("y_done"), i + 1)
                r = trows(i)
                dst = o_["y_prompt"][0, i * P:(i + 1) * P, :] if i < 4 else o_["y_sample"].rearrange("b t d -> (b t) d")
                sp.dma_start(dst, x1[0:r, i, :]).then_inc(sem("out"), 16)
            sp.wait_ge(sem("out"), 16 * 7)

        @block.gpsimd
        def _(pool):
            zrow = v2(o_mixa, D)
            pool.memset(zrow, 0.0).then_inc(sem("pool_step"), 1)
            pool.wait_ge(sem("pool_step"), 1)
            pool.wait_ge(sem("proj"), 3)
            for n in range(OVER * CAP // P):
                pool.dma_start(ysd[E * CAP + n * P:E * CAP + (n + 1) * P, :], zrow).then_inc(sem("rows_zero"), 16)
            for j in range(4):
                y = V4[:, j, :]
                pool.wait_ge(sem("gn_y"), j + 1)
                pool.tensor_tensor(y, y, SG4[:, j, :], ALU.add).then_inc(sem("pool_step"), 1)
                pool.wait_ge(sem("pool_step"), j + 2)
                pool.tensor_tensor(mixR[:, j, :], y, G4[:, j, :], ALU.mult).then_inc(sem("gn_out"), 1)
            pool.wait_ge(sem("idx_ready"), 1)
            pool.wait_ge(sem("x1_st"), 80)
            pool.wait_ge(sem("logit_ps"), 5)

            def gather(e):
                if e >= 2:
                    pool.wait_ge(sem("xg_turn"), e - 1)
                pool.indirect_dma_start(out=xg[0:CAP, e % 2, :], out_offset=None, in_=x1d[:, :],
                                        in_offset=bass.IndirectOffsetOnAxis(ap=idx_i[0:CAP, e:e + 1], axis=0)) \
                    .then_inc(sem(f"xg{e % 2}"), 16)

            for e in range(E):
                gather(e)
            pool.wait_ge(sem("slots"), 1)
            more = pool.value_load(flag_i[0:1, :], min_val=0, max_val=OVER)
            with pool.If(more > 0):
                pool.dma_start(tokid[:, :], i_["tokid"][:, :]).then_inc(sem("o_idx"), 16)
                pool.memset(zidx[:, :], 0).then_inc(sem("o_zero"), 1)
                pool.wait_ge(sem("o_zero"), 1)
                pool.dma_start(idxd.rearrange("(p e) o -> p (e o)", e=BLOCKS * CAP // P), zidx[:, 0:BLOCKS * CAP // P]) \
                    .then_inc(sem("o_idx"), 16)
                pool.wait_ge(sem("o_idx"), 32)
                for i in range(5):
                    r = trows(i)
                    for n in range(2):
                        pool.indirect_dma_start(out=idxd[:, :], in_=tokid[0:r, i:i + 1], in_offset=None,
                                                out_offset=bass.IndirectOffsetOnAxis(ap=slot_i[0:r, i, n:n + 1], axis=0)) \
                            .then_inc(sem("o_idx"), 16)
                pool.wait_ge(sem("o_idx"), 192)
                pool.dma_start(idx_i[0:CAP, E:BLOCKS], idxd[E * CAP:SLOTS, :].rearrange("(e p) o -> p (e o)", p=CAP),
                               allow_slow_non_contiguous=True).then_inc(sem("o_idx"), 16)
                pool.wait_ge(sem("o_idx"), 208)
                pool.wait_ge(sem("xg_turn"), E)
                for o in range(OVER):
                    if o:
                        pool.wait_ge(sem("over_pe"), 4 * o - 3)
                    pool.indirect_dma_start(out=xg[0:CAP, 0, :], out_offset=None, in_=x1d[:, :],
                                            in_offset=bass.IndirectOffsetOnAxis(ap=idx_i[0:CAP, E + o:E + o + 1], axis=0)) \
                        .then_inc(sem("o_xg"), 16)
                pool.wait_ge(sem("o_yst"), 16 * OVER)
            pool.wait_ge(sem("y_st0"), 16 * E // 2)
            pool.wait_ge(sem("y_st1"), 16 * E // 2)
            pool.wait_ge(sem("down_ps"), E)
            for i in range(5):
                r = trows(i)
                for n in range(2):
                    pool.indirect_dma_start(out=yab[0:r, i, n, :], out_offset=None, in_=ysd[:, :],
                                            in_offset=bass.IndirectOffsetOnAxis(ap=slot_i[0:r, i, n:n + 1], axis=0)) \
                        .then_inc(sem(f"yab{min(i, 2)}"), 16)
            pool.wait_ge(sem("ld_ln2"), 32)
            for i in range(5):
                x, r = x1[0:trows(i), i, :], trows(i)
                pool.wait_ge(sem("ln2_nrm"), i + 1)
                pool.tensor_tensor(x, x, ln2[0:r, 0, :], ALU.mult).then_inc(sem("pool_step"), 1)
                pool.wait_ge(sem("pool_step"), i + 6)
                pool.tensor_tensor(x, x, ln2[0:r, 1, :], ALU.add).then_inc(sem("y_done"), 1)

        @block.tensor
        def _(pe):
            mm = pe.matmul

            def transpose_x():
                for n in range(10):
                    i, h = n // 2, n % 2
                    rows = P if i < 4 else 72
                    if h == 0:
                        pe.wait_ge(sem(f"ld_rows{i % 2}"), 16 * (i // 2 + 1))
                    if n == 0:
                        pe.wait_ge(sem("ld_first"), 32)
                    if n >= 2:
                        pe.wait_ge(sem(("xt_act", "xt_dve")[n % 2]), n // 2)
                    for k in range(4):
                        c = (4 * h + k) * P
                        ins = pe.transpose(ps[:, 5 + n % 2, k * P:k * P + rows], xst[0:rows, i % 2, c:c + P],
                                           ident[0:rows, 0:rows])
                    ins.then_inc(sem("xt_ps"), 1)
                pe.wait_ge(sem("xt_act"), 5)
                pe.wait_ge(sem("xt_dve"), 5)

            def project(ct):
                pe.wait_ge(sem(f"win{ct % RING}"), 16 * (ct // RING + 1))
                wait_read(pe, ct - 2)
                for k in range(KT):
                    mm(ps[:, ct % 2, :], ring[:, ct % RING, k, :], xT[:, k, 0:NP_], start=k == 0, stop=k == KT - 1)
                wait_read(pe, ct - 1)
                if ct == 12 or ct == 15 or ct == 18:
                    pe.wait_ge(sem("norm_read"), (ct - 9) // 3)
                if ct == 13 or ct == 16 or ct == 19:
                    pe.wait_ge(sem("bonus_read"), (ct - 10) // 3)
                for k in range(KT):
                    ins = mm(ps[:, 2, 0:72], ring[:, ct % RING, k, :], xT[:, k, NP_:584],
                             start=k == 0, stop=k == KT - 1)
                ins.then_inc(sem("proj"), 1)

            def lora(n):
                kind, j = n // 4, n % 4
                if n == 0:
                    pe.wait_ge(sem("ld_lora"), 64)
                    pe.wait_ge(sem("lora_in"), 1)
                if n == 8:
                    pe.wait_ge(sem("lora_in"), 2)
                if n >= 2:
                    pe.wait_ge(sem("lora_evac"), n - 1)
                r = (slice(0, 64), slice(64, 128), slice(0, 128))[kind]
                w = (LW, LW, GW)[kind][r, j * P:(j + 1) * P]
                src = (WA, WA, GL)[kind][r, :]
                b = 3 + 2 * (n % 2)
                mm(ps[:, b, :], w, src[:, 0:NP_], start=True, stop=True)
                mm(ps[:, b + 1, 0:NS], w, src[:, NP_:NT], start=True, stop=True).then_inc(sem("lora_ps"), 1)

            def kv_turn():
                pe.wait_ge(sem("att_evac"), 6)
                pe.wait_ge(sem("lora_evac"), 12)
                for t in range(4):
                    ins = pe.transpose(ps[:, 5, t * P:(t + 1) * P], vT[:, t * P:(t + 1) * P], ident)
                ins.then_inc(sem("kv_ps"), 1)
                pe.transpose(ps[0:NS, 6, 0:P], vT[:, NP_:NT], ident)
                pe.transpose(ps[:, 6, P:2 * P], kT[:, 4 * P:5 * P], ident)
                pe.transpose(ps[0:NS, 6, 2 * P:3 * P], kTs, ident).then_inc(sem("kv_ps"), 1)
                pe.wait_ge(sem("ld_cache"), 32)
                for h in range(2):
                    pe.wait_ge(sem("kv_tok"), h + 1)
                    for b in range(4):
                        ins = pe.transpose(ps[:, 5 + h, b * P:(b + 1) * P], kc[:, 4 * h + b, :], ident)
                    ins.then_inc(sem("kv_ps"), 1)

            def scores(n):
                if n >= 1:
                    pe.wait_ge(sem("s_read"), n)
                if n < 8:
                    nb, kv = n // 2, n % 2
                    r = slice(kv * 64, kv * 64 + 64)
                    for g in range(4):
                        ins = mm(ps[:, 3 + g // 2, (g % 2) * 256:(g % 2) * 256 + 256],
                                 qT[r, g, nb * P:(nb + 1) * P], kT[r, nb * P:(nb + 2) * P], start=True, stop=True)
                else:
                    pe.wait_ge(sem("kv_tok"), 4)
                    for kv in range(2):
                        r = slice(kv * 64, kv * 64 + 64)
                        for b in range(NB):
                            q = qTs[r, b].rearrange("p g t -> p (g t)")
                            o = slice(32 * (b % 4), 32 * (b % 4) + 32)
                            c = (b // 4) * 192
                            tp = (kv * 64, 32 * (b % 4))
                            mm(ps[o, 3 + kv, c:c + P], q, kcT[r, b, :], start=True, stop=True)
                            ins = mm(ps[o, 3 + kv, c + P:c + 192], q, kTs[r, :], start=True, stop=True)
                ins.then_inc(sem("s_ps"), 1)

            def p_turn(n):
                pe.wait_ge(sem("p_ready"), n + 1)
                if n == 0:
                    pe.wait_ge(sem("kv_tok"), 4)
                if n >= 1:
                    pe.wait_ge(sem("pv_evac"), n)
                w = 256 if n < 8 else 192
                Sn = Sb[:, n % 2, 0:4 * w].rearrange("p (g w) -> p g w", g=4)
                for kb in range(2):
                    kw = min(P, w - kb * P)
                    for g in range(4):
                        ins = pe.transpose(ps[0:kw, 5 + kb, g * P:(g + 1) * P], Sn[:, g, kb * P:kb * P + kw], ident)
                    ins.then_inc(sem("pt_ps"), 1)

            def pv(n):
                pe.wait_ge(sem("pt_act"), n + 1)
                pe.wait_ge(sem("pt_dve"), n + 1)
                if n < 8:
                    nb, kv = n // 2, n % 2
                    r = slice(kv * 64, kv * 64 + 64)
                    mm(ps[r, 5, :], Vt[:, nb, r], PT[:, 0, :], start=True, stop=False)
                    ins = mm(ps[r, 5, :], Vt[:, nb + 1, r], PT[:, 1, :], start=False, stop=True)
                else:
                    for kv in range(2):
                        r = slice(kv * 64, kv * 64 + 64)
                        for b in range(NB):
                            c = (kv * 2 + b // 4) * P + 32 * (b % 4)
                            mm(ps[r, 5, b * 32:b * 32 + 32], vc[:, b, r], PT[:, 0, c:c + 32], start=True, stop=False)
                            ins = mm(ps[r, 5, b * 32:b * 32 + 32], Vs[0:NS, r], PT[0:NS, 1, c:c + 32],
                                     start=False, stop=True)
                ins.then_inc(sem("pv_ps"), 1)

            def head_sum(n):
                if n == 0:
                    pe.wait_ge(sem("lora_evac"), 12)
                    pe.wait_ge(sem("ld_const"), 16)
                else:
                    pe.wait_ge(sem(("bonus_read", "norm_read")[n % 2]), (n + 1) // 2)
                pe.wait_ge(sem(("hsum_in_a", "hsum_in_b")[n % 2]), n // 2 + 1)
                pe.wait_ge(sem("mixed"), min(14, 6 + n // 2 * 3 + n % 2))
                s = SQ[:, n % 2, :]
                mm(ps[:, 7, :], C("blk"), s[:, 0:NP_], start=True, stop=True)
                mm(ps[:, 2, 0:NS], C("blk"), s[:, NP_:NT], start=True, stop=True).then_inc(sem("hsum_ps"), 1)

            transpose_x()
            for ct in range(COLT):
                if 2 <= ct < 8:
                    lora(2 * (ct - 2))
                project(ct)
                if 2 <= ct < 8:
                    lora(2 * (ct - 2) + 1)
                if ct == 7:
                    kv_turn()
                if ct >= RW0:
                    k = ct - RW0
                    if 2 <= k < 11:
                        pv(k - 2)
                    if k < 9:
                        scores(k)
                    if 1 <= k < 10:
                        p_turn(k - 1)
                    if k >= 3:
                        j, ph = k // 3 - 1, k % 3
                        if ph == 0:
                            head_sum(2 * j)
                        if ph == 1:
                            head_sum(2 * j + 1)
            head_sum(6)
            head_sum(7)

            def state_in(h):
                if h == 0:
                    pe.wait_ge(sem("pv_evac"), 9)
                if h >= 2:
                    pe.wait_ge(sem("st_ev"), h - 1)
                pe.wait_ge(sem(f"ld_st{h % 2}"), 16 * (h // 2 + 1))
                for n in range(8):
                    ins = pe.transpose(ps[:, 5 + h % 2, n * HD:(n + 1) * HD], stage[h % 2][0:HD, n * P:(n + 1) * P],
                                       ident[0:HD, 0:HD])
                ins.then_inc(sem("st_ps"), 1)

            def wy(q):
                R, L = rows(q), levels(q)
                if q == 0:
                    pe.wait_ge(sem("prep"), 4)
                    pe.wait_ge(sem("bonus_read"), 4)
                    pe.wait_ge(sem("st_ev"), 4)
                else:
                    pe.wait_ge(sem("post_dve"), 5 * q)
                    pe.wait_ge(sem("post_act"), q)
                for n, T4 in enumerate((A4, B4, K4, V4)):
                    for u in range(4):
                        ins = pe.transpose(ps[0:R, n, u * P:(u + 1) * P], unit(T4, q, u), ident)
                    ins.then_inc(sem("tok_ps"), 1)
                for p in range(2):
                    for u in range(4):
                        ins = mm(ps[0:R, 4 + p, u * R:(u + 1) * R], unit(A4, q, u, par_rows(p)),
                                 unit(B4, q, u, par_rows(p)), start=True, stop=True)
                    ins.then_inc(sem("n_ps"), 1)

                def gram(T4, p, name):
                    for u in range(4):
                        t0 = q * NT + u * P if q < 4 else u * NT + NP_
                        both = rwkv7[par_rows(p), 0:4:3, t0:t0 + R]
                        c = (u % 2) * 2 * R
                        ins = mm(ps[0:R, 2 * p + u // 2, c:c + 2 * R].rearrange("p (a b) -> p a b", a=2),
                                 unit(T4, q, u, par_rows(p)), both, start=True, stop=True)
                    ins.then_inc(sem(name), 1)

                for p in range(2):
                    pe.wait_ge(sem(("tok_act", "tok_dve")[p]), 2 * q + 2)
                    gram(B4, p, "bg_ps")

                def turn_x(l, p, bank):
                    pe.wait_ge(sem("x_ready"), 10 * q + 2 * l + p + 1)
                    for u in range(4):
                        ins = pe.transpose(ps[0:R, bank, u * R:(u + 1) * R], X[p][0:R, u * R:(u + 1) * R],
                                           ident[0:R, 0:R])
                    ins.then_inc(sem("xt2_ps"), 1)

                for p in range(2):
                    turn_x(0, p, 6 + p)
                for p in range(2):
                    pe.wait_ge(sem("bg_ev"), 2 * q + p + 1)
                    gram(K4, p, "kg_ps")
                for l in range(1, L + 1):
                    for p in range(2):
                        if l > 1:
                            pe.wait_ge(sem("x_ready"), 10 * q + 2 * (l - 1) + p + 1)
                        for u in range(4):
                            nt = BG[p][0:R, u * 2 * R + R:(u + 1) * 2 * R]
                            ins = mm(ps[0:R, 4 + p, u * R:(u + 1) * R], nt, X[p][0:R, u * R:(u + 1) * R],
                                     start=True, stop=True)
                        ins.then_inc(sem("w1_ps"), 1)
                        if l > 1:
                            turn_x(l - 1, p, 2 + p)
                    if l == 1:
                        for p in range(2):
                            pe.wait_ge(sem("kg_ev"), 2 * q + 2)
                            for u in range(4):
                                ak = KG[p][0:R, u * 2 * R + R:(u + 1) * 2 * R]
                                ins = mm(ps[0:R, p, u * HD:(u + 1) * HD], ak, TOK[3][0:R, u, par_rows(p)],
                                         start=True, stop=True)
                            ins.then_inc(sem("akv_ps"), 1)
                    for p in range(2):
                        pe.wait_ge(sem("w1_ev"), 10 * q + 2 * (l - 1) + p + 1)
                        pe.wait_ge(sem("xt2_ev"), 10 * q + 2 * (l - 1) + p + 1)
                        for u in range(4):
                            c = slice(u * R, (u + 1) * R)
                            if l < L:
                                ins = mm(ps[0:R, 6 + p, c], XT[p][0:R, c], W1[p][0:R, c], start=True, stop=True)
                            else:
                                ins = mm(ps[0:R, 6 + p, c], W1[p][0:R, c], XT[p][0:R, c], start=True, stop=True)
                        ins.then_inc(sem("xl_ps"), 1)
                for p in range(2):
                    pe.wait_ge(sem("t_ready"), 2 * q + p + 1)
                    pe.wait_ge(sem("rhs_ev"), 2 * q + p + 1)
                    for u in range(4):
                        ins = mm(ps[0:R, p, u * P:(u + 1) * P], XT[p][0:R, u * R:(u + 1) * R],
                                 RHS[p][0:R, u * P:(u + 1) * P], start=True, stop=True)
                    ins.then_inc(sem("gh_ps"), 1)
                pe.wait_ge(sem("gh_ev"), 2 * q + 2)
                for p in range(2):
                    for u in range(4):
                        ins = mm(ps[par_rows(p), 2, u * R:(u + 1) * R], GH[p][0:R, u * P:u * P + HD],
                                 BG[p][0:R, u * 2 * R:u * 2 * R + R], start=True, stop=True)
                ins.then_inc(sem("post_ps"), 1)
                for p in range(2):
                    for u in range(4):
                        o = ps[par_rows(p), 3, u * R:(u + 1) * R]
                        mm(o, GH[p][0:R, u * P + HD:(u + 1) * P], BG[p][0:R, u * 2 * R:u * 2 * R + R],
                           start=True, stop=False)
                        ins = mm(o, TOK[3][0:R, u, par_rows(p)], KG[p][0:R, u * 2 * R:u * 2 * R + R],
                                 start=False, stop=True)
                ins.then_inc(sem("post_ps"), 1)
                if q < 4:
                    for cp in range(2):
                        r = slice(64 * cp, 64 * cp + 64)
                        for p in range(2):
                            for u in range(4):
                                ins = mm(ps[par_rows(p), 6 + cp, u * HD:(u + 1) * HD], GH[p][r, u * P:u * P + HD],
                                         TOK[1][r, u, par_rows(p)], start=True, stop=True)
                    ins.then_inc(sem("post_ps"), 1) if cp else None
                    for cp in range(2):
                        r = slice(64 * cp, 64 * cp + 64)
                        for p in range(2):
                            for u in range(4):
                                o = ps[par_rows(p), 4 + cp, u * HD:(u + 1) * HD]
                                mm(o, TOK[1][r, u, par_rows(p)], GH[p][r, u * P + HD:(u + 1) * P],
                                   start=True, stop=False)
                                ins = mm(o, TOK[2][r, u, par_rows(p)], TOK[3][r, u, par_rows(p)],
                                         start=False, stop=True)
                    ins.then_inc(sem("post_ps"), 1)

            def sample_states():
                for p in range(2):
                    for u in range(4):
                        ins = mm(ps[par_rows(p), 6, u * HD:(u + 1) * HD], TOK[0][0:NS, u, par_rows(p)],
                                 XT[p][0:NS, u * NS:(u + 1) * NS], start=True, stop=True)
                ins.then_inc(sem("gt_ps"), 1)
                pe.wait_ge(sem("post_dve"), 21)
                for p in range(2):
                    for u in range(4):
                        for b in range(NB):
                            c = b * TS
                            ins = mm(ps[par_rows(p), 0, u * NS + c:u * NS + c + TS], Z0[par_rows(p), u, b, :],
                                     R4[par_rows(p), u, NP_ + c:NP_ + c + TS], start=True, stop=True)
                ins.then_inc(sem("ys_ps"), 1)
                pe.wait_ge(sem("gt_ev"), 1)
                for n in range(8):
                    u, p = n // 2, n % 2
                    if n >= 2:
                        pe.wait_ge(sem("um_ev"), n - 1)
                    mm(ps[0:NS, 4 + p, :], GTs[par_rows(p), u * NS:(u + 1) * NS],
                       Z0[par_rows(p), u].rearrange("p b v -> p (b v)"), start=True, stop=True).then_inc(sem("u_ps"), 1)
                    if n >= 1:
                        chain(n)
                        z1(n - 1)
                z1(7)

            def z1(n):
                u, p = n // 2, n % 2
                pe.wait_ge(sem("um_ev"), n + 1)
                if u >= 2 and p == 0:
                    pe.wait_ge(sem("z1_ev"), u - 1)
                o = ps[par_rows(p), 6 + u % 2, :]
                mm(o, TOK[1][0:NS, u, par_rows(p)], W1[p][0:NS, :], start=True, stop=False)
                mm(o, TOK[2][0:NS, u, par_rows(p)], NM[p][0:NS, :], start=False, stop=True).then_inc(sem("z1_ps"), 1)

            def sample_out(b):
                if b == 0:
                    pe.wait_ge(sem("z1_ev"), 4)
                if b >= 2:
                    pe.wait_ge(sem("so_ev"), b - 1)
                for j in range(4):
                    ins = pe.transpose(ps[0:HD, 6 + b % 2, j * P:(j + 1) * P], Z0[:, j, b, :], ident)
                ins.then_inc(sem("so_ps"), 1)

            def prompt_out():
                pe.wait_ge(sem("so_ev"), 8)
                for j in range(4):
                    ins = pe.transpose(ps[0:HD, 7, j * P:(j + 1) * P], Zp[:, 7, j, :], ident)
                ins.then_inc(sem("so_ps"), 1)

            def zin(c, j, p):
                return B4[par_rows(p), j, 0:HD] if c == 1 else Zp[par_rows(p), c - 1, j, :]

            def chain(c):
                if c > 1:
                    pe.wait_ge(sem("z_ready"), c - 1)
                for p in range(2):
                    for j in range(4):
                        ins = mm(ps[par_rows(p), 1, j * HD:(j + 1) * HD], A4[par_rows(p), j, c * HD:(c + 1) * HD],
                                 zin(c, j, p), start=True, stop=True)
                ins.then_inc(sem("z_ps"), 1)

            def y_of(j):
                if j == 0:
                    pe.wait_ge(sem("um_ev"), 8)
                if j == 3:
                    pe.wait_ge(sem("post_act"), 5)
                for c in range(1, CHUNKS):
                    if j == 0:
                        pe.wait_ge(sem("z_ready"), max(1, c - 1))
                    for p in range(2):
                        ins = mm(ps[par_rows(p), (4, 5, 2, 3)[j], c * HD:(c + 1) * HD], zin(c, j, p),
                                 R4[par_rows(p), j, c * HD:(c + 1) * HD], start=True, stop=True)
                ins.then_inc(sem("y_ps"), 1)

            def head_mean(n):
                b = 2 * (n % 2)
                if n == 0:
                    pe.wait_ge(sem("ys_ev"), 1)
                    pe.wait_ge(sem("z_ready"), 7)
                    pe.wait_ge(sem("y_ev"), 1)
                if n == 1:
                    pe.wait_ge(sem("y_ev"), 4)
                if n >= 2:
                    pe.wait_ge(sem(("centred", "var_read")[n % 2]), n // 2)
                if n % 2:
                    pe.wait_ge(sem("gsq"), n // 2 + 1)
                src = (V4[:, n // 2, :], SQ[:, 0, :])[n % 2]
                mm(ps[:, b, :], C("blk"), src[:, 0:NP_], start=True, stop=True)
                mm(ps[:, b + 1, 0:NS], C("blk"), src[:, NP_:NT], start=True, stop=True).then_inc(sem("hm_ps"), 1)

            def out_proj(i, hs, ks):
                r = trows(i)
                if i == 0 and 0 in ks:
                    pe.wait_ge(sem("ld_wo"), 16)
                    pe.wait_ge(sem("y_ev"), 2)
                if i == 1 and 0 in ks:
                    pe.wait_ge(sem("so_ev"), NB + 1)
                if i >= 2:
                    pe.wait_ge(sem("pre_ln"), i - 1)
                for h in hs:
                    for k in ks:
                        m = (mixA[:, k, :] if k < 4 else mixR[:, k - 4, :])[:, i * P:i * P + r]
                        ins = mm(ps[0:r, 4 + 2 * (i % 2) + h, :], m, wo[:, k, h * 512:(h + 1) * 512],
                                 start=k == 0, stop=k == KT - 1)
                if KT - 1 in ks:
                    ins.then_inc(sem("op_ps"), 1)

            for h in range(4):
                state_in(h)
            for q in range(5):
                wy(q)
            sample_states()
            for j in range(4):
                y_of(j)
            sample_out(0)
            sample_out(1)
            head_mean(0)
            for b in range(2, 5):
                sample_out(b)
            head_mean(1)
            for b in range(5, NB):
                sample_out(b)
            prompt_out()
            for n in range(2, 8):
                head_mean(n)
                if n < 6:
                    out_proj((n - 2) // 2, (n % 2, ), range(4))

            def turn_x1(i):
                r = trows(i)
                pe.wait_ge(sem("x1_ready"), i + 1)
                if i == 0:
                    pe.wait_ge(sem("y_ev"), 4)
                for h in range(2):
                    if i:
                        pe.wait_ge(sem(("x1t_act", "x1t_dve")[h]), i)
                    for k in range(4):
                        c = (4 * h + k) * P
                        ins = pe.transpose(ps[:, 2 + h, k * P:k * P + r], x1[0:r, i, c:c + P], ident[0:r, 0:r])
                    ins.then_inc(sem("x1t_ps"), 1)

            def logits(i):
                r = trows(i)
                pe.wait_ge(sem("x1t_act"), i + 1)
                pe.wait_ge(sem("x1t_dve"), i + 1)
                if i:
                    pe.wait_ge(sem("lg_ev"), i)
                for k in range(KT):
                    ins = mm(ps[0:r, 0, 0:E], x1T[:, k, 0:r], wr[:, k, :], start=k == 0, stop=k == KT - 1)
                ins.then_inc(sem("logit_ps"), 1)

            pe.wait_ge(sem("gn_out"), 4)
            for i in range(5):
                out_proj(i, range(2), range(4, KT) if i < 2 else range(KT))
                if i >= 1:
                    turn_x1(i - 1)
                if i >= 2:
                    logits(i - 2)
            logits(3)
            turn_x1(4)
            logits(4)

            pe.wait_ge(sem("chosen"), 1)
            for i in range(5):
                o = ps[:, RANKB, i * E:(i + 1) * E]
                mm(o, C("before"), rt[:, i, :], start=True, stop=i == 0)
                for k in range(i):
                    mm(o, C("ones"), rt[:, k, :], start=False, stop=k == i - 1)
            for k in range(5):
                ins = mm(ps[:, RANKB, 5 * E:6 * E], C("ones"), rt[:, k, :], start=k == 0, stop=k == 4)
            ins.then_inc(sem("rank_ps"), 1)

            pe.wait_ge(sem("idx_in"), 2)
            for n in range(10):
                k, i = n // 5, n % 5
                ins = mm(ps[0:CAP, 2, 0:E], OH[k][:, i, 0:CAP], TI[k][:, i, :], start=n == 0, stop=n == 9)
            ins.then_inc(sem("idx_ps"), 1)

            R_ = CAP

            def turn_xg(e, s, first=False):
                pe.wait_ge(sem(f"xg{s}"), e * 8 + (16 - 8 * s))
                if not first:
                    pe.wait_ge(sem("xgT_act"), e)
                    pe.wait_ge(sem("xgT_dve"), e)
                for k in range(KT):
                    ins = pe.transpose(ps[:, k // 4, (k % 4) * P:(k % 4) * P + R_], xg[0:R_, s, k * P:(k + 1) * P],
                                       ident[0:R_, 0:R_])
                ins.then_inc(sem("xg_turn"), 1)

            def gate_up(e, s, first=False):
                pe.wait_ge(sem("xgT_act"), e + 1)
                pe.wait_ge(sem("xgT_dve"), e + 1)
                for W, nm, b in ((WG, "gate", 2), (WU, "up", 3)):
                    pe.wait_ge(sem(f"w{nm}{s}"), e * 8 + (16 - 8 * s))
                    if not first:
                        pe.wait_ge(sem("h_ready"), e)
                    for k in range(KT):
                        ins = mm(ps[0:R_, b, :], xgT[s][:, k, 0:R_], W[s][:, k, :], start=k == 0, stop=k == KT - 1)
                    ins.then_inc(sem(nm + "_ps"), 1)

            def turn_h(e, s, first=False):
                pe.wait_ge(sem("h_ready"), e + 1)
                if not first:
                    pe.wait_ge(sem("ht_ready"), e)
                for k in range(FT):
                    ins = pe.transpose(ps[:, 4, k * P:k * P + R_], hh[0:R_, s, k * P:(k + 1) * P], ident[0:R_, 0:R_])
                ins.then_inc(sem("ht_ps"), 1)

            def down(e, s, first=False):
                pe.wait_ge(sem("ht_ready"), e + 1)
                pe.wait_ge(sem(f"wdown{s}"), e * 8 + (16 - 8 * s))
                if not first:
                    pe.wait_ge(sem("y_act"), e)
                    pe.wait_ge(sem("y_dve"), e)
                for h in range(2):
                    for k in range(FT):
                        ins = mm(ps[0:R_, 5 + h, :], hT[s][:, k, 0:R_], WD[s][:, k, h * 512:(h + 1) * 512],
                                 start=k == 0, stop=k == FT - 1)
                ins.then_inc(sem("down_ps"), 1)

            turn_xg(0, 0, True)
            gate_up(0, 0, True)
            turn_xg(1, 1)
            turn_h(0, 0, True)
            gate_up(1, 1)
            turn_xg(2, 0)
            down(0, 0, True)
            turn_h(1, 1)
            with pe.Fori(1, E // 2 - 1) as it:
                for s in range(2):
                    e = 2 * it + s
                    gate_up(e, s)
                    turn_xg(e + 1, 1 - s)
                    down(e - 1, 1 - s)
                    turn_h(e, s)
            gate_up(E - 2, 0)
            turn_xg(E - 1, 1)
            down(E - 3, 1)
            turn_h(E - 2, 0)
            gate_up(E - 1, 1)
            down(E - 2, 0)
            turn_h(E - 1, 1)
            down(E - 1, 1)

            pe.wait_ge(sem("slots"), 1)
            more = pe.value_load(flag_i[0:1, :], min_val=0, max_val=OVER)
            with pe.If(more > 0):
                pe.wait_ge(sem("y_act"), E)
                pe.wait_ge(sem("y_dve"), E)
                with pe.Fori(0, OVER) as it:
                    pe.wait_ge(sem("o_xg"), 16 * it + 16)
                    for k in range(KT):
                        ins = pe.transpose(ps[:, k // 4, (k % 4) * P:(k % 4) * P + R_],
                                           xg[0:R_, 0, k * P:(k + 1) * P], ident[0:R_, 0:R_])
                    ins.then_inc(sem("over_pe"), 1)
                    pe.wait_ge(sem("over_act"), 4 * it + 1)
                    pe.wait_ge(sem("o_w"), 48 * it + 48)
                    for W, b in ((WG, 2), (WU, 3)):
                        for k in range(KT):
                            ins = mm(ps[0:R_, b, :], xgT[0][:, k, 0:R_], W[0][:, k, :], start=k == 0,
                                     stop=k == KT - 1)
                    ins.then_inc(sem("over_pe"), 1)
                    pe.wait_ge(sem("o_h"), it + 1)
                    for k in range(FT):
                        ins = pe.transpose(ps[:, 4, k * P:k * P + R_], hh[0:R_, 0, k * P:(k + 1) * P],
                                           ident[0:R_, 0:R_])
                    ins.then_inc(sem("over_pe"), 1)
                    pe.wait_ge(sem("over_act"), 4 * it + 3)
                    for h in range(2):
                        for k in range(FT):
                            ins = mm(ps[0:R_, 5 + h, :], hT[0][:, k, 0:R_], WD[0][:, k, h * 512:(h + 1) * 512],
                                     start=k == 0, stop=k == FT - 1)
                    ins.then_inc(sem("over_pe"), 1)

        @block.scalar
        def _(act):
            T = Tally(act)
            A = act.activation
            for i in range(5):
                if i >= 2:
                    act.wait_ge(sem("xt_ps"), 2 * (i - 1))
                src = i_["x_prompt"][0, i * P:(i + 1) * P, :] if i < 4 else i_["xs9"][:, :]
                act.dma_start(xst[0:src.shape[0], i % 2, :], src).then_inc(sem(f"ld_rows{i % 2}"), 16)
                if i >= 1:
                    for n in ((2 * (i - 1), ) if i < 4 else (6, 8)):
                        act.wait_ge(sem("xt_ps"), n + 1)
                        r = 72 if n == 8 else P
                        T.up(A(xT[:, 0:4, (n // 2) * P:(n // 2) * P + r],
                               ps[:, 5, :].rearrange("p (k c) -> p k c", c=P)[:, :, 0:r], ACT.Copy), "xt_act")

            def scale_mix(ct):
                m = mix_index(ct)
                act.wait_ge(sem("proj"), ct + 1)
                if m >= 2:
                    act.wait_ge(sem("mixed"), m - 1)
                else:
                    act.wait_ge(sem("zeroed"), 3)
                mu = par[:, MU + m:MU + m + 1]
                A(mixtmp[:, m % 2, 1:513], ps[:, ct % 2, :], ACT.Copy, scale=mu)
                so = 0
                T.up(A(mixtmp[:, m % 2, 520:592], ps[:, 2, so:so + 72], ACT.Copy, scale=mu), "mix_scaled")

            def cols(ct):
                return ps[:, 2, 0:72].rearrange("p (b t) -> p b t", t=9)[:, :, 1:9]

            def evac_att(ct):
                act.wait_ge(sem("proj"), ct + 1)
                n = ct - ATT0
                if n < 4:
                    A(qT[:, n, :], ps[:, ct % 2, :], ACT.Copy, scale=ATT_SCALE)
                    ins = A(qTs[:, :, n, :], cols(ct), ACT.Copy, scale=ATT_SCALE)
                else:
                    d, ds = (kT[:, P:P + NP_], kTs) if n == 4 else (vT[:, 0:NP_], vT[:, NP_:NT])
                    A(d, ps[:, ct % 2, :], ACT.Copy)
                    ins = A(ds.rearrange("p (b t) -> p b t", t=TS), cols(ct), ACT.Copy)
                T.up(ins, "att_evac")

            def lora_act(n):
                kind, j = n // 4, n % 4
                act.wait_ge(sem("lora_ps"), n + 1)
                dst = (SG4, B4, G4)[kind][:, j, :]
                fn = ACT.Copy if kind == 2 else ACT.Sigmoid
                b = 0.0 if kind == 2 else par[:, (W0, A0)[kind] + j:(W0, A0)[kind] + j + 1]
                bank = 3 + 2 * (n % 2)
                T.up(A(dst, ps[:, bank:bank + 2, :].rearrange("p a b -> p (a b)")[:, 0:NT], fn, bias=b), "lora_evac")

            def exps(n):
                act.wait_ge(sem("s_max"), n + 1)
                w = 256 if n < 8 else 192
                Sn = Sb[:, n % 2, 0:4 * w].rearrange("p (g w) -> p g w", g=4)
                st = att_st[:, n % 2]
                for g in range(4):
                    A(Sn[:, g, :], Sn[:, g, :], ACT.Exp, bias=st[:, 1, g:g + 1], accum_out=st[:, 3, g:g + 1])
                T.up(A(st[:, 4, :], st[:, 2, :], ACT.Exp), "exp_done")

            def pt_copy(n):
                act.wait_ge(sem("pt_ps"), 2 * n + 1)
                if n >= 1:
                    act.wait_ge(sem("pv_ps"), n)
                T.up(A(PT[:, 0, :], ps[:, 5, :], ACT.Copy), "pt_act")

            def pv_copy(n):
                act.wait_ge(sem("pv_ps"), n + 1)
                if n == 0:
                    act.wait_ge(sem("rows_zero"), 16 * (OVER * CAP // P))
                if n < 8:
                    nb, kv = n // 2, n % 2
                    r = slice(kv * 64, kv * 64 + 64)
                    ins = A(mixA[r, :, nb * P:(nb + 1) * P], ps[r, 5, :].rearrange("p (g t) -> p g t", g=4), ACT.Copy)
                else:
                    src = ps[:, 5, 0:256].rearrange("p (b g t) -> p g b t", g=4, t=TS)
                    for g in range(4):
                        ins = A(mixA[:, g, NP_:NT].rearrange("p (b t) -> p b t", t=TS), src[:, g], ACT.Copy)
                T.up(ins, "pv_evac")

            def prep_square(j):
                act.wait_ge(sem("kraw"), j + 1)
                if j >= 1:
                    act.wait_ge(sem("prep"), j)
                T.up(A(SQ[:, 0, :], A4[:, j, :], ACT.Square), "hsum_in_a")

            def prep_norm(j):
                act.wait_ge(sem("hsum_ps"), 2 * j + 1)
                A(SQ[:, 0, 0:NP_], ps[:, 7, :], ACT.Sqrt)
                T.up(A(SQ[:, 0, NP_:NT], ps[:, 2, 0:NS], ACT.Sqrt), "norm_read")

            def prep_exps(j):
                act.wait_ge(sem("cum"), 2 * j + 1)
                if j >= 2:
                    act.wait_ge(sem("prep"), j - 1)
                A(PI[:, j % 2, :], PM[:, j % 2, :], ACT.Exp, scale=DECAY_SCALE)
                act.wait_ge(sem("cum"), 2 * j + 2)
                T.up(A(SG4[:, j, :], SG4[:, j, :], ACT.Exp, scale=-DECAY_SCALE), "pexp")
                act.wait_ge(sem("pexp"), 2 * j + 1)
                T.up(A(PM[:, j % 2, :], PM[:, j % 2, :], ACT.Exp, scale=-DECAY_SCALE), "pexp")

            for ct in range(COLT):
                if ct < 2:
                    scale_mix(ct)
                    act.wait_ge(sem("mixed"), ct + 1)
                    if ct == 0:
                        T.up(A(WA[0:64, :], WA[0:64, :], ACT.Tanh), "lora_in")
                    else:
                        T.up(A(GL, GL, ACT.Sigmoid), "lora_in")
                elif ct < 8:
                    lora_act(2 * (ct - 2))
                    evac_att(ct)
                    lora_act(2 * (ct - 2) + 1)
                else:
                    k = ct - RW0
                    scale_mix(ct)
                    if 2 <= k < 11:
                        pv_copy(k - 2)
                    if k < 9:
                        exps(k)
                    if 1 <= k < 10:
                        pt_copy(k - 1)
                    if k >= 3 and k % 3 == 0:
                        prep_norm(k // 3 - 1)
                    if k % 3 == 2:
                        prep_square(k // 3)
                        prep_exps(k // 3)
            prep_norm(3)

            for h in range(4):
                act.wait_ge(sem("st_ps"), h + 1)
                if h == 0:
                    act.wait_ge(sem("prep"), 4)
                    act.wait_ge(sem("bonus_read"), 4)
                T.up(A(Z0[:, :, 2 * h:2 * h + 2, :],
                       ps[:, 5 + h % 2, :].rearrange("p (b j v) -> p j b v", b=2, v=HD), ACT.Copy), "st_ev")
            for j in range(4):
                A(SG4[:, j, :], SG4[:, j, :], ACT.Identity, bias=par[:, GNB + j:GNB + j + 1])

            def wy(q):
                R, L = rows(q), levels(q)
                if q == 0:
                    act.wait_ge(sem("kv_out"), 64)
                for n in range(2):
                    act.wait_ge(sem("tok_ps"), 4 * q + n + 1)
                    T.up(A(TOK[n][0:R], ps[0:R, n, :].rearrange("p (u c) -> p u c", u=4), ACT.Copy), "tok_act")
                act.wait_ge(sem("tok_act"), 2 * q + 1)

                def xt_copy(l, p, bank):
                    act.wait_ge(sem("xt2_ps"), 10 * q + 2 * l + p + 1)
                    if l:
                        act.wait_ge(sem("xl_ps"), 10 * q + 2 * (l - 1) + p + 1)
                    T.up(A(XT[p][0:R, 0:4 * R], ps[0:R, bank, 0:4 * R], ACT.Copy), "xt2_ev")

                for p in range(2):
                    xt_copy(0, p, 6 + p)
                    A(RHS[p].rearrange("p (u c) -> p u c", u=4)[0:R, :, 0:HD], TOK[0][0:R, :, par_rows(p)], ACT.Copy)
                for p in range(2):
                    act.wait_ge(sem("akv_ps"), 2 * q + p + 1)
                    T.up(A(RHS[p].rearrange("p (u c) -> p u c", u=4)[0:R, :, HD:P],
                           ps[0:R, p, 0:256].rearrange("p (u c) -> p u c", u=4), ACT.Copy), "rhs_ev")
                for l in range(1, L):
                    for p in range(2):
                        xt_copy(l, p, 2 + p)
                for p in range(2):
                    act.wait_ge(sem("gh_ps"), 2 * q + p + 1)
                    T.up(A(GH[p][0:R, :], ps[0:R, p, :], ACT.Copy), "gh_ev")
                act.wait_ge(sem("post_ps"), 4 * q + 2)
                T.up(A(units(V4, q), ps[:, 3, 0:4 * R].rearrange("p (u c) -> p u c", u=4), ACT.Copy), "post_act")

            for q in range(5):
                wy(q)
            act.wait_ge(sem("gt_ps"), 1)
            T.up(A(GTs, ps[:, 6, 0:256], ACT.Copy), "gt_ev")
            def state_copy(b):
                act.wait_ge(sem("so_ps"), b + 1)
                d = souts[b][0:HD, :] if b < NB else GH[1][0:HD, :]
                T.up(A(d, ps[0:HD, 6 + min(b, 7) % 2, :], ACT.Copy), "so_ev")

            def gn_square(j):
                act.wait_ge(sem("centred"), j + 1)
                if j:
                    act.wait_ge(sem("hm_ps"), 2 * j)
                T.up(A(SQ[:, 0, :], V4[:, j, :], ACT.Square), "gsq")

            for b in range(5):
                state_copy(b)
            gn_square(0)
            for b in range(5, NB + 1):
                state_copy(b)
            for j in range(4):
                if j:
                    gn_square(j)
                act.wait_ge(sem("hm_ps"), 2 * j + 2)
                if j:
                    act.wait_ge(sem("gn_y"), j)
                T.up(A(SQ[:, 1, :], ps[:, 2:4, :].rearrange("p a b -> p (a b)")[:, 0:NT], ACT.Sqrt,
                       scale=1.0 / HD, bias=gn_eps), "var_read")

            def root(n, i):
                act.wait_ge(sem(n + "_var"), i + 1)
                r = trows(i)
                T.up(A(lnst[0:r, i % 2, 14:15], lnst[0:r, i % 2, 13:14], ACT.Sqrt, bias=ln_eps[0:r]), n + "_sd")

            for i in range(5):
                root("ln1", i)
                r = trows(i)
                act.wait_ge(sem("x1t_ps"), 2 * i + 1)
                if i:
                    act.wait_ge(sem("logit_ps"), i)
                T.up(A(x1T[:, 0:4, 0:r], ps[:, 2, :].rearrange("p (k c) -> p k c", c=P)[:, :, 0:r], ACT.Copy),
                     "x1t_act")
            act.wait_ge(sem("lg_max"), 1)
            T.up(A(PR, PR, ACT.Exp), "lg_exp")
            R_ = CAP

            def xg_copy(e, s, first=False):
                act.wait_ge(sem("xg_turn"), e + 1)
                if not first:
                    act.wait_ge(sem("up_ps"), e - 1)
                T.up(A(xgT[s][:, 0:4, 0:R_], ps[:, 0, :].rearrange("p (k c) -> p k c", c=P)[:, :, 0:R_], ACT.Copy),
                     "xgT_act")

            def silu(e, s, first=False):
                act.wait_ge(sem("gate_ps"), e + 1)
                if not first:
                    act.wait_ge(sem("h_ready"), e - 1)
                T.up(A(sg[0:R_, s, :], ps[0:R_, 2, :], ACT.Silu), "silu")

            def h_copy(e, s, first=False):
                act.wait_ge(sem("ht_ps"), e + 1)
                if not first:
                    act.wait_ge(sem("down_ps"), e - 1)
                T.up(A(hT[s][:, :, 0:R_], ps[:, 4, :].rearrange("p (k c) -> p k c", c=P)[:, :, 0:R_], ACT.Copy),
                     "ht_ready")

            def y_copy(e, s, first=False):
                act.wait_ge(sem("down_ps"), e + 1)
                if not first:
                    act.wait_ge(sem(f"y_st{s}"), e * 8 - 8 * s)
                T.up(A(yst[0:R_, s, 0:512], ps[0:R_, 5, :], ACT.Copy), "y_act")
                act.wait_ge(sem("y_act"), e + 1)
                act.wait_ge(sem("y_dve"), e + 1)
                dst = ysd[e * CAP:(e + 1) * CAP, :] if isinstance(e, int) else ysd[bass.ds(e * CAP, CAP), :]
                act.dma_start(dst, yst[0:R_, s, :]).then_inc(sem(f"y_st{s}"), 16)

            xg_copy(0, 0, True)
            silu(0, 0, True)
            xg_copy(1, 1, True)
            h_copy(0, 0, True)
            silu(1, 1, True)
            xg_copy(2, 0)
            h_copy(1, 1, True)
            y_copy(0, 0, True)
            silu(2, 0)
            xg_copy(3, 1)
            h_copy(2, 0)
            y_copy(1, 1, True)
            silu(3, 1)
            xg_copy(4, 0)
            h_copy(3, 1)
            y_copy(2, 0)
            with act.Fori(2, E // 2 - 1) as it:
                for s in range(2):
                    e = 2 * it + s
                    silu(e, s)
                    xg_copy(e + 1, 1 - s)
                    h_copy(e, s)
                    y_copy(e - 1, 1 - s)
            silu(E - 2, 0)
            xg_copy(E - 1, 1)
            h_copy(E - 2, 0)
            y_copy(E - 3, 1)
            silu(E - 1, 1)
            y_copy(E - 2, 0)
            h_copy(E - 1, 1)
            y_copy(E - 1, 1)
            act.wait_ge(sem("slots"), 1)
            more = act.value_load(flag_i[0:1, :], min_val=0, max_val=OVER)
            with act.If(more > 0):
                act.wait_ge(sem("y_st0"), 8 * E)
                with act.Fori(0, OVER) as it:
                    act.wait_ge(sem("over_pe"), 4 * it + 1)
                    A(xgT[0][:, 0:4, 0:R_], ps[:, 0, :].rearrange("p (k c) -> p k c", c=P)[:, :, 0:R_], ACT.Copy)
                    A(xgT[0][:, 4:8, 0:R_], ps[:, 1, :].rearrange("p (k c) -> p k c", c=P)[:, :, 0:R_], ACT.Copy) \
                        .then_inc(sem("over_act"), 1)
                    act.wait_ge(sem("over_pe"), 4 * it + 2)
                    A(sg[0:R_, 0, :], ps[0:R_, 2, :], ACT.Silu).then_inc(sem("over_act"), 1)
                    act.wait_ge(sem("over_pe"), 4 * it + 3)
                    A(hT[0][:, :, 0:R_], ps[:, 4, :].rearrange("p (k c) -> p k c", c=P)[:, :, 0:R_], ACT.Copy) \
                        .then_inc(sem("over_act"), 1)
                    act.wait_ge(sem("over_pe"), 4 * it + 4)
                    A(yst[0:R_, 0, :], ps[0:R_, 5:7, :].rearrange("p a b -> p (a b)"), ACT.Copy) \
                        .then_inc(sem("over_act"), 1)
                    act.wait_ge(sem("over_act"), 4 * it + 4)
                    act.dma_start(ysd[bass.ds(it * CAP + E * CAP, CAP), :], yst[0:R_, 0, :]) \
                        .then_inc(sem("o_yst"), 16)
                    act.wait_ge(sem("o_yst"), 16 * it + 16)
            for i in range(5):
                root("ln2", i)
                r = trows(i)
                act.wait_ge(sem("ln2_rs"), i + 1)
                T.up(A(x1[0:r, i, :], x1[0:r, i, :], ACT.Identity, scale=lnst[0:r, i % 2, 15:16],
                       bias=lnst[0:r, i % 2, 16:17]), "ln2_nrm")

        @block.vector
        def _(dve):
            T = Tally(dve)
            TT, TSc, STT = dve.tensor_tensor, dve.tensor_scalar, dve.scalar_tensor_tensor
            T.up(dve.memset(mixtmp[:, :, 0:1], 0.0), "zeroed")
            T.up(dve.memset(kT[:, 0:P], 0.0), "zeroed")
            T.up(dve.memset(Vt[:, 0, :], 0.0), "zeroed")
            dve.wait_ge(sem("ld_first"), 32)
            T.link(TSc(par[:, OMU:OMU + 14], par[:, MU:MU + 14], -1.0, 1.0, ALU.mult, ALU.add), "dve_step")
            for n in range(1, 10, 2):
                dve.wait_ge(sem("xt_ps"), n + 1)
                i, r = n // 2, (72 if n == 9 else P)
                T.up(dve.tensor_copy(xT[:, 4:8, i * P:i * P + r],
                                     ps[:, 6, :].rearrange("p (k c) -> p k c", c=P)[:, :, 0:r]), "xt_dve")

            def mix(ct):
                m = mix_index(ct)
                dve.wait_ge(sem("mix_scaled"), m + 1)
                if ct == 8 + 0:
                    pass
                d, omu, so = mix_dst(m), par[:, OMU + m:OMU + m + 1], 0
                STT(d[:, 0:NP_], ps[:, ct % 2, :], omu, mixtmp[:, m % 2, 0:512], ALU.mult, ALU.add)
                T.up(STT(d[:, NP_:NT].rearrange("p (b t) -> p b t", t=TS),
                         ps[:, 2, so:so + 72].rearrange("p (b t) -> p b t", t=9)[:, :, 1:9], omu,
                         mixtmp[:, m % 2, 520:592].rearrange("p (b t) -> p b t", t=9)[:, :, 0:8],
                         ALU.mult, ALU.add), "mixed")

            def kv_tok():
                dve.wait_ge(sem("kv_ps"), 1)
                T.up(dve.tensor_copy(Vt[:, 1:5, :], ps[:, 5, :].rearrange("p (t c) -> p t c", c=P)), "kv_tok")
                dve.wait_ge(sem("kv_ps"), 2)
                dve.tensor_copy(Vs[0:NS, :], ps[0:NS, 6, 0:P])
                dve.tensor_copy(Kt3, ps[:, 6, P:2 * P])
                T.up(dve.tensor_copy(Ks[0:NS, :], ps[0:NS, 6, 2 * P:3 * P]), "kv_tok")
                for h in range(2):
                    dve.wait_ge(sem("kv_ps"), 3 + h)
                    T.up(dve.tensor_copy(kcT[:, 4 * h:4 * h + 4, :], ps[:, 5 + h, :].rearrange("p (b c) -> p b c", c=P)),
                         "kv_tok")

            def row_max(n):
                dve.wait_ge(sem("s_ps"), n + 1)
                if n == 0:
                    dve.wait_ge(sem("ld_const"), 16)
                if n >= 2:
                    dve.wait_ge(sem("pt_ps"), 2 * (n - 1))
                w = 256 if n < 8 else 192
                Sn = Sb[:, n % 2, 0:4 * w].rearrange("p (g w) -> p g w", g=4)
                st = att_st[:, n % 2]
                if n < 8:
                    nb, kv = n // 2, n % 2
                    m = C("band")[:, 256 * (nb > 0):256 * (nb > 0) + 256].unsqueeze(1).to_broadcast([P, 4, 256])
                    T.link(TT(Sn, ps[:, 3:5, :].rearrange("p a (g w) -> p (a g) w", g=2), m, ALU.add), "s_read")
                    sink = par[:, SINK + 4 * kv:SINK + 4 * kv + 4]
                else:
                    dm = C("bandd").rearrange("p (b w) -> p b w", w=192)
                    for kv in range(2):
                        ins = TT(Sn[:, 2 * kv:2 * kv + 2, :],
                                 ps[:, 3 + kv, 0:384].rearrange("p (b w) -> p b w", w=192), dm, ALU.add)
                    T.link(ins, "s_read")
                    sink = par[:, SINKD:SINKD + 2].unsqueeze(2).to_broadcast([P, 2, 2])
                T.link(dve.tensor_reduce(st[:, 0, :], Sn, AX, ALU.max), "dve_step")
                f = (lambda a: a) if n < 8 else (lambda a: a.rearrange("p (k b) -> p k b", k=2))
                T.link(TT(f(st[:, 0, :]), f(st[:, 0, :]), sink, ALU.max), "dve_step")
                T.link(TSc(st[:, 1, :], st[:, 0, :], -1.0, None, ALU.mult), "dve_step")
                T.up(TT(f(st[:, 2, :]), sink, f(st[:, 1, :]), ALU.add), "s_max")

            def normalise(n):
                dve.wait_ge(sem("exp_done"), n + 1)
                w = 256 if n < 8 else 192
                Sn = Sb[:, n % 2, 0:4 * w].rearrange("p (g w) -> p g w", g=4)
                st = att_st[:, n % 2]
                T.link(TT(st[:, 5, :], st[:, 3, :], st[:, 4, :], ALU.add), "dve_step")
                T.link(dve.reciprocal(st[:, 6, :], st[:, 5, :]), "dve_step")
                T.up(TT(Sn, Sn, st[:, 6, :].unsqueeze(2).to_broadcast([P, 4, w]), ALU.mult), "p_ready")

            def pt_copy(n):
                dve.wait_ge(sem("pt_ps"), 2 * n + 2)
                if n >= 1:
                    dve.wait_ge(sem("pv_ps"), n)
                r = P if n < 8 else NS
                T.up(dve.tensor_copy(PT[0:r, 1, :], ps[0:r, 6, :]), "pt_dve")

            def pcol(o, j):
                return par[:, o + j:o + j + 1]

            def prep_a(j):
                if j == 0:
                    dve.wait_ge(sem("lora_evac"), 12)
                if j >= 2:
                    dve.wait_ge(sem("prep"), j - 1)
                T.up(TSc(A4[:, j, :], K4[:, j, :], pcol(KK_, j), None, ALU.mult), "kraw")
                T.link(dve.tensor_tensor_scan(PM[:, j % 2, :], C("reset"), SG4[:, j, :], 0.0, ALU.mult, ALU.add), "cum")
                T.up(TT(SG4[:, j, :], PM[:, j % 2, :], SG4[:, j, :], ALU.subtract), "cum")
                if j >= 1:
                    dve.wait_ge(sem("hsum_ps"), 2 * j)
                s = SQ[:, 1, :]
                T.link(TSc(s, B4[:, j, :], -1.0, pcol(KA, j), ALU.add, ALU.mult), "dve_step")
                T.link(STT(K4[:, j, :], s, 1.0, K4[:, j, :], ALU.add, ALU.mult), "dve_step")
                T.up(STT(s, R4[:, j, :], pcol(RK, j), K4[:, j, :], ALU.mult, ALU.mult), "hsum_in_b")

            def prep_b(j):
                s = SQ[:, 0, :]
                dve.wait_ge(sem("norm_read"), j + 1)
                T.link(TSc(s, s, 1e-12, None, ALU.max), "dve_step")
                T.link(dve.reciprocal(s, s), "dve_step")
                T.link(TT(A4[:, j, :], A4[:, j, :], s, ALU.mult), "dve_step")
                T.link(TT(B4[:, j, :], B4[:, j, :], A4[:, j, :], ALU.mult), "dve_step")
                dve.wait_ge(sem("pexp"), 2 * j + 2)
                TT(R4[:, j, :], R4[:, j, :], PM[:, j % 2, :], ALU.mult)
                TT(K4[:, j, :], K4[:, j, :], PI[:, j % 2, :], ALU.mult)
                TT(B4[:, j, :], B4[:, j, :], PI[:, j % 2, :], ALU.mult)
                dve.tensor_copy(PL[:, j, 0:8], PM[:, j % 2, CHUNK - 1:NP_:CHUNK])
                dve.tensor_copy(PL[:, j, 8:16], PM[:, j % 2, NP_ + TS - 1:NT:TS])
                T.link(STT(A4[:, j, :], A4[:, j, :], -1.0, SG4[:, j, :], ALU.mult, ALU.mult), "prep")

            def prep_c(j):
                dve.wait_ge(sem("hsum_ps"), 2 * j + 2)
                TT(SG4[:, j, 0:NP_], ps[:, 7, :], V4[:, j, 0:NP_], ALU.mult)
                T.up(TT(SG4[:, j, NP_:NT], ps[:, 2, 0:NS], V4[:, j, NP_:NT], ALU.mult), "bonus_read")

            for ct in range(COLT):
                if ct < 2:
                    mix(ct)
                elif ct < 8:
                    if ct == 7:
                        kv_tok()
                else:
                    k = ct - RW0
                    mix(ct)
                    if 1 <= k < 10:
                        normalise(k - 1)
                    if k < 9:
                        row_max(k)
                    if 1 <= k < 10:
                        pt_copy(k - 1)
                    if k % 3 == 2:
                        prep_a(k // 3)
                    if k >= 3 and k % 3 == 0:
                        prep_b(k // 3 - 1)
                    if k >= 4 and k % 3 == 1:
                        prep_c(k // 3 - 1)
            prep_b(3)
            prep_c(3)
            T.up(dve.memset(gn_eps, GN_EPS), "zeroed")

            def wy(q):
                R, L = rows(q), levels(q)
                tag = "" if q < 4 else "_s"
                if q == 0:
                    dve.wait_ge(sem("kv_out"), 64)
                    dve.wait_ge(sem("pv_ps"), 9)
                up4 = C("upper" + tag)[0:R]
                low = C("lower" + tag)[0:R].unsqueeze(1).to_broadcast([R, 4, R])
                lev = C("level").rearrange("p (l c) -> p l c", l=6)

                def b4(a):
                    return a[0:R, 0:4 * R].rearrange("p (u c) -> p u c", u=4)

                def lv(l):
                    return lev[0:R, l, 0:R].unsqueeze(1).to_broadcast([R, 4, R])

                for n in range(2, 4):
                    dve.wait_ge(sem("tok_ps"), 4 * q + n + 1)
                    T.up(dve.tensor_copy(TOK[n][0:R], ps[0:R, n, :].rearrange("p (u c) -> p u c", u=4)), "tok_dve")
                for p in range(2):
                    dve.wait_ge(sem("n_ps"), 2 * q + p + 1)
                    T.link(TT(b4(NM[p]), b4(ps[:, 4 + p, :]), low, ALU.mult), "dve_step")
                    T.link(TT(b4(X[p]), b4(NM[p]), lv(0), ALU.mult), "dve_step")
                    T.up(TT(b4(X[p]), b4(X[p]), ident[0:R, 0:R].unsqueeze(1).to_broadcast([R, 4, R]), ALU.add),
                         "x_ready")
                for G, pn, en in ((BG, "bg_ps", "bg_ev"), (KG, "kg_ps", "kg_ev")):
                    for p in range(2):
                        dve.wait_ge(sem(pn), 2 * q + p + 1)
                        T.up(TT(G[p][0:R, 0:8 * R].rearrange("p (a b) -> p a b", a=2),
                                ps[0:R, 2 * p:2 * p + 2, 0:4 * R],
                                up4.unsqueeze(1).to_broadcast([R, 2, 4 * R]), ALU.mult), en)
                for l in range(1, L + 1):
                    for p in range(2):
                        dve.wait_ge(sem("w1_ps"), 10 * q + 2 * (l - 1) + p + 1)
                        if l > 1:
                            dve.wait_ge(sem("xl_ps"), 10 * q + 2 * (l - 2) + p + 1)
                        T.up(TT(b4(W1[p]), b4(ps[:, 4 + p, :]), lv(l), ALU.mult), "w1_ev")
                    for p in range(2):
                        dve.wait_ge(sem("xl_ps"), 10 * q + 2 * (l - 1) + p + 1)
                        if l < L:
                            T.up(TT(b4(X[p]), b4(ps[:, 6 + p, :]), b4(X[p]), ALU.add), "x_ready")
                        else:
                            T.up(TT(b4(XT[p]), b4(ps[:, 6 + p, :]), b4(XT[p]), ALU.add), "t_ready")
                dve.wait_ge(sem("post_ps"), 4 * q + 1)
                T.up(TT(units(R4, q), ps[:, 2, 0:4 * R].rearrange("p (u c) -> p u c", u=4), units(R4, q), ALU.add),
                     "post_dve")
                if q == 4:
                    return
                dve.wait_ge(sem("post_ps"), 4 * q + 3)
                for cp in range(2):
                    T.up(TT(A4[:, q, 0:NP_].rearrange("p (u c k) -> p u c k", u=4, c=2)[:, :, cp, :],
                            ps[:, 6 + cp, 0:256].rearrange("p (u k) -> p u k", u=4),
                            C("ident2").unsqueeze(1).to_broadcast([P, 4, HD]), ALU.add), "post_dve")
                dve.wait_ge(sem("post_ps"), 4 * q + 4)
                for cp in range(2):
                    T.up(TT(B4[:, q, 0:NP_].rearrange("p (u c k) -> p u c k", u=4, c=2)[:, :, cp, :],
                            ps[:, 4 + cp, 0:256].rearrange("p (u k) -> p u k", u=4),
                            PL[:, q, cp:8:2].unsqueeze(2).to_broadcast([P, 4, HD]), ALU.mult), "post_dve")

            for q in range(5):
                wy(q)

            dve.wait_ge(sem("ys_ps"), 1)
            dve.wait_ge(sem("post_act"), 5)
            T.up(TT(V4[:, :, NP_:NT], ps[:, 0, 0:256].rearrange("p (u t) -> p u t", u=4), V4[:, :, NP_:NT], ALU.add),
                 "ys_ev")
            batch = C("batch")[0:NS].unsqueeze(2).to_broadcast([NS, NB, HD])

            def bv(a):
                return a[0:NS, :].rearrange("p (b v) -> p b v", b=NB)

            def z1_copy(u):
                dve.wait_ge(sem("z1_ps"), 2 * u + 2)
                Zu = Z0[:, u]
                T.link(TT(Zu, ps[:, 6 + u % 2, :].rearrange("p (b v) -> p b v", b=NB), Zu, ALU.add), "dve_step")
                T.up(TT(Zu, Zu, PL[:, u, 8:16].unsqueeze(2).to_broadcast([P, NB, HD]), ALU.mult), "z1_ev")

            def z_step(c):
                dve.wait_ge(sem("z_ps"), c)
                T.link(TT(Zp[:, c], ps[:, 1, 0:256].rearrange("p (j v) -> p j v", j=4),
                          PL[:, :, c:c + 1].to_broadcast([P, 4, HD]), ALU.mult), "dve_step")
                T.up(TT(Zp[:, c], Zp[:, c], B4[:, :, c * HD:(c + 1) * HD], ALU.add), "z_ready")

            for n in range(8):
                u, p = n // 2, n % 2
                dve.wait_ge(sem("u_ps"), n + 1)
                if n >= 2:
                    dve.wait_ge(sem("z1_ps"), n - 1)
                H = GH[p][0:NS, u * P + HD:(u + 1) * P].unsqueeze(1).to_broadcast([NS, NB, HD])
                T.link(TT(bv(W1[p]), bv(ps[:, 4 + p, :]), H, ALU.add), "dve_step")
                TT(bv(NM[p]), TOK[3][0:NS, u, par_rows(p)].unsqueeze(1).to_broadcast([NS, NB, HD]), batch, ALU.mult)
                T.up(TT(bv(W1[p]), bv(W1[p]), batch, ALU.mult), "um_ev")
                if n >= 1:
                    z_step(n)
                if p == 0 and u >= 1:
                    z1_copy(u - 1)
            z1_copy(3)

            for j in range(4):
                dve.wait_ge(sem("y_ps"), j + 1)
                T.up(TT(V4[:, j, CHUNK:NP_], ps[:, (4, 5, 2, 3)[j], CHUNK:NP_], V4[:, j, CHUNK:NP_], ALU.add), "y_ev")

            for j in range(4):
                y, s = V4[:, j, :], SQ[:, 1, :]
                dve.wait_ge(sem("hm_ps"), 2 * j + 1)
                if j == 0:
                    dve.wait_ge(sem("y_ev"), 4)
                T.up(STT(y, ps[:, 0:2, :].rearrange("p a b -> p (a b)")[:, 0:NT], -1.0 / HD, y, ALU.mult, ALU.add),
                     "centred")
                dve.wait_ge(sem("centred"), j + 1)
                dve.wait_ge(sem("var_read"), j + 1)
                T.link(dve.reciprocal(s, s), "dve_step")
                T.up(STT(y, y, pcol(GNG, j), s, ALU.mult, ALU.mult), "gn_y")

            T.up(dve.memset(ln_eps, LN_EPS), "zeroed")
            T.up(dve.memset(rt[:, :, :], 0.0), "zeroed")
            dve.wait_ge(sem("zeroed"), 6)

            def norm(i, n, lnp):
                r = trows(i)
                x, st = x1[0:r, i, :], lnst[0:r, i % 2]
                for h in range(2):
                    ins = dve.bn_stats(st[:, 6 * h:6 * h + 6], x[:, h * 512:(h + 1) * 512])
                T.link(ins, "dve_step")
                T.up(dve.bn_aggr(st[:, 12:14], st[:, 0:12]), n + "_var")
                dve.wait_ge(sem("ln1_sd"), i + 1)
                T.link(dve.reciprocal(st[:, 15:16], st[:, 14:15]), "dve_step")
                T.link(TSc(x, x, st[:, 12:13], st[:, 15:16], ALU.subtract, ALU.mult), "dve_step")
                T.link(TT(x, x, lnp[0:r, 0, :], ALU.mult), "dve_step")
                T.up(TT(x, x, lnp[0:r, 1, :], ALU.add), ("x1_ready", "y_done")[n == "ln2"])

            def x1t_copy(i):
                r = trows(i)
                dve.wait_ge(sem("x1t_ps"), 2 * i + 2)
                if i:
                    dve.wait_ge(sem("logit_ps"), i)
                T.up(dve.tensor_copy(x1T[:, 4:8, 0:r], ps[:, 3, :].rearrange("p (k c) -> p k c", c=P)[:, :, 0:r]),
                     "x1t_dve")

            def lg_copy(i):
                r = trows(i)
                dve.wait_ge(sem("logit_ps"), i + 1)
                T.up(dve.tensor_copy(rt[0:r, i, :], ps[0:r, 0, 0:E]), "lg_ev")

            dve.wait_ge(sem("ld_ln1"), 32)
            for i in range(5):
                r = trows(i)
                dve.wait_ge(sem("op_ps"), i + 1)
                dve.wait_ge(sem(f"ld_rows{i % 2}"), 16 * ((3, 2)[i % 2] + i // 2 + 1))
                T.link(STT(x1[0:r, i, :], xres[0:r, i % 2, :], ALPHA,
                           ps[0:r, 4 + 2 * (i % 2):6 + 2 * (i % 2), :].rearrange("p a b -> p (a b)"), ALU.mult, ALU.add),
                       "pre_ln")
                norm(i, "ln1", ln1)
                if i >= 1:
                    x1t_copy(i - 1)
                if i >= 2:
                    lg_copy(i - 2)
            lg_copy(3)
            x1t_copy(4)
            lg_copy(4)

            L = lambda ins: T.link(ins, "dve_step")
            def bE(a):
                return a.unsqueeze(2).to_broadcast([P, 5, E])
            def q4(a):
                return a.rearrange("p i (g e) -> p (i g) e", g=4)
            def f20(a):
                return a.rearrange("p i g -> p (i g)")
            def b4_(a):
                return f20(a).unsqueeze(2).to_broadcast([P, 20, 4])
            iota20 = C("iota4").unsqueeze(1).to_broadcast([P, 20, 4])
            iota5 = C("iota4").unsqueeze(1).to_broadcast([P, 5, 4])
            dve.wait_ge(sem("lg_ev"), 5)
            L(dve.tensor_reduce(S5[:, 0, :], rt[:, :, :], AX, ALU.max))
            T.up(TT(PR, rt[:, :, :], bE(S5[:, 0, :]), ALU.subtract), "lg_max")
            dve.wait_ge(sem("lg_exp"), 1)
            L(dve.tensor_reduce(S5[:, 1, :], PR, AX, ALU.add))
            L(dve.reciprocal(S5[:, 2, :], S5[:, 1, :]))
            L(TT(PR, PR, bE(S5[:, 2, :]), ALU.mult))
            L(TT(SEL, PR, par[:, RB:RB + E].unsqueeze(1).to_broadcast([P, 5, E]), ALU.add))

            def first_max(v, m, c, hot, bm, io):
                L(dve.tensor_reduce(m, v, AX, ALU.max))
                L(TT(c, v, bm(m), ALU.is_equal))
                L(STT(c, c, -8.0, io, ALU.mult, ALU.add))
                L(dve.tensor_reduce(f20(C1) if hot is not BGR else S5[:, 4, :], c, AX, ALU.min))
                return c

            b20 = lambda m: m.unsqueeze(2).to_broadcast([P, 20, 4])
            first_max(q4(SEL), f20(G1), q4(CN), O1, b20, iota20)
            L(TT(q4(O1), q4(CN), b4_(C1), ALU.is_equal))
            L(STT(SEL, O1, NEG, SEL, ALU.mult, ALU.add))
            first_max(q4(SEL), f20(G2), q4(CN), O2, b20, iota20)
            L(TT(q4(O2), q4(CN), b4_(C1), ALU.is_equal))
            L(TT(SC, G1, G2, ALU.add))
            b5 = lambda m: m.unsqueeze(2).to_broadcast([P, 5, 4])
            first_max(SC, S5[:, 3, :], CNB, BGR, b5, iota5)
            L(TT(BGR, CNB, b5(S5[:, 4, :]), ALU.is_equal))
            L(TT(BGR, BGR, C("valid").unsqueeze(2).to_broadcast([P, 5, 4]), ALU.mult))
            L(TT(q4(M1), q4(O1), b4_(BGR), ALU.mult))
            L(TT(q4(M2), q4(O2), b4_(BGR), ALU.mult))
            T.up(TT(rt[:, :, :], M1, M2, ALU.add), "chosen")
            for n, M in ((0, M1), (1, M2)):
                L(TT(TI[n], M, C("tokf").unsqueeze(2).to_broadcast([P, 5, E]), ALU.mult))
            dve.wait_ge(sem("rank_ps"), 1)
            L(dve.tensor_copy(CN, ps[:, RANKB, 0:5 * E].rearrange("p (i e) -> p i e", e=E)))
            for n, M in ((0, M1), (1, M2)):
                L(TT(EQ, M, CN, ALU.mult))
                L(dve.tensor_reduce(S5[:, n, :], EQ, AX, ALU.add))
                T.up(TT(OH[n], C("rank").unsqueeze(1).to_broadcast([P, 5, P]),
                        S5[:, n, :].unsqueeze(2).to_broadcast([P, 5, P]), ALU.is_equal), "idx_in")
            L(dve.tensor_copy(CT, ps[:, RANKB, 5 * E:6 * E]))
            dve.wait_ge(sem("idx_ps"), 1)
            T.up(dve.tensor_copy(idx_i[0:CAP, 0:E], ps[0:CAP, 2, 0:E]), "idx_ready")
            for n, M in ((0, M1), (1, M2)):
                L(TT(EQ, M, PR, ALU.mult))
                L(dve.tensor_reduce(S5[:, 6 + n, :], EQ, AX, ALU.add))
            L(TT(S5[:, 5, :], S5[:, 6, :], S5[:, 7, :], ALU.add))
            L(TT(S5[:, 5, :], S5[:, 5, :], C("spare"), ALU.add))
            L(dve.reciprocal(S5[:, 8, :], S5[:, 5, :]))
            for n in range(2):
                L(TT(S5[:, 9 + n, :], S5[:, 6 + n, :], S5[:, 8, :], ALU.mult))
            L(TSc(NV, CT, float(CAP), None, ALU.is_gt))
            for n in range(2, (NT + CAP - 1) // CAP):
                L(STT(NV, CT, float(n * CAP), NV, ALU.is_gt, ALU.add))
            L(TT(TR, C("tri").rearrange("p (a b) -> p a b", b=E), NV.unsqueeze(1).to_broadcast([P, E, E]), ALU.mult))
            L(dve.tensor_reduce(ST, TR, AX, ALU.add))
            L(TSc(B2, ST, float(CAP), float((E - 1) * CAP), ALU.mult, ALU.add))
            L(TT(B2, B2, C("slot0"), ALU.subtract))
            bi = lambda a: a.unsqueeze(1).to_broadcast([P, 5, E])
            L(TSc(PO, CN, float(CAP), None, ALU.is_ge))
            L(TT(PO, PO, bi(B2), ALU.mult))
            L(TT(PO, PO, CN, ALU.add))
            L(TT(PO, PO, bi(C("slot0")), ALU.add))
            for n, M in ((0, M1), (1, M2)):
                L(TT(EQ, M, PO, ALU.mult))
                L(dve.tensor_reduce(S5[:, n, :], EQ, AX, ALU.add))
                L(dve.tensor_copy(slot_i[:, :, n], S5[:, n, :]))
            L(dve.tensor_reduce(S5[:, 11, 0:1], NV, AX, ALU.add))
            L(dve.tensor_copy(flag_i, S5[:, 11, 0:1]))
            L(TT(IT, ST.unsqueeze(1).to_broadcast([P, OVER, E]), C("item").unsqueeze(2).to_broadcast([P, OVER, E]),
                 ALU.is_le))
            L(dve.tensor_reduce(IV[:, 0, 0:OVER], IT, AX, ALU.add))
            L(TSc(IV[:, 1, 0:OVER], IV[:, 0, 0:OVER], -1.0, None, ALU.add))
            T.link(dve.tensor_copy(eid_i, IV[:, 1, 0:OVER]), "slots")

            R_ = CAP

            def xg_copy(e, s, first=False):
                dve.wait_ge(sem("xg_turn"), e + 1)
                if not first:
                    dve.wait_ge(sem("up_ps"), e - 1)
                T.up(dve.tensor_copy(xgT[s][:, 4:8, 0:R_], ps[:, 1, :].rearrange("p (k c) -> p k c", c=P)[:, :, 0:R_]),
                     "xgT_dve")

            def h_mul(e, s, first=False):
                dve.wait_ge(sem("silu"), e + 1)
                dve.wait_ge(sem("up_ps"), e + 1)
                if not first:
                    dve.wait_ge(sem("ht_ps"), e - 1)
                T.up(TT(hh[0:R_, s, :], sg[0:R_, s, :], ps[0:R_, 3, :], ALU.mult), "h_ready")

            def y_copy(e, s, first=False):
                dve.wait_ge(sem("down_ps"), e + 1)
                if not first:
                    dve.wait_ge(sem(f"y_st{s}"), e * 8 - 8 * s)
                T.up(dve.tensor_copy(yst[0:R_, s, 512:D], ps[0:R_, 6, :]), "y_dve")

            dve.wait_ge(sem("x1_st"), 80)
            xg_copy(0, 0, True)
            for i in range(5):
                r = trows(i)
                T.up(TSc(x1[0:r, i, :], x1[0:r, i, :], ALPHA, None, ALU.mult), "dve_step")
            scaled = T.n["dve_step"]
            h_mul(0, 0, True)
            xg_copy(1, 1, True)
            h_mul(1, 1, True)
            xg_copy(2, 0)
            y_copy(0, 0, True)
            h_mul(2, 0)
            xg_copy(3, 1)
            y_copy(1, 1, True)
            h_mul(3, 1)
            xg_copy(4, 0)
            y_copy(2, 0)
            with dve.Fori(2, E // 2 - 1) as it:
                for s in range(2):
                    e = 2 * it + s
                    h_mul(e, s)
                    xg_copy(e + 1, 1 - s)
                    y_copy(e - 1, 1 - s)
            h_mul(E - 2, 0)
            xg_copy(E - 1, 1)
            y_copy(E - 3, 1)
            h_mul(E - 1, 1)
            y_copy(E - 2, 0)
            y_copy(E - 1, 1)
            more = dve.value_load(flag_i[0:1, :], min_val=0, max_val=OVER)
            with dve.If(more > 0):
                with dve.Fori(0, OVER) as it:
                    dve.wait_ge(sem("over_act"), 4 * it + 2)
                    TT(hh[0:R_, 0, :], sg[0:R_, 0, :], ps[0:R_, 3, :], ALU.mult).then_inc(sem("o_h"), 1)
            dve.wait_ge(sem("dve_step"), scaled)
            for i in range(6):
                if i < 5:
                    r = trows(i)
                    x, st = x1[0:r, i, :], lnst[0:r, i % 2]
                    dve.wait_ge(sem(f"yab{min(i, 2)}"), 32 if i < 2 else 96)
                    T.link(STT(x, yab[0:r, i, 0, :], S5[0:r, 9, i:i + 1], x, ALU.mult, ALU.add), "dve_step")
                    T.link(STT(x, yab[0:r, i, 1, :], S5[0:r, 10, i:i + 1], x, ALU.mult, ALU.add), "dve_step")
                    if i >= 2:
                        dve.wait_ge(sem("ln2_nrm"), i - 1)
                    for h in range(2):
                        ins = dve.bn_stats(st[:, 6 * h:6 * h + 6], x[:, h * 512:(h + 1) * 512])
                    T.link(ins, "dve_step")
                    T.up(dve.bn_aggr(st[:, 12:14], st[:, 0:12]), "ln2_var")
                if i >= 1:
                    st = lnst[0:trows(i - 1), (i - 1) % 2]
                    dve.wait_ge(sem("ln2_sd"), i)
                    T.link(dve.reciprocal(st[:, 15:16], st[:, 14:15]), "dve_step")
                    T.up(STT(st[:, 16:17], st[:, 12:13], -1.0, st[:, 15:16], ALU.mult, ALU.mult), "ln2_rs")


def kernel(**inputs):
    import concourse.bacc as _bacc
    from concourse.bass_utils import run_bass_kernel_spmd as _run

    a = {k: np.asarray(v) for k, v in inputs.items()}
    q = [np.r_[j * 64:j * 64 + 64, 256 + j * 64:256 + j * 64 + 64] for j in range(4)]
    rw = 768
    wa = np.r_[rw + 512:rw + 576, rw + 1600:rw + 1664]
    gl = np.arange(rw + 1664, rw + 1792)
    rwkv = [rw + o + j * 128 + np.arange(128) for j in range(4) for o in (0, 576, 1088)]
    tiles = [wa, gl] + q + [np.arange(512, 640), np.arange(640, 768)] + rwkv
    perm = np.concatenate(tiles)
    win = a["w_in"][0][:, perm].reshape(KT, P, COLT, P).transpose(2, 1, 0, 3).reshape(COLT, P, KT * P)
    mu = a["mu_rwkv"][0][np.concatenate([wa, gl] + rwkv) - rw].reshape(14, P).T
    vec = [a[n].reshape(4, P).T for n in ("decay_w0", "aaa_a0", "k_k", "k_a", "r_k", "gn_g", "gn_b")]
    sinks = a["sinks"][0]
    sd = np.stack([np.tile(np.repeat(sinks[kv * 4:kv * 4 + 4], 8), 4) for kv in range(2)], 1)
    params = np.concatenate([mu, np.zeros_like(mu)] + vec + [np.tile(sinks[None], (P, 1)), sd,
                             np.tile(a["router_bias"][None], (P, 1))], 1)
    table = constant_table()
    arrays = {
        "consts": np.concatenate([table[k] for k in CAT], 1),
        "params": params, "win": win,
        "xs9": np.concatenate([a["state_shift"][0][:, None], a["x_sample"]], 1).reshape(72, D),
    }
    wo = a["w_o"][0]
    rows_ = np.concatenate(q + [512 + np.arange(512)])
    arrays["wo"] = wo[rows_].reshape(KT, P, D).transpose(1, 0, 2).reshape(P, KT * D)
    arrays["tokid"] = (np.arange(5)[None] * P + np.arange(P)[:, None]).astype(np.int32)
    for n in ("x_prompt", "x_sample", "state_wkv", "w_router", "w_gate", "w_up", "w_down", "ln1_g", "ln1_b",
              "ln2_g", "ln2_b", "cache_k", "cache_v", "decay_w2", "aaa_a2", "gate_g2"):
        arrays[n] = a[n]
    nc = _bacc.Bacc("TRN2", target_bir_lowering=False, num_devices=1)
    arrays = {f"in_{k}": np.ascontiguousarray(v) for k, v in arrays.items()}
    i_ = {k[3:]: nc.dram_tensor(k, v.shape, mybir.dt.from_np(v.dtype), kind="ExternalInput").ap()
          for k, v in arrays.items()}
    o_ = {n: nc.dram_tensor("out_" + n, s, F32, kind="ExternalOutput").ap() for n, s in OUTS}
    hymba_step(nc, i_, o_)
    r = _run(nc, [arrays], core_ids=[0])
    return tuple(r.results[0]["out_" + n] for n, _ in OUTS)
```

```python
from contextlib import ExitStack
import math

import numpy as np

import concourse.bass as bass
from concourse import mybir

ALU = mybir.AluOpType
ACT = mybir.ActivationFunctionType
AX = mybir.AxisListType.X
F32 = mybir.dt.float32
I32 = mybir.dt.int32
BF16 = mybir.dt.bfloat16

P = 128
D = 1024
KT = D // P
NP_ = 512
NS = 64
NB = 8
TS = NS // NB
NT = NP_ + NS
HD = 64
CHUNK = 64
CHUNKS = NP_ // CHUNK
WIN = 128
E = 16
FF = 512
FT = FF // P
CAP = 128
OVER = 2 * NT // (CAP + 1)
BLOCKS = E + OVER
SLOTS = BLOCKS * CAP
COLT = 20
RING = 6
RANKB = 1
ALPHA = 2.0 ** 0.25
DECAY_SCALE = math.exp(-0.5)
GN_EPS = 64e-5
LN_EPS = 1e-5
NEG = -1e30
ATT_SCALE = HD ** -0.5

MU, OMU, W0, A0, KK_, KA, RK, GNG, GNB, SINK, SINKD, RB, NPV = (
    0, 14, 28, 32, 36, 40, 44, 48, 52, 56, 64, 66, 82)


def constant_table():
    i = np.arange(P)
    s, t = i[:, None], i[None, :]
    t_ = {}
    t_["ident"] = np.eye(P)
    for tag, n, c in (("", P, CHUNK), ("_s", NS, TS)):
        same = (s // c == t // c)[:, :n]
        up = np.concatenate([(same & (s <= t[:, :n])), (same & (s < t[:, :n]))] * 2, 1).astype(float)
        t_["upper" + tag] = up
    lev = []
    for m in (1, 2, 4, 8, 16, 32):
        lev.append(((s // (2 * m) == t // (2 * m)) & (s // m % 2 == 1) & (t // m % 2 == 0)).astype(float))
    t_["level"] = np.concatenate(lev, 1)
    kj = np.arange(2 * P)[None, :]
    diff = s + P - kj
    band = (diff >= 0) & (diff < WIN)
    t_["band"] = np.where(np.concatenate([band & (kj >= P), band], 1), 0.0, NEG)
    row = np.arange(P)
    rb, rt = row // 32, row % 8
    dm = np.full((P, 2, 192), NEG)
    w = np.arange(WIN)
    for b2 in range(2):
        dm[:, b2, :WIN] = np.where(w[None, :] > rt[:, None], 0.0, NEG)
        c = np.arange(NS)
        ok = (c[None, :] // TS == (b2 * 4 + rb)[:, None]) & (c[None, :] % TS <= rt[:, None])
        dm[:, b2, WIN:] = np.where(ok, 0.0, NEG)
    t_["bandd"] = dm.reshape(P, 384)
    t_["ident2"] = (s % HD == np.arange(HD)[None, :]).astype(float)
    t_["blk"] = (s // HD == t // HD).astype(float)
    t_["before"] = (s < t).astype(float)
    t_["ones"] = np.ones((P, P))
    t_["reset"] = np.ones((P, NT))
    t_["reset"][:, 0:NP_:CHUNK] = 0
    t_["reset"][:, NP_::TS] = 0
    t_["batch"] = (s % NS // TS == np.arange(NB)[None, :]).astype(float)
    t_["rank"] = np.tile(np.arange(float(P)), (P, 1))
    tok = np.arange(5)[None, :] * P + i[:, None]
    t_["tok_high"] = (tok // 32 * 32).astype(float)
    t_["tok_low"] = (tok % 32).astype(float)
    t_["iota4"] = np.tile(np.arange(4.0), (P, 1))
    t_["slot0"] = np.tile(np.arange(E) * float(CAP), (P, 1))
    t_["item"] = np.tile(np.arange(float(OVER)), (P, 1))
    t_["tri"] = np.tile((np.arange(E)[None, :] < np.arange(E)[:, None]).astype(float).reshape(1, -1), (P, 1))
    tok = np.arange(5)[None, :] * P + i[:, None]
    t_["valid"] = (tok < NT).astype(float)
    t_["spare"] = (tok >= NT).astype(float)
    return {k: np.ascontiguousarray(v, dtype=np.float32) for k, v in t_.items()}


def constant_layout():
    off, at = 0, {}
    for k, v in constant_table().items():
        at[k] = (off, v.shape[1])
        off += v.shape[1]
    return at, off


CAT, NCONST = constant_layout()

OUTS = [("y_prompt", (1, NP_, D)), ("y_sample", (NB, TS, D)), ("k_prompt", (1, 1, WIN, 2, HD)),
        ("v_prompt", (1, 1, WIN, 2, HD)), ("wkv_prompt", (1, 1, 8, HD, HD)), ("shift_prompt", (1, 1, D)),
        ("k_sample", (1, NB, TS, 2, HD)), ("v_sample", (1, NB, TS, 2, HD)),
        ("wkv_sample", (1, NB, 8, HD, HD)), ("shift_sample", (1, NB, D))]


def hymba_step(nc, i_, o_):
    with ExitStack() as ctx:
        sems = {}

        def sem(name):
            if name not in sems:
                sems[name] = ctx.enter_context(nc.semaphore(name))
            return sems[name]

        top = [0]

        def take(n):
            top[0] += n
            return top[0] - n

        o_const, o_par = take(NCONST), take(NPV)
        o_xt, o_mixa, o_ring = take(KT * 584), take(4 * NT), take(8192)
        o_rwkv, o_u = take(7 * 4 * NT), take(12288)
        o_temp = take(6 * NT)
        o_mixtmp = take(2 * 592)
        arena = ctx.enter_context(nc.sbuf_tensor("arena", [P, top[0]], F32))

        def v2(off, n):
            return arena[:, off:off + n]

        def v3(off, a, b):
            return v2(off, a * b).rearrange("p (a b) -> p a b", b=b)

        def v4(off, a, b, c):
            return v2(off, a * b * c).rearrange("p (a b c) -> p a b c", b=b, c=c)

        def C(name):
            o, w = CAT[name]
            return v2(o_const + o, w)

        ident = C("ident")
        consts, par = v2(o_const, NCONST), v2(o_par, NPV)
        xT = v3(o_xt, KT, 584)
        mixA = v3(o_mixa, 4, NT)
        ring = v4(o_ring, RING, KT, P)
        xst = [v2(o_ring + n * D, D) for n in (6, 7, 5, 4)]
        R4, K4, V4, A4, B4, SG4, G4 = (v3(o_rwkv + n * 4 * NT, 4, NT) for n in range(7))
        WA, GL = A4[:, 0, :], A4[:, 1, :]
        u = o_u
        qT = v3(u, 4, NP_); u += 4 * NP_
        qTs = v4(u, NB, 4, TS); u += 4 * NS
        kT = v2(u, P + NP_); u += P + NP_
        kTs = v2(u, NS); u += NS
        vT = v2(u, NT); u += NT
        Vt = v3(u, 5, P); u += 5 * P
        Vs = v2(u, P); u += P
        Kt3 = v2(u, P); u += P
        Ks = v2(u, P); u += P
        kc = v3(u, NB, P); u += NB * P
        vc = v3(u, NB, P); u += NB * P
        kcT = v3(u, NB, P); u += NB * P
        Sb = v3(u, 2, 1024); u += 2048
        PT = v3(u, 2, 512); u += 1024
        LW = v2(u, 512); u += 512
        GW = v2(u, 512); u += 512
        assert u <= o_u + 12288
        PM, PI, SQ = (v3(o_temp + 2 * n * NT, 2, NT) for n in range(3))
        mixtmp = v3(o_mixtmp, 2, 592)
        u = o_u
        TOK = [v3(u + n * 512, 4, P) for n in range(4)]; u += 2048
        BG = [v2(u + n * 1024, 1024) for n in range(2)]; u += 2048
        KG = [v2(u + n * 1024, 1024) for n in range(2)]; u += 2048
        o_x = u + 2 * 512
        NM, X, XT, W1, RHS, GH = ([v2(u + (2 * k + n) * 512, 512) for n in range(2)] for k in range(6))
        rwkv7 = v3(o_rwkv, 7, 4 * NT)
        Z0 = v4(o_temp, 4, NB, HD)
        stage = [v2(o_xt, 1024), v2(o_xt + 1024, 1024), v2(o_mixtmp, 1024), v2(o_temp + 2048, 1024)]
        Zp = v4(o_xt + 4 * NT, 8, 4, HD)
        mixR = v3(o_xt, 4, NT)
        GQ = RHS[0].rearrange("p (u c) -> p u c", u=4)
        YT = [(BG, KG)[n // 4][n // 2 % 2][NS:2 * NS, (n % 2) * 512:(n % 2) * 512 + 512] for n in range(8)]
        SD = [SQ[:, 1, :], v2(o_x, NT)]
        wo = v3(o_ring, KT, D)
        ln1 = v3(o_xt + 4 * NT, 2, D)
        x1 = v3(o_rwkv + 24576, 5, D)
        xres = v3(o_rwkv + 24576 + 5 * D, 2, D)
        x1T = v3(o_mixtmp, KT, P)
        WG = [v3(o_rwkv + n * 4096, KT, FF) for n in range(2)]
        WU = [v3(o_rwkv + (2 + n) * 4096, KT, FF) for n in range(2)]
        WD = [v3(o_rwkv + (4 + n) * 4096, FT, D) for n in range(2)]
        u = o_xt
        xg = v3(u, 2, D); u += 2 * D
        xgT = [v3(u + n * D, KT, P) for n in range(2)]; u += 2 * D
        sg = v3(u, 2, FF); u += 2 * FF
        hh = v3(u, 2, FF); u += 2 * FF
        hT = [v3(u + n * FF, FT, P) for n in range(2)]; u += 2 * FF
        yst = v3(u, 2, D); u += 2 * D
        yab = v4(o_rwkv, 5, 2, D)
        ln2 = v3(u, 2, D); u += 2 * D

        def small(*dims):
            nonlocal u
            n = 1
            for d_ in dims:
                n *= d_
            u += n
            assert u <= o_ring + 8192 + 0
            return v2(u - n, n) if len(dims) == 1 else v3(u - n, *dims) if len(dims) == 2 else v4(u - n, *dims)

        wr = ctx.enter_context(nc.sbuf_tensor("wr", [P, KT, E], F32))[:, :, :]
        rt = ctx.enter_context(nc.sbuf_tensor("rt", [P, 5, E], F32))
        lnst = ctx.enter_context(nc.sbuf_tensor("lnst", [P, 2, 20], F32))
        ln_eps = ctx.enter_context(nc.sbuf_tensor("ln_eps", [P, 1], F32))[:, :]
        tokid = ctx.enter_context(nc.sbuf_tensor("tokid", [P, 5], I32))
        zidx = ctx.enter_context(nc.sbuf_tensor("zidx", [P, BLOCKS], I32))
        PR, SEL, CN, O1, O2, EQ, M1, M2, PO = (small(5, E) for _ in range(9))
        G1, G2, C1, SC, BGR, CNB = (small(5, 4) for _ in range(6))
        S5 = small(12, 5)
        NV, ST, B2, CT = (small(E) for _ in range(4))
        TR = small(E, E)
        IT = small(OVER, E)
        IV = small(2, 32)
        OH = [small(5 * P // 2).bitcast(BF16).rearrange("p (i c) -> p i c", i=5) for _ in range(2)]
        TI = [small(5 * E).bitcast(BF16).rearrange("p (i h e) -> p i h e", i=5, h=2) for _ in range(2)]
        CH = small(3 * E).bitcast(BF16).rearrange("p (i e) -> p i e", e=E)
        BEF, ONE = (small(P // 2).bitcast(BF16) for _ in range(2))
        smalli = ctx.enter_context(nc.sbuf_tensor("smalli", [P, 10 + BLOCKS + 1 + OVER], I32))
        slot_i = smalli[:, 0:10].rearrange("p (a b) -> p a b", b=2)
        idx_i = smalli[:, 10:10 + BLOCKS]
        flag_i = smalli[:, 10 + BLOCKS:11 + BLOCKS]
        eid_i = smalli[:, 11 + BLOCKS:11 + BLOCKS + OVER]
        x1d = nc.dram_tensor("x1_rows", [NT, D], F32).ap()
        ysd = nc.dram_tensor("expert_rows", [SLOTS, D], F32).ap()
        idxd = nc.dram_tensor("slot_token", [SLOTS, 1], I32).ap()

        def trows(i):
            return P if i < 4 else NS
        att_st = ctx.enter_context(nc.sbuf_tensor("att_st", [P, 2, 8, 4], F32))
        gn_eps = ctx.enter_context(nc.sbuf_tensor("gn_eps", [P, 1], F32))[:, :]
        PL = ctx.enter_context(nc.sbuf_tensor("PL", [P, 4, 16], F32))

        ps = ctx.enter_context(nc.psum_tensor("ps", [P, 8, 512], F32))

        block = ctx.enter_context(nc.Block())

        ATT0, RW0 = 2, 8

        def mix_index(ct):
            return ct if ct < 2 else ct - 6

        def mix_dst(m):
            if m == 0:
                return WA
            if m == 1:
                return GL
            return (R4, K4, V4)[(m - 2) % 3][:, (m - 2) // 3, :]

        souts = [BG[0][:, 0:512], BG[0][:, 512:1024], BG[1][:, 0:512], BG[1][:, 512:1024],
                 KG[0][:, 0:512], KG[0][:, 512:1024], KG[1][:, 0:512], KG[1][:, 512:1024]]

        def rows(q):
            return P if q < 4 else NS

        def levels(q):
            return 5 if q < 4 else 2

        def unit(T4, q, u, r=slice(0, P)):
            return T4[r, q, u * P:(u + 1) * P] if q < 4 else T4[r, u, NP_:NT]

        def units(T4, q):
            return T4[:, q, 0:NP_].rearrange("p (u t) -> p u t", u=4) if q < 4 else T4[:, :, NP_:NT]

        def hsum_bank(j):
            return 2 if j < 3 else 6

        def par_rows(p):
            return slice(64 * p, 64 * p + 64)

        class Tally:

            def __init__(self, eng):
                self.eng, self.n = eng, {}

            def up(self, ins, name):
                ins.then_inc(sem(name), 1)
                self.n[name] = self.n.get(name, 0) + 1

            def link(self, ins, name):
                self.up(ins, name)
                self.eng.wait_ge(sem(name), self.n[name])

        def wait_read(eng, p):
            if p < 0:
                return
            if ATT0 <= p < RW0:
                eng.wait_ge(sem("att_evac"), p - ATT0 + 1)
            else:
                eng.wait_ge(sem("mixed"), mix_index(p) + 1)

        @block.sync
        def _(sp):
            sp.dma_start(ident, i_["consts"][:, 0:P]).then_inc(sem("ld_first"), 16)
            sp.dma_start(par, i_["params"][:, :]).then_inc(sem("ld_first"), 16)

            def load_win(ct):
                if ct >= RING:
                    sp.wait_ge(sem("proj"), ct - RING + 1)
                sp.dma_start(ring[:, ct % RING, :, :], i_["win"][ct].rearrange("p (k c) -> p k c", c=P)) \
                  .then_inc(sem(f"win{ct % RING}"), 16)

            load_win(0)
            load_win(1)
            sp.wait_ge(sem("xt_ps"), 4)
            load_win(2)
            load_win(3)
            sp.wait_ge(sem("xt_ps"), 8)
            sp.dma_start(wr, i_["w_router"].rearrange("(k p) e -> p k e", p=P)).then_inc(sem("ld_lora"), 16)
            sp.dma_start(LW[0:64, :], i_["decay_w2"][0]).then_inc(sem("ld_lora"), 16)
            sp.dma_start(LW[64:128, :], i_["aaa_a2"][0]).then_inc(sem("ld_lora"), 16)
            sp.dma_start(GW, i_["gate_g2"][0]).then_inc(sem("ld_lora"), 16)
            load_win(4)
            load_win(5)
            sp.dma_start(v2(o_const + P, NCONST - P), i_["consts"][:, P:NCONST]).then_inc(sem("ld_const"), 16)
            sp.dma_start(kc, i_["cache_k"][0].rearrange("b w h d -> w b (h d)")).then_inc(sem("ld_bulk"), 16)
            sp.dma_start(vc, i_["cache_v"][0].rearrange("b w h d -> w b (h d)")).then_inc(sem("ld_bulk"), 16)
            for ct in range(RING, 2 * RING + 2):
                load_win(ct)
            sp.wait_ge(sem("kv_tok"), 2)
            sp.dma_start(o_["k_prompt"].rearrange("l b w h d -> (l b w) (h d)"), Kt3).then_inc(sem("kv_out"), 16)
            sp.dma_start(o_["v_prompt"].rearrange("l b w h d -> (l b w) (h d)"), Vt[:, 4, :]).then_inc(sem("kv_out"), 16)
            sp.dma_start(o_["k_sample"].rearrange("l b w h d -> (l b w) (h d)"), Ks[0:NS, :]).then_inc(sem("kv_out"), 16)
            sp.dma_start(o_["v_sample"].rearrange("l b w h d -> (l b w) (h d)"), Vs[0:NS, :]).then_inc(sem("kv_out"), 16)
            for ct in range(2 * RING + 2, COLT):
                load_win(ct)
            sp.wait_ge(sem("proj"), COLT)
            sp.dma_start(wo.rearrange("p k c -> p (k c)"), i_["wo"][:, :]).then_inc(sem("ld_bulk"), 16)
            sp.dma_start(o_["shift_prompt"][0], i_["x_prompt"][0, NP_ - 1:NP_, :]).then_inc(sem("out"), 16)
            sp.dma_start(o_["shift_sample"][0], i_["x_sample"][:, TS - 1, :]).then_inc(sem("out"), 16)
            for h in range(4):
                if h == 2:
                    sp.wait_ge(sem("mixed"), 14)
                if h == 3:
                    sp.wait_ge(sem("prep"), 5)
                sp.dma_start(stage[h][0:HD, :].rearrange("v (b h k) -> v b h k", b=2, k=HD),
                             i_["state_wkv"][0, 2 * h:2 * h + 2].rearrange("b h v k -> v b h k")) \
                  .then_inc(sem("ld_st"), 16)
            sp.wait_ge(sem("so_ev"), 8)
            for b in range(NB):
                sp.dma_start(o_["wkv_sample"][0, b].rearrange("h v k -> v h k"),
                             souts[b][0:HD, :].rearrange("v (h k) -> v h k", k=HD)).then_inc(sem("st_out"), 16)
            sp.wait_ge(sem("so_ev"), NB + 1)
            sp.dma_start(o_["wkv_prompt"][0, 0].rearrange("h v k -> v h k"),
                         GH[1][0:HD, :].rearrange("v (h k) -> v h k", k=HD)).then_inc(sem("st_out"), 16)

            def load_residual(i):
                sp.dma_start(xres[0:P, i, :], i_["x_prompt"][0, i * P:(i + 1) * P, :]).then_inc(sem(f"ld_rows{i}"), 16)

            sp.wait_ge(sem("so_ps"), NB + 1)
            for r_ in range(2):
                sp.dma_start(ln1[:, r_, :], i_[("ln1_g", "ln1_b")[r_]][0:1, :].to_broadcast([P, D])) \
                  .then_inc(sem("ld_norm"), 16)
            load_residual(0)
            sp.wait_ge(sem("st_out"), 16 * (NB + 1))
            sp.wait_ge(sem("gn_out"), 4)
            load_residual(1)

            def load_expert(e, s, ahead=True):
                for nm, W, src in (("gate", WG, i_["w_gate"]), ("up", WU, i_["w_up"]), ("down", WD, i_["w_down"])):
                    if ahead:
                        sp.wait_ge(sem(nm + "_ps"), e - 1)
                    w = src[0, bass.ds(e, 1)] if ahead else src[0, e:e + 1]
                    sp.dma_start(W[s], w.rearrange("a (k p) n -> p (a k) n", p=P)).then_inc(sem(f"w{nm}{s}"), 16)

            load_expert(0, 0, False)
            for i in range(5):
                if i == 1:
                    load_expert(1, 1, False)
                r = trows(i)
                sp.wait_ge(sem("x1_ready"), i + 1)
                sp.dma_start(x1d[i * P:i * P + r, :], x1[0:r, i, :]).then_inc(sem("x1_st"), 16)
                if i + 2 < 5:
                    n = i + 2
                    src = i_["x_prompt"][0, n * P:(n + 1) * P, :] if n < 4 else i_["x_sample"].rearrange("b t d -> (b t) d")
                    sp.dma_start(xres[0:trows(n), n % 2, :], src).then_inc(sem(f"ld_rows{n % 2}"), 16)
            sp.wait_ge(sem("logit_ps"), 5)
            for r_ in range(2):
                sp.dma_start(ln2[:, r_, :], i_[("ln2_g", "ln2_b")[r_]][0:1, :].to_broadcast([P, D])) \
                  .then_inc(sem("ld_norm"), 16)
            with sp.Fori(1, E // 2) as it:
                for s in range(2):
                    load_expert(2 * it + s, s)

            sp.wait_ge(sem("slots"), 2)
            more = sp.value_load(flag_i[0:1, :], min_val=0, max_val=OVER)
            with sp.If(more > 0):
                sp.wait_ge(sem("down_ps"), E)
                sp.wait_ge(sem("up_ps"), E)

                def load_more(o):
                    e = sp.value_load(eid_i[0:1, bass.ds(o, 1)], min_val=0, max_val=E - 1)
                    for W, src in ((WG, i_["w_gate"]), (WU, i_["w_up"]), (WD, i_["w_down"])):
                        sp.dma_start(W[0], src[0, bass.ds(e, 1)].rearrange("a (k p) n -> p (a k) n", p=P)) \
                          .then_inc(sem("o_w"), 16)

                load_more(0)
                with sp.Fori(1, OVER) as it:
                    sp.wait_ge(sem("over_pe"), 4 * it)
                    load_more(it)
            for i in range(5):
                if i < 3:
                    sp.wait_ge(sem("y_done"), i + 1)
                else:
                    sp.wait_ge(sem("y_last"), i - 2)
                r = trows(i)
                dst = o_["y_prompt"][0, i * P:(i + 1) * P, :] if i < 4 else o_["y_sample"].rearrange("b t d -> (b t) d")
                sp.dma_start(dst, x1[0:r, i, :]).then_inc(sem("out"), 16)
            sp.wait_ge(sem("out"), 16 * 7)

        @block.gpsimd
        def _(pool):
            zrow = v2(o_mixa, D)
            T = Tally(pool)
            T.link(pool.memset(zrow, 0.0), "pool_step")
            pool.wait_ge(sem("proj"), 3)
            for n in range(OVER * CAP // P):
                pool.dma_start(ysd[E * CAP + n * P:E * CAP + (n + 1) * P, :], zrow).then_inc(sem("rows_zero"), 16)
            for n in range(8):
                y = YT[n]
                pool.wait_ge(sem("yt_ev"), n + 1)
                by_batch = y.rearrange("t (b v) -> t b v", b=NB)
                own = C("batch")[NS:2 * NS].unsqueeze(2).to_broadcast([NS, NB, HD])
                T.link(pool.tensor_tensor(by_batch, by_batch, own, ALU.mult), "pool_step")
                for w in (256, 128, 64):
                    T.link(pool.tensor_tensor(y[:, 0:w], y[:, 0:w], y[:, w:2 * w], ALU.add),
                           "pool_step" if w > 64 else "yt_sum")
            for j in range(4):
                y = V4[:, j, :]
                pool.wait_ge(sem("gn_y"), j + 1)
                T.link(pool.tensor_tensor(y, y, SG4[:, j, :], ALU.add), "pool_step")
                pool.tensor_tensor(mixR[:, j, :], y, G4[:, j, :], ALU.mult).then_inc(sem("gn_out"), 1)
            pool.wait_ge(sem("slots"), 1)
            pool.wait_ge(sem("x1_st"), 80)
            pool.wait_ge(sem("logit_ps"), 5)

            def gather(e):
                if e >= 2:
                    pool.wait_ge(sem("xg_turn"), e - 1)
                pool.indirect_dma_start(out=xg[0:CAP, e % 2, :], out_offset=None, in_=x1d[:, :],
                                        in_offset=bass.IndirectOffsetOnAxis(ap=idx_i[0:CAP, e:e + 1], axis=0)) \
                    .then_inc(sem(f"xg{e % 2}"), 16)

            for e in range(E):
                gather(e)
            pool.wait_ge(sem("slots"), 2)
            more = pool.value_load(flag_i[0:1, :], min_val=0, max_val=OVER)
            with pool.If(more > 0):
                pool.dma_start(tokid[:, :], i_["tokid"][:, :]).then_inc(sem("o_idx"), 16)
                pool.memset(zidx[:, :], 0).then_inc(sem("o_zero"), 1)
                pool.wait_ge(sem("o_zero"), 1)
                pool.dma_start(idxd.rearrange("(p e) o -> p (e o)", e=BLOCKS * CAP // P), zidx[:, 0:BLOCKS * CAP // P]) \
                    .then_inc(sem("o_idx"), 16)
                pool.wait_ge(sem("o_idx"), 32)
                for i in range(5):
                    r = trows(i)
                    for n in range(2):
                        pool.indirect_dma_start(out=idxd[:, :], in_=tokid[0:r, i:i + 1], in_offset=None,
                                                out_offset=bass.IndirectOffsetOnAxis(ap=slot_i[0:r, i, n:n + 1], axis=0)) \
                            .then_inc(sem("o_idx"), 16)
                pool.wait_ge(sem("o_idx"), 192)
                pool.dma_start(idx_i[0:CAP, E:BLOCKS], idxd[E * CAP:SLOTS, :].rearrange("(e p) o -> p (e o)", p=CAP),
                               allow_slow_non_contiguous=True).then_inc(sem("o_idx"), 16)
                pool.wait_ge(sem("o_idx"), 208)
                pool.wait_ge(sem("xg_turn"), E)
                for o in range(OVER):
                    if o:
                        pool.wait_ge(sem("over_pe"), 4 * o - 3)
                    pool.indirect_dma_start(out=xg[0:CAP, 0, :], out_offset=None, in_=x1d[:, :],
                                            in_offset=bass.IndirectOffsetOnAxis(ap=idx_i[0:CAP, E + o:E + o + 1], axis=0)) \
                        .then_inc(sem("o_xg"), 16)
                pool.wait_ge(sem("o_yst"), 16 * OVER)
            pool.wait_ge(sem("y_st0"), 16 * E // 2)
            pool.wait_ge(sem("y_st1"), 16 * E // 2)
            pool.wait_ge(sem("down_ps"), E)
            for i in range(5):
                r = trows(i)
                for n in range(2):
                    pool.indirect_dma_start(out=yab[0:r, i, n, :], out_offset=None, in_=ysd[:, :],
                                            in_offset=bass.IndirectOffsetOnAxis(ap=slot_i[0:r, i, n:n + 1], axis=0)) \
                        .then_inc(sem(f"yab{min(i, 2)}"), 16)
            pool.wait_ge(sem("ld_norm"), 64)
            for i in range(3):
                x, r = x1[0:trows(i), i, :], trows(i)
                pool.wait_ge(sem("ln2_nrm"), i + 1)
                T.link(pool.tensor_tensor(x, x, ln2[0:r, 0, :], ALU.mult), "pool_step")
                pool.tensor_tensor(x, x, ln2[0:r, 1, :], ALU.add).then_inc(sem("y_done"), 1)

        @block.tensor
        def _(pe):
            mm = pe.matmul

            def transpose_x():
                for n in range(10):
                    i, h = n // 2, n % 2
                    rows = P if i < 4 else 72
                    if h == 0:
                        pe.wait_ge(sem(f"ld_rows{i % 4}"), 16 * (i // 4 + 1))
                    if n == 0:
                        pe.wait_ge(sem("ld_first"), 32)
                    if n >= 2:
                        pe.wait_ge(sem(("xt_act", "xt_dve")[n % 2]), n // 2)
                    for k in range(4):
                        c = (4 * h + k) * P
                        ins = pe.transpose(ps[:, 5 + n % 2, k * P:k * P + rows], xst[i % 4][0:rows, c:c + P],
                                           ident[0:rows, 0:rows])
                    ins.then_inc(sem("xt_ps"), 1)
                pe.wait_ge(sem("xt_act"), 5)
                pe.wait_ge(sem("xt_dve"), 5)

            def project(ct):
                pe.wait_ge(sem(f"win{ct % RING}"), 16 * (ct // RING + 1))
                wait_read(pe, ct - 2)
                for k in range(KT):
                    mm(ps[:, ct % 2, :], ring[:, ct % RING, k, :], xT[:, k, 0:NP_], start=k == 0, stop=k == KT - 1)
                wait_read(pe, ct - 1)
                if ct == 12 or ct == 15 or ct == 18:
                    pe.wait_ge(sem("norm_read"), (ct - 9) // 3)
                if ct == 13 or ct == 16 or ct == 19:
                    pe.wait_ge(sem("bonus_read"), (ct - 10) // 3)
                for k in range(KT):
                    ins = mm(ps[:, 2, 0:72], ring[:, ct % RING, k, :], xT[:, k, NP_:584],
                             start=k == 0, stop=k == KT - 1)
                ins.then_inc(sem("proj"), 1)

            def lora(n):
                kind, j = n // 4, n % 4
                if n == 0:
                    pe.wait_ge(sem("ld_lora"), 64)
                    pe.wait_ge(sem("lora_in"), 1)
                if n == 8:
                    pe.wait_ge(sem("lora_in"), 2)
                if n >= 2:
                    pe.wait_ge(sem("lora_evac"), n - 1)
                r = (slice(0, 64), slice(64, 128), slice(0, 128))[kind]
                w = (LW, LW, GW)[kind][r, j * P:(j + 1) * P]
                src = (WA, WA, GL)[kind][r, :]
                b = 3 + 2 * (n % 2)
                mm(ps[:, b, :], w, src[:, 0:NP_], start=True, stop=True)
                mm(ps[:, b + 1, 0:NS], w, src[:, NP_:NT], start=True, stop=True).then_inc(sem("lora_ps"), 1)

            def kv_turn():
                pe.wait_ge(sem("att_evac"), 6)
                pe.wait_ge(sem("lora_evac"), 12)
                for t in range(4):
                    ins = pe.transpose(ps[:, 5, t * P:(t + 1) * P], vT[:, t * P:(t + 1) * P], ident)
                ins.then_inc(sem("kv_ps"), 1)
                pe.transpose(ps[0:NS, 6, 0:P], vT[:, NP_:NT], ident)
                pe.transpose(ps[:, 6, P:2 * P], kT[:, 4 * P:5 * P], ident)
                pe.transpose(ps[0:NS, 6, 2 * P:3 * P], kTs, ident).then_inc(sem("kv_ps"), 1)
                pe.wait_ge(sem("ld_bulk"), 32)
                for h in range(2):
                    pe.wait_ge(sem("kv_tok"), h + 1)
                    for b in range(4):
                        ins = pe.transpose(ps[:, 5 + h, b * P:(b + 1) * P], kc[:, 4 * h + b, :], ident)
                    ins.then_inc(sem("kv_ps"), 1)

            def scores(n):
                if n >= 1:
                    pe.wait_ge(sem("s_read"), n)
                if n < 8:
                    nb, kv = n // 2, n % 2
                    r = slice(kv * 64, kv * 64 + 64)
                    for g in range(4):
                        ins = mm(ps[:, 3 + g // 2, (g % 2) * 256:(g % 2) * 256 + 256],
                                 qT[r, g, nb * P:(nb + 1) * P], kT[r, nb * P:(nb + 2) * P], start=True, stop=True)
                else:
                    pe.wait_ge(sem("kv_tok"), 4)
                    for kv in range(2):
                        r = slice(kv * 64, kv * 64 + 64)
                        for b in range(NB):
                            q = qTs[r, b].rearrange("p g t -> p (g t)")
                            o = slice(32 * (b % 4), 32 * (b % 4) + 32)
                            c = (b // 4) * 192
                            tp = (kv * 64, 32 * (b % 4))
                            mm(ps[o, 3 + kv, c:c + P], q, kcT[r, b, :], start=True, stop=True)
                            ins = mm(ps[o, 3 + kv, c + P:c + 192], q, kTs[r, :], start=True, stop=True)
                ins.then_inc(sem("s_ps"), 1)

            def p_turn(n):
                pe.wait_ge(sem("p_ready"), n + 1)
                if n == 0:
                    pe.wait_ge(sem("kv_tok"), 4)
                if n >= 1:
                    pe.wait_ge(sem("pv_evac"), n)
                w = 256 if n < 8 else 192
                Sn = Sb[:, n % 2, 0:4 * w].rearrange("p (g w) -> p g w", g=4)
                for kb in range(2):
                    kw = min(P, w - kb * P)
                    for g in range(4):
                        ins = pe.transpose(ps[0:kw, 5 + kb, g * P:(g + 1) * P], Sn[:, g, kb * P:kb * P + kw], ident)
                    ins.then_inc(sem("pt_ps"), 1)

            def pv(n):
                pe.wait_ge(sem("pt_act"), n + 1)
                pe.wait_ge(sem("pt_dve"), n + 1)
                if n < 8:
                    nb, kv = n // 2, n % 2
                    r = slice(kv * 64, kv * 64 + 64)
                    mm(ps[r, 5, :], Vt[:, nb, r], PT[:, 0, :], start=True, stop=False)
                    ins = mm(ps[r, 5, :], Vt[:, nb + 1, r], PT[:, 1, :], start=False, stop=True)
                else:
                    for kv in range(2):
                        r = slice(kv * 64, kv * 64 + 64)
                        for b in range(NB):
                            c = (kv * 2 + b // 4) * P + 32 * (b % 4)
                            mm(ps[r, 5, b * 32:b * 32 + 32], vc[:, b, r], PT[:, 0, c:c + 32], start=True, stop=False)
                            ins = mm(ps[r, 5, b * 32:b * 32 + 32], Vs[0:NS, r], PT[0:NS, 1, c:c + 32],
                                     start=False, stop=True)
                ins.then_inc(sem("pv_ps"), 1)

            def head_sum(n):
                if n == 0:
                    pe.wait_ge(sem("lora_evac"), 12)
                    pe.wait_ge(sem("ld_const"), 16)
                else:
                    pe.wait_ge(sem(("bonus_read", "norm_read")[n % 2]), (n + 1) // 2)
                pe.wait_ge(sem(("hsum_in_a", "hsum_in_b")[n % 2]), n // 2 + 1)
                if n < 6:
                    pe.wait_ge(sem("mixed"), 6 + n // 2 * 3 + n % 2)
                s = SQ[:, n % 2, :]
                mm(ps[:, 7, :], C("blk"), s[:, 0:NP_], start=True, stop=True)
                mm(ps[:, hsum_bank(n // 2), 0:NS], C("blk"), s[:, NP_:NT], start=True, stop=True) \
                    .then_inc(sem("hsum_ps"), 1)

            transpose_x()
            for ct in range(COLT):
                if 2 <= ct < 8:
                    lora(2 * (ct - 2))
                project(ct)
                if 2 <= ct < 8:
                    lora(2 * (ct - 2) + 1)
                if ct == 7:
                    kv_turn()
                if ct >= RW0:
                    k = ct - RW0
                    if 3 <= k < 12:
                        pv(k - 3)
                    if k < 9:
                        scores(k)
                    if 2 <= k < 11:
                        p_turn(k - 2)
                    if k >= 3:
                        j, ph = k // 3 - 1, k % 3
                        if ph == 0:
                            head_sum(2 * j)
                        if ph == 1:
                            head_sum(2 * j + 1)

            def state_in(h):
                if h == 0:
                    pe.wait_ge(sem("ld_st"), 64)
                    pe.wait_ge(sem("post_dve"), 20)
                for n in range(8):
                    ins = pe.transpose(ps[:, 4 + h, n * HD:(n + 1) * HD], stage[h][0:HD, n * P:(n + 1) * P],
                                       ident[0:HD, 0:HD])
                ins.then_inc(sem("st_ps"), 1)

            def wy(q):
                R, L = rows(q), levels(q)
                pe.wait_ge(sem("prep"), min(q + 1, 4))
                if q == 0:
                    pe.wait_ge(sem("mixed"), 14)
                    pe.wait_ge(sem("pv_evac"), 9)
                    pe.wait_ge(sem("bonus_read"), 3)
                for n, T4 in enumerate((A4, B4, K4, V4)):
                    if q and n == 2:
                        pe.wait_ge(sem("post_dve"), 5 * q - 4)
                    if q and n == 3:
                        pe.wait_ge(sem("post_act"), q)
                    for u in range(4):
                        ins = pe.transpose(ps[0:R, n, u * P:(u + 1) * P], unit(T4, q, u), ident)
                    ins.then_inc(sem("tok_ps"), 1)
                if q:
                    pe.wait_ge(sem("post_dve"), 5 * q)
                if q == 4:
                    pe.wait_ge(sem("st_ev"), 4)
                for p in range(2):
                    for u in range(4):
                        ins = mm(ps[0:R, 4 + p, u * R:(u + 1) * R], unit(A4, q, u, par_rows(p)),
                                 unit(B4, q, u, par_rows(p)), start=True, stop=True)
                    ins.then_inc(sem("n_ps"), 1)

                if q == 1:
                    head_sum(6)
                    head_sum(7)

                def gram(T4, p, name):
                    for u in range(4):
                        t0 = q * NT + u * P if q < 4 else u * NT + NP_
                        both = rwkv7[par_rows(p), 0:4:3, t0:t0 + R]
                        c = (u % 2) * 2 * R
                        ins = mm(ps[0:R, 2 * p + u // 2, c:c + 2 * R].rearrange("p (a b) -> p a b", a=2),
                                 unit(T4, q, u, par_rows(p)), both, start=True, stop=True)
                    ins.then_inc(sem(name), 1)

                for p in range(2):
                    pe.wait_ge(sem(("tok_act", "tok_dve")[p]), 2 * q + 2)
                    gram(B4, p, "bg_ps")

                def turn_x(l, p, bank):
                    pe.wait_ge(sem("x_ready"), 10 * q + 2 * l + p + 1)
                    for u in range(4):
                        ins = pe.transpose(ps[0:R, bank, u * R:(u + 1) * R], X[p][0:R, u * R:(u + 1) * R],
                                           ident[0:R, 0:R])
                    ins.then_inc(sem("xt2_ps"), 1)

                if q == 1:
                    pe.wait_ge(sem("bonus_read"), 4)
                for p in range(2):
                    turn_x(0, p, 6 + p)
                for p in range(2):
                    pe.wait_ge(sem("bg_ev"), 2 * q + p + 1)
                    gram(K4, p, "kg_ps")
                for l in range(1, L + 1):
                    for p in range(2):
                        if l > 1:
                            pe.wait_ge(sem("x_ready"), 10 * q + 2 * (l - 1) + p + 1)
                        for u in range(4):
                            nt = BG[p][0:R, u * 2 * R + R:(u + 1) * 2 * R]
                            ins = mm(ps[0:R, 4 + p, u * R:(u + 1) * R], nt, X[p][0:R, u * R:(u + 1) * R],
                                     start=True, stop=True)
                        ins.then_inc(sem("w1_ps"), 1)
                        if l > 1:
                            turn_x(l - 1, p, 2 + p)
                    if l == 1:
                        for p in range(2):
                            pe.wait_ge(sem("kg_ev"), 2 * q + 2)
                            for u in range(4):
                                ak = KG[p][0:R, u * 2 * R + R:(u + 1) * 2 * R]
                                ins = mm(ps[0:R, p, u * HD:(u + 1) * HD], ak, TOK[3][0:R, u, par_rows(p)],
                                         start=True, stop=True)
                            ins.then_inc(sem("akv_ps"), 1)
                    for p in range(2):
                        pe.wait_ge(sem("w1_ev"), 10 * q + 2 * (l - 1) + p + 1)
                        pe.wait_ge(sem("xt2_ev"), 10 * q + 2 * (l - 1) + p + 1)
                        for u in range(4):
                            c = slice(u * R, (u + 1) * R)
                            if l < L:
                                ins = mm(ps[0:R, 6 + p, c], XT[p][0:R, c], W1[p][0:R, c], start=True, stop=True)
                            else:
                                ins = mm(ps[0:R, 6 + p, c], W1[p][0:R, c], XT[p][0:R, c], start=True, stop=True)
                        ins.then_inc(sem("xl_ps"), 1)
                for p in range(2):
                    pe.wait_ge(sem("t_ready"), 2 * q + p + 1)
                    pe.wait_ge(sem("rhs_ev"), 2 * q + p + 1)
                    for u in range(4):
                        ins = mm(ps[0:R, p, u * P:(u + 1) * P], XT[p][0:R, u * R:(u + 1) * R],
                                 RHS[p][0:R, u * P:(u + 1) * P], start=True, stop=True)
                    ins.then_inc(sem("gh_ps"), 1)
                pe.wait_ge(sem("gh_ev"), 2 * q + 2)
                for p in range(2):
                    for u in range(4):
                        ins = mm(ps[par_rows(p), 2, u * R:(u + 1) * R], GH[p][0:R, u * P:u * P + HD],
                                 BG[p][0:R, u * 2 * R:u * 2 * R + R], start=True, stop=True)
                ins.then_inc(sem("post_ps"), 1)
                for p in range(2):
                    for u in range(4):
                        o = ps[par_rows(p), 3, u * R:(u + 1) * R]
                        mm(o, GH[p][0:R, u * P + HD:(u + 1) * P], BG[p][0:R, u * 2 * R:u * 2 * R + R],
                           start=True, stop=False)
                        ins = mm(o, TOK[3][0:R, u, par_rows(p)], KG[p][0:R, u * 2 * R:u * 2 * R + R],
                                 start=False, stop=True)
                ins.then_inc(sem("post_ps"), 1)
                if q < 4:
                    for cp in range(2):
                        r = slice(64 * cp, 64 * cp + 64)
                        for p in range(2):
                            for u in range(4):
                                ins = mm(ps[par_rows(p), 6 + cp, u * HD:(u + 1) * HD], GH[p][r, u * P:u * P + HD],
                                         TOK[1][r, u, par_rows(p)], start=True, stop=True)
                    ins.then_inc(sem("post_ps"), 1) if cp else None
                    for cp in range(2):
                        r = slice(64 * cp, 64 * cp + 64)
                        for p in range(2):
                            for u in range(4):
                                o = ps[par_rows(p), 4 + cp, u * HD:(u + 1) * HD]
                                mm(o, TOK[1][r, u, par_rows(p)], GH[p][r, u * P + HD:(u + 1) * P],
                                   start=True, stop=False)
                                ins = mm(o, TOK[2][r, u, par_rows(p)], TOK[3][r, u, par_rows(p)],
                                         start=False, stop=True)
                    ins.then_inc(sem("post_ps"), 1)

            def sample_states():
                for p in range(2):
                    for u in range(4):
                        ins = mm(ps[par_rows(p), 6, u * HD:(u + 1) * HD], TOK[0][0:NS, u, par_rows(p)],
                                 XT[p][0:NS, u * NS:(u + 1) * NS], start=True, stop=True)
                ins.then_inc(sem("gt_ps"), 1)
                pe.wait_ge(sem("gt_ev"), 1)
                for n in range(8):
                    u, p = n // 2, n % 2
                    if n >= 2:
                        pe.wait_ge(sem("um_ev"), n - 1)
                        pe.wait_ge(sem("yt_ev"), n - 1)
                    mm(ps[:, 4 + p, :], GQ[par_rows(p), u, :],
                       Z0[par_rows(p), u].rearrange("p b v -> p (b v)"), start=True, stop=True).then_inc(sem("u_ps"), 1)
                    if n >= 1:
                        chain(n)
                        z1(n - 1)
                z1(7)

            def sample_y():
                for n in range(8):
                    u, p = n // 2, n % 2
                    pe.wait_ge(sem("yt_sum"), n + 1)
                    ins = mm(ps[par_rows(p), 0, u * NS:(u + 1) * NS], YT[n][:, 0:HD], C("ident2")[NS:2 * NS, :],
                             start=True, stop=True)
                ins.then_inc(sem("ys_ps"), 1)

            def z1(n):
                u, p = n // 2, n % 2
                pe.wait_ge(sem("um_ev"), n + 1)
                if u >= 2 and p == 0:
                    pe.wait_ge(sem("z1_ev"), u - 1)
                o = ps[par_rows(p), 6 + u % 2, :]
                mm(o, TOK[1][0:NS, u, par_rows(p)], W1[p][0:NS, :], start=True, stop=False)
                mm(o, TOK[2][0:NS, u, par_rows(p)], NM[p][0:NS, :], start=False, stop=True).then_inc(sem("z1_ps"), 1)

            def sample_out(b):
                if b == 0:
                    pe.wait_ge(sem("z1_ev"), 4)
                if b >= 2:
                    pe.wait_ge(sem("so_ev"), b - 1)
                for j in range(4):
                    ins = pe.transpose(ps[0:HD, 6 + b % 2, j * P:(j + 1) * P], Z0[:, j, b, :], ident)
                ins.then_inc(sem("so_ps"), 1)

            def prompt_out():
                pe.wait_ge(sem("so_ev"), 8)
                for j in range(4):
                    ins = pe.transpose(ps[0:HD, 7, j * P:(j + 1) * P], Zp[:, 7, j, :], ident)
                ins.then_inc(sem("so_ps"), 1)

            def zin(c, j, p):
                return B4[par_rows(p), j, 0:HD] if c == 1 else Zp[par_rows(p), c - 1, j, :]

            def chain(c):
                if c > 1:
                    pe.wait_ge(sem("z_ready"), c - 1)
                for p in range(2):
                    for j in range(4):
                        ins = mm(ps[par_rows(p), 1, j * HD:(j + 1) * HD], A4[par_rows(p), j, c * HD:(c + 1) * HD],
                                 zin(c, j, p), start=True, stop=True)
                ins.then_inc(sem("z_ps"), 1)

            def y_of(j):
                if j == 0:
                    pe.wait_ge(sem("um_ev"), 8)
                    pe.wait_ge(sem("yt_ev"), 8)
                if j == 3:
                    pe.wait_ge(sem("post_act"), 5)
                for c in range(1, CHUNKS):
                    if j == 0:
                        pe.wait_ge(sem("z_ready"), max(1, c - 1))
                    for p in range(2):
                        ins = mm(ps[par_rows(p), (4, 5, 2, 3)[j], c * HD:(c + 1) * HD], zin(c, j, p),
                                 R4[par_rows(p), j, c * HD:(c + 1) * HD], start=True, stop=True)
                ins.then_inc(sem("y_ps"), 1)

            def head_sum_of(src, bank, name):
                mm(ps[:, bank, :], C("blk"), src[:, 0:NP_], start=True, stop=True)
                mm(ps[:, bank + 1, 0:NS], C("blk"), src[:, NP_:NT], start=True, stop=True).then_inc(sem(name), 1)

            def head_mean(j):
                if j == 0:
                    pe.wait_ge(sem("ys_ev"), 1)
                    pe.wait_ge(sem("z_ready"), 7)
                    pe.wait_ge(sem("y_ev"), 1)
                else:
                    pe.wait_ge(sem("centred"), j)
                    pe.wait_ge(sem("y_ev"), j + 1)
                head_sum_of(V4[:, j, :], 0, "hm_ps")

            def head_square(j):
                pe.wait_ge(sem("gsq"), j + 1)
                if j == 0:
                    pe.wait_ge(sem("y_ev"), 4)
                else:
                    pe.wait_ge(sem("var_read"), j)
                head_sum_of(SQ[:, 0, :], 2, "hs_ps")

            def out_proj(i, hs, ks):
                r = trows(i)
                if i == 0 and 0 in ks:
                    pe.wait_ge(sem("ld_bulk"), 48)
                    pe.wait_ge(sem("y_ev"), 2)
                if i == 1 and 0 in ks:
                    pe.wait_ge(sem("so_ev"), NB + 1)
                if i >= 2:
                    pe.wait_ge(sem("pre_ln"), i - 1)
                for h in hs:
                    for k in ks:
                        if i == 0 and k >= 4:
                            pe.wait_ge(sem("gn_out"), k - 3)
                        m = (mixA[:, k, :] if k < 4 else mixR[:, k - 4, :])[:, i * P:i * P + r]
                        ins = mm(ps[0:r, 4 + 2 * (i % 2) + h, :], m, wo[:, k, h * 512:(h + 1) * 512],
                                 start=k == 0, stop=k == KT - 1)
                if KT - 1 in ks:
                    ins.then_inc(sem("op_ps"), 1)

            for q in range(4):
                wy(q)
            for h in range(4):
                state_in(h)
            wy(4)
            sample_states()
            for j in range(4):
                y_of(j)
            sample_y()
            sample_out(0)
            sample_out(1)
            head_mean(0)
            sample_out(2)
            sample_out(3)
            head_mean(1)
            head_square(0)
            sample_out(4)
            sample_out(5)
            head_mean(2)
            head_square(1)
            sample_out(6)
            sample_out(7)
            prompt_out()
            out_proj(0, (0, ), range(4))
            head_mean(3)
            head_square(2)
            out_proj(0, (1, ), range(4))
            head_square(3)
            out_proj(1, range(2), range(4))

            def turn_x1(i):
                r = trows(i)
                pe.wait_ge(sem("x1_ready"), i + 1)
                if i == 0:
                    pe.wait_ge(sem("y_ev"), 4)
                for h in range(2):
                    if i:
                        pe.wait_ge(sem(("x1t_act", "x1t_dve")[h]), i)
                    for k in range(4):
                        c = (4 * h + k) * P
                        ins = pe.transpose(ps[:, 2 + h, k * P:k * P + r], x1[0:r, i, c:c + P], ident[0:r, 0:r])
                    ins.then_inc(sem("x1t_ps"), 1)

            def logits(i):
                r = trows(i)
                pe.wait_ge(sem("x1t_act"), i + 1)
                pe.wait_ge(sem("x1t_dve"), i + 1)
                if i:
                    pe.wait_ge(sem("lg_ev"), i)
                for k in range(KT):
                    ins = mm(ps[0:r, 0, 0:E], x1T[:, k, 0:r], wr[:, k, :], start=k == 0, stop=k == KT - 1)
                ins.then_inc(sem("logit_ps"), 1)

            out_proj(0, range(2), range(4, 7))
            out_proj(1, range(2), range(4, 7))
            out_proj(0, range(2), range(7, 8))
            out_proj(1, range(2), range(7, 8))
            out_proj(2, range(2), range(KT))
            turn_x1(0)
            turn_x1(1)
            logits(0)
            for i in range(3, 5):
                out_proj(i, range(2), range(KT))
                turn_x1(i - 1)
                logits(i - 2)
            logits(3)
            turn_x1(4)
            logits(4)

            pe.wait_ge(sem("chosen"), 1)
            mm(ps[:, RANKB, 0:6 * E], BEF, CH.rearrange("p i e -> p (i e)"), start=True, stop=False)
            for k in range(5):
                ins = mm(ps[:, RANKB, (k + 1) * E:6 * E].rearrange("p (i e) -> p i e", e=E), ONE,
                         CH[:, k:k + 1, :].to_broadcast([P, 5 - k, E]), start=False, stop=k == 4)
            ins.then_inc(sem("route_ps"), 1)

            pe.wait_ge(sem("chosen"), 3)
            for n in range(20):
                k, i, h = n // 10, n // 2 % 5, n % 2
                ins = mm(ps[0:CAP, 2, 0:E], OH[k][:, i, 0:CAP], TI[k][:, i, h, :], start=n == 0, stop=n == 19)
            ins.then_inc(sem("route_ps"), 1)

            R_ = CAP

            def turn_xg(e, s, first=False):
                pe.wait_ge(sem(f"xg{s}"), e * 8 + (16 - 8 * s))
                if not first:
                    pe.wait_ge(sem("xgT_act"), e)
                    pe.wait_ge(sem("xgT_dve"), e)
                for k in range(KT):
                    ins = pe.transpose(ps[:, k // 4, (k % 4) * P:(k % 4) * P + R_], xg[0:R_, s, k * P:(k + 1) * P],
                                       ident[0:R_, 0:R_])
                ins.then_inc(sem("xg_turn"), 1)

            def gate_up(e, s, first=False):
                pe.wait_ge(sem("xgT_act"), e + 1)
                pe.wait_ge(sem("xgT_dve"), e + 1)
                for W, nm, b in ((WG, "gate", 2), (WU, "up", 3)):
                    pe.wait_ge(sem(f"w{nm}{s}"), e * 8 + (16 - 8 * s))
                    if not first:
                        pe.wait_ge(sem("h_ready"), e)
                    for k in range(KT):
                        ins = mm(ps[0:R_, b, :], xgT[s][:, k, 0:R_], W[s][:, k, :], start=k == 0, stop=k == KT - 1)
                    ins.then_inc(sem(nm + "_ps"), 1)

            def turn_h(e, s, first=False):
                pe.wait_ge(sem("h_ready"), e + 1)
                if not first:
                    pe.wait_ge(sem("ht_ready"), e)
                for k in range(FT):
                    ins = pe.transpose(ps[:, 4, k * P:k * P + R_], hh[0:R_, s, k * P:(k + 1) * P], ident[0:R_, 0:R_])
                ins.then_inc(sem("ht_ps"), 1)

            def down(e, s, first=False):
                pe.wait_ge(sem("ht_ready"), e + 1)
                pe.wait_ge(sem(f"wdown{s}"), e * 8 + (16 - 8 * s))
                if not first:
                    pe.wait_ge(sem("y_act"), e)
                    pe.wait_ge(sem("y_dve"), e)
                for h in range(2):
                    for k in range(FT):
                        ins = mm(ps[0:R_, 5 + h, :], hT[s][:, k, 0:R_], WD[s][:, k, h * 512:(h + 1) * 512],
                                 start=k == 0, stop=k == FT - 1)
                ins.then_inc(sem("down_ps"), 1)

            turn_xg(0, 0, True)
            gate_up(0, 0, True)
            turn_xg(1, 1)
            turn_h(0, 0, True)
            gate_up(1, 1)
            turn_xg(2, 0)
            down(0, 0, True)
            turn_h(1, 1)
            with pe.Fori(1, E // 2 - 1) as it:
                for s in range(2):
                    e = 2 * it + s
                    gate_up(e, s)
                    turn_xg(e + 1, 1 - s)
                    down(e - 1, 1 - s)
                    turn_h(e, s)
            gate_up(E - 2, 0)
            turn_xg(E - 1, 1)
            down(E - 3, 1)
            turn_h(E - 2, 0)
            gate_up(E - 1, 1)
            down(E - 2, 0)
            turn_h(E - 1, 1)
            down(E - 1, 1)

            pe.wait_ge(sem("slots"), 2)
            more = pe.value_load(flag_i[0:1, :], min_val=0, max_val=OVER)
            with pe.If(more > 0):
                pe.wait_ge(sem("y_act"), E)
                pe.wait_ge(sem("y_dve"), E)
                with pe.Fori(0, OVER) as it:
                    pe.wait_ge(sem("o_xg"), 16 * it + 16)
                    for k in range(KT):
                        ins = pe.transpose(ps[:, k // 4, (k % 4) * P:(k % 4) * P + R_],
                                           xg[0:R_, 0, k * P:(k + 1) * P], ident[0:R_, 0:R_])
                    ins.then_inc(sem("over_pe"), 1)
                    pe.wait_ge(sem("over_act"), 4 * it + 1)
                    pe.wait_ge(sem("o_w"), 48 * it + 48)
                    for W, b in ((WG, 2), (WU, 3)):
                        for k in range(KT):
                            ins = mm(ps[0:R_, b, :], xgT[0][:, k, 0:R_], W[0][:, k, :], start=k == 0,
                                     stop=k == KT - 1)
                    ins.then_inc(sem("over_pe"), 1)
                    pe.wait_ge(sem("o_h"), it + 1)
                    for k in range(FT):
                        ins = pe.transpose(ps[:, 4, k * P:k * P + R_], hh[0:R_, 0, k * P:(k + 1) * P],
                                           ident[0:R_, 0:R_])
                    ins.then_inc(sem("over_pe"), 1)
                    pe.wait_ge(sem("over_act"), 4 * it + 3)
                    for h in range(2):
                        for k in range(FT):
                            ins = mm(ps[0:R_, 5 + h, :], hT[0][:, k, 0:R_], WD[0][:, k, h * 512:(h + 1) * 512],
                                     start=k == 0, stop=k == FT - 1)
                    ins.then_inc(sem("over_pe"), 1)

        @block.scalar
        def _(act):
            T = Tally(act)
            A = act.activation
            for i in range(5):
                if i == 4:
                    act.wait_ge(sem("xt_ps"), 2)
                for t in (range(4) if i == 0 else (4, ) if i == 4 else ()):
                    src = i_["x_prompt"][0, t * P:(t + 1) * P, :] if t < 4 else i_["xs9"][:, :]
                    act.dma_start(xst[t % 4][0:src.shape[0], :], src).then_inc(sem(f"ld_rows{t % 4}"), 16)
                if i >= 1:
                    for n in ((2 * (i - 1), ) if i < 4 else (6, 8)):
                        act.wait_ge(sem("xt_ps"), n + 1)
                        r = 72 if n == 8 else P
                        T.up(A(xT[:, 0:4, (n // 2) * P:(n // 2) * P + r],
                               ps[:, 5, :].rearrange("p (k c) -> p k c", c=P)[:, :, 0:r], ACT.Copy), "xt_act")

            def scale_mix(ct):
                m = mix_index(ct)
                act.wait_ge(sem("proj"), ct + 1)
                if m >= 2:
                    act.wait_ge(sem("mixed"), m - 1)
                else:
                    act.wait_ge(sem("zeroed"), 3)
                mu = par[:, MU + m:MU + m + 1]
                A(mixtmp[:, m % 2, 1:513], ps[:, ct % 2, :], ACT.Copy, scale=mu)
                T.up(A(mixtmp[:, m % 2, 520:592], ps[:, 2, 0:72], ACT.Copy, scale=mu), "mix_scaled")

            def cols(ct):
                return ps[:, 2, 0:72].rearrange("p (b t) -> p b t", t=9)[:, :, 1:9]

            def evac_att(ct):
                act.wait_ge(sem("proj"), ct + 1)
                n = ct - ATT0
                if n < 4:
                    A(qT[:, n, :], ps[:, ct % 2, :], ACT.Copy, scale=ATT_SCALE)
                    ins = A(qTs[:, :, n, :], cols(ct), ACT.Copy, scale=ATT_SCALE)
                else:
                    d, ds = (kT[:, P:P + NP_], kTs) if n == 4 else (vT[:, 0:NP_], vT[:, NP_:NT])
                    A(d, ps[:, ct % 2, :], ACT.Copy)
                    ins = A(ds.rearrange("p (b t) -> p b t", t=TS), cols(ct), ACT.Copy)
                T.up(ins, "att_evac")

            def lora_act(n):
                kind, j = n // 4, n % 4
                act.wait_ge(sem("lora_ps"), n + 1)
                dst = (SG4, B4, G4)[kind][:, j, :]
                fn = ACT.Copy if kind == 2 else ACT.Sigmoid
                b = 0.0 if kind == 2 else par[:, (W0, A0)[kind] + j:(W0, A0)[kind] + j + 1]
                bank = 3 + 2 * (n % 2)
                T.up(A(dst, ps[:, bank:bank + 2, :].rearrange("p a b -> p (a b)")[:, 0:NT], fn, bias=b), "lora_evac")

            def exps(n):
                act.wait_ge(sem("s_max"), n + 1)
                w = 256 if n < 8 else 192
                Sn = Sb[:, n % 2, 0:4 * w].rearrange("p (g w) -> p g w", g=4)
                st = att_st[:, n % 2]
                for g in range(4):
                    A(Sn[:, g, :], Sn[:, g, :], ACT.Exp, bias=st[:, 1, g:g + 1], accum_out=st[:, 3, g:g + 1])
                T.up(A(st[:, 4, :], st[:, 2, :], ACT.Exp), "exp_done")

            def pt_copy(n):
                act.wait_ge(sem("pt_ps"), 2 * n + 1)
                if n >= 1:
                    act.wait_ge(sem("pv_ps"), n)
                T.up(A(PT[:, 0, :], ps[:, 5, :], ACT.Copy), "pt_act")

            def pv_copy(n):
                act.wait_ge(sem("pv_ps"), n + 1)
                if n == 0:
                    act.wait_ge(sem("rows_zero"), 16 * (OVER * CAP // P))
                if n < 8:
                    nb, kv = n // 2, n % 2
                    r = slice(kv * 64, kv * 64 + 64)
                    ins = A(mixA[r, :, nb * P:(nb + 1) * P], ps[r, 5, :].rearrange("p (g t) -> p g t", g=4), ACT.Copy)
                else:
                    src = ps[:, 5, 0:256].rearrange("p (b g t) -> p g b t", g=4, t=TS)
                    for g in range(4):
                        ins = A(mixA[:, g, NP_:NT].rearrange("p (b t) -> p b t", t=TS), src[:, g], ACT.Copy)
                T.up(ins, "pv_evac")

            def prep_square(j):
                act.wait_ge(sem("kraw"), j + 1)
                if j >= 1:
                    act.wait_ge(sem("prep"), j)
                T.up(A(SQ[:, 0, :], A4[:, j, :], ACT.Square), "hsum_in_a")

            def prep_norm(j):
                act.wait_ge(sem("hsum_ps"), 2 * j + 1)
                A(SQ[:, 0, 0:NP_], ps[:, 7, :], ACT.Sqrt)
                T.up(A(SQ[:, 0, NP_:NT], ps[:, hsum_bank(j), 0:NS], ACT.Sqrt), "norm_read")

            def prep_exps(j):
                act.wait_ge(sem("cum"), 2 * j + 1)
                if j >= 2:
                    act.wait_ge(sem("prep"), j - 1)
                A(PI[:, j % 2, :], PM[:, j % 2, :], ACT.Exp, scale=DECAY_SCALE)
                act.wait_ge(sem("cum"), 2 * j + 2)
                T.up(A(SG4[:, j, :], SG4[:, j, :], ACT.Exp, scale=-DECAY_SCALE), "pexp")
                act.wait_ge(sem("pexp"), 2 * j + 1)
                T.up(A(PM[:, j % 2, :], PM[:, j % 2, :], ACT.Exp, scale=-DECAY_SCALE), "pexp")

            for ct in range(COLT):
                if ct < 2:
                    scale_mix(ct)
                    act.wait_ge(sem("mixed"), ct + 1)
                    if ct == 0:
                        T.up(A(WA[0:64, :], WA[0:64, :], ACT.Tanh), "lora_in")
                    else:
                        T.up(A(GL, GL, ACT.Sigmoid), "lora_in")
                elif ct < 8:
                    lora_act(2 * (ct - 2))
                    evac_att(ct)
                    lora_act(2 * (ct - 2) + 1)
                else:
                    k = ct - RW0
                    scale_mix(ct)
                    if 3 <= k < 12:
                        pv_copy(k - 3)
                    if 2 <= k < 11:
                        pt_copy(k - 2)
                    if k < 9:
                        exps(k)
                    if k >= 3 and k % 3 == 0:
                        prep_norm(k // 3 - 1)
                    if k % 3 == 2:
                        prep_square(k // 3)
                        prep_exps(k // 3)

            def states_in(h):
                act.wait_ge(sem("st_ps"), h + 1)
                if h == 0:
                    act.wait_ge(sem("prep"), 5)
                T.up(A(Z0[:, :, 2 * h:2 * h + 2, :],
                       ps[:, 4 + h, :].rearrange("p (b j v) -> p j b v", b=2, v=HD), ACT.Copy), "st_ev")

            def wy(q):
                R, L = rows(q), levels(q)
                if q == 0:
                    act.wait_ge(sem("kv_out"), 64)
                for n in range(2):
                    act.wait_ge(sem("tok_ps"), 4 * q + n + 1)
                    T.up(A(TOK[n][0:R], ps[0:R, n, :].rearrange("p (u c) -> p u c", u=4), ACT.Copy), "tok_act")
                act.wait_ge(sem("tok_act"), 2 * q + 1)
                if q == 1:
                    prep_norm(3)

                def xt_copy(l, p, bank):
                    act.wait_ge(sem("xt2_ps"), 10 * q + 2 * l + p + 1)
                    if l:
                        act.wait_ge(sem("xl_ps"), 10 * q + 2 * (l - 1) + p + 1)
                    T.up(A(XT[p][0:R, 0:4 * R], ps[0:R, bank, 0:4 * R], ACT.Copy), "xt2_ev")

                for p in range(2):
                    xt_copy(0, p, 6 + p)
                    A(RHS[p].rearrange("p (u c) -> p u c", u=4)[0:R, :, 0:HD], TOK[0][0:R, :, par_rows(p)], ACT.Copy)
                for p in range(2):
                    act.wait_ge(sem("akv_ps"), 2 * q + p + 1)
                    T.up(A(RHS[p].rearrange("p (u c) -> p u c", u=4)[0:R, :, HD:P],
                           ps[0:R, p, 0:256].rearrange("p (u c) -> p u c", u=4), ACT.Copy), "rhs_ev")
                for l in range(1, L):
                    for p in range(2):
                        xt_copy(l, p, 2 + p)
                for p in range(2):
                    act.wait_ge(sem("gh_ps"), 2 * q + p + 1)
                    T.up(A(GH[p][0:R, :], ps[0:R, p, :], ACT.Copy), "gh_ev")
                act.wait_ge(sem("post_ps"), 4 * q + 2)
                T.up(A(units(V4, q), ps[:, 3, 0:4 * R].rearrange("p (u c) -> p u c", u=4), ACT.Copy), "post_act")

            for q in range(4):
                wy(q)
            for h in range(4):
                states_in(h)
            for j in range(4):
                A(SG4[:, j, :], SG4[:, j, :], ACT.Identity, bias=par[:, GNB + j:GNB + j + 1])
            wy(4)
            act.wait_ge(sem("gt_ps"), 1)
            A(GQ[:, :, 0:NS], ps[:, 6, 0:256].rearrange("p (u c) -> p u c", u=4), ACT.Copy)
            act.wait_ge(sem("post_dve"), 21)
            T.up(A(GQ[:, :, NS:P], R4[:, :, NP_:NT], ACT.Copy), "gt_ev")
            for n in range(8):
                act.wait_ge(sem("u_ps"), n + 1)
                T.up(A(YT[n], ps[NS:2 * NS, 4 + n % 2, :], ACT.Copy), "yt_ev")
            def state_copy(b):
                act.wait_ge(sem("so_ps"), b + 1)
                d = souts[b][0:HD, :] if b < NB else GH[1][0:HD, :]
                T.up(A(d, ps[0:HD, 6 + min(b, 7) % 2, :], ACT.Copy), "so_ev")

            def gn_square(j):
                act.wait_ge(sem("centred"), j + 1)
                if j:
                    act.wait_ge(sem("hs_ps"), j)
                T.up(A(SQ[:, 0, :], V4[:, j, :], ACT.Square), "gsq")

            def gn_root(j):
                act.wait_ge(sem("hs_ps"), j + 1)
                if j >= 2:
                    act.wait_ge(sem("gn_y"), j - 1)
                T.up(A(SD[j % 2], ps[:, 2:4, :].rearrange("p a b -> p (a b)")[:, 0:NT], ACT.Sqrt,
                       scale=1.0 / HD, bias=gn_eps), "var_read")

            for b in range(4):
                state_copy(b)
            gn_square(0)
            state_copy(4)
            state_copy(5)
            gn_root(0)
            gn_square(1)
            for b in range(6, NB + 1):
                state_copy(b)
            gn_root(1)
            gn_square(2)
            gn_root(2)
            gn_square(3)
            gn_root(3)

            def root(n, i):
                act.wait_ge(sem(n + "_var"), i + 1)
                r = trows(i)
                T.up(A(lnst[0:r, i % 2, 14:15], lnst[0:r, i % 2, 13:14], ACT.Sqrt, bias=ln_eps[0:r]), n + "_sd")

            def x1t_copy(i):
                r = trows(i)
                act.wait_ge(sem("x1t_ps"), 2 * i + 1)
                if i:
                    act.wait_ge(sem("logit_ps"), i)
                T.up(A(x1T[:, 0:4, 0:r], ps[:, 2, :].rearrange("p (k c) -> p k c", c=P)[:, :, 0:r], ACT.Copy),
                     "x1t_act")

            for i in range(5):
                root("ln1", i)
                if i >= 1:
                    x1t_copy(i - 1)
            x1t_copy(4)
            act.wait_ge(sem("lg_max"), 1)
            T.up(A(PR, PR, ACT.Exp), "lg_exp")
            R_ = CAP

            def xg_copy(e, s, first=False):
                act.wait_ge(sem("xg_turn"), e + 1)
                if not first:
                    act.wait_ge(sem("up_ps"), e - 1)
                T.up(A(xgT[s][:, 0:4, 0:R_], ps[:, 0, :].rearrange("p (k c) -> p k c", c=P)[:, :, 0:R_], ACT.Copy),
                     "xgT_act")

            def silu(e, s, first=False):
                act.wait_ge(sem("gate_ps"), e + 1)
                if not first:
                    act.wait_ge(sem("h_ready"), e - 1)
                T.up(A(sg[0:R_, s, :], ps[0:R_, 2, :], ACT.Silu), "silu")

            def h_copy(e, s, first=False):
                act.wait_ge(sem("ht_ps"), e + 1)
                if not first:
                    act.wait_ge(sem("down_ps"), e - 1)
                T.up(A(hT[s][:, :, 0:R_], ps[:, 4, :].rearrange("p (k c) -> p k c", c=P)[:, :, 0:R_], ACT.Copy),
                     "ht_ready")

            def y_copy(e, s, first=False):
                act.wait_ge(sem("down_ps"), e + 1)
                if not first:
                    act.wait_ge(sem(f"y_st{s}"), e * 8 - 8 * s)
                T.up(A(yst[0:R_, s, 0:512], ps[0:R_, 5, :], ACT.Copy), "y_act")
                act.wait_ge(sem("y_act"), e + 1)
                act.wait_ge(sem("y_dve"), e + 1)
                dst = ysd[e * CAP:(e + 1) * CAP, :] if isinstance(e, int) else ysd[bass.ds(e * CAP, CAP), :]
                act.dma_start(dst, yst[0:R_, s, :]).then_inc(sem(f"y_st{s}"), 16)

            xg_copy(0, 0, True)
            silu(0, 0, True)
            xg_copy(1, 1, True)
            h_copy(0, 0, True)
            silu(1, 1, True)
            xg_copy(2, 0)
            h_copy(1, 1, True)
            y_copy(0, 0, True)
            silu(2, 0)
            xg_copy(3, 1)
            h_copy(2, 0)
            y_copy(1, 1, True)
            silu(3, 1)
            xg_copy(4, 0)
            h_copy(3, 1)
            y_copy(2, 0)
            with act.Fori(2, E // 2 - 1) as it:
                for s in range(2):
                    e = 2 * it + s
                    silu(e, s)
                    xg_copy(e + 1, 1 - s)
                    h_copy(e, s)
                    y_copy(e - 1, 1 - s)
            silu(E - 2, 0)
            xg_copy(E - 1, 1)
            h_copy(E - 2, 0)
            y_copy(E - 3, 1)
            silu(E - 1, 1)
            y_copy(E - 2, 0)
            h_copy(E - 1, 1)
            y_copy(E - 1, 1)
            act.wait_ge(sem("slots"), 2)
            more = act.value_load(flag_i[0:1, :], min_val=0, max_val=OVER)
            with act.If(more > 0):
                act.wait_ge(sem("y_st0"), 8 * E)
                with act.Fori(0, OVER) as it:
                    act.wait_ge(sem("over_pe"), 4 * it + 1)
                    A(xgT[0][:, 0:4, 0:R_], ps[:, 0, :].rearrange("p (k c) -> p k c", c=P)[:, :, 0:R_], ACT.Copy)
                    A(xgT[0][:, 4:8, 0:R_], ps[:, 1, :].rearrange("p (k c) -> p k c", c=P)[:, :, 0:R_], ACT.Copy) \
                        .then_inc(sem("over_act"), 1)
                    act.wait_ge(sem("over_pe"), 4 * it + 2)
                    A(sg[0:R_, 0, :], ps[0:R_, 2, :], ACT.Silu).then_inc(sem("over_act"), 1)
                    act.wait_ge(sem("over_pe"), 4 * it + 3)
                    A(hT[0][:, :, 0:R_], ps[:, 4, :].rearrange("p (k c) -> p k c", c=P)[:, :, 0:R_], ACT.Copy) \
                        .then_inc(sem("over_act"), 1)
                    act.wait_ge(sem("over_pe"), 4 * it + 4)
                    A(yst[0:R_, 0, :], ps[0:R_, 5:7, :].rearrange("p a b -> p (a b)"), ACT.Copy) \
                        .then_inc(sem("over_act"), 1)
                    act.wait_ge(sem("over_act"), 4 * it + 4)
                    act.dma_start(ysd[bass.ds(it * CAP + E * CAP, CAP), :], yst[0:R_, 0, :]) \
                        .then_inc(sem("o_yst"), 16)
                    act.wait_ge(sem("o_yst"), 16 * it + 16)
            for i in range(5):
                root("ln2", i)
                r = trows(i)
                act.wait_ge(sem("ln2_rs"), i + 1)
                T.up(A(x1[0:r, i, :], x1[0:r, i, :], ACT.Identity, scale=lnst[0:r, i % 2, 15:16],
                       bias=lnst[0:r, i % 2, 16:17]), "ln2_nrm")

        @block.vector
        def _(dve):
            T = Tally(dve)
            TT, TSc, STT = dve.tensor_tensor, dve.tensor_scalar, dve.scalar_tensor_tensor
            T.up(dve.memset(mixtmp[:, :, 0:1], 0.0), "zeroed")
            T.up(dve.memset(kT[:, 0:P], 0.0), "zeroed")
            T.up(dve.memset(Vt[:, 0, :], 0.0), "zeroed")
            dve.wait_ge(sem("ld_first"), 32)
            T.link(TSc(par[:, OMU:OMU + 14], par[:, MU:MU + 14], -1.0, 1.0, ALU.mult, ALU.add), "dve_step")
            for n in range(1, 10, 2):
                dve.wait_ge(sem("xt_ps"), n + 1)
                i, r = n // 2, (72 if n == 9 else P)
                T.up(dve.tensor_copy(xT[:, 4:8, i * P:i * P + r],
                                     ps[:, 6, :].rearrange("p (k c) -> p k c", c=P)[:, :, 0:r]), "xt_dve")

            def mix(ct):
                m = mix_index(ct)
                dve.wait_ge(sem("mix_scaled"), m + 1)
                d, omu = mix_dst(m), par[:, OMU + m:OMU + m + 1]
                STT(d[:, 0:NP_], ps[:, ct % 2, :], omu, mixtmp[:, m % 2, 0:512], ALU.mult, ALU.add)
                T.up(STT(d[:, NP_:NT].rearrange("p (b t) -> p b t", t=TS),
                         ps[:, 2, 0:72].rearrange("p (b t) -> p b t", t=9)[:, :, 1:9], omu,
                         mixtmp[:, m % 2, 520:592].rearrange("p (b t) -> p b t", t=9)[:, :, 0:8],
                         ALU.mult, ALU.add), "mixed")

            def kv_tok():
                dve.wait_ge(sem("kv_ps"), 1)
                T.up(dve.tensor_copy(Vt[:, 1:5, :], ps[:, 5, :].rearrange("p (t c) -> p t c", c=P)), "kv_tok")
                dve.wait_ge(sem("kv_ps"), 2)
                dve.tensor_copy(Vs[0:NS, :], ps[0:NS, 6, 0:P])
                dve.tensor_copy(Kt3, ps[:, 6, P:2 * P])
                T.up(dve.tensor_copy(Ks[0:NS, :], ps[0:NS, 6, 2 * P:3 * P]), "kv_tok")
                for h in range(2):
                    dve.wait_ge(sem("kv_ps"), 3 + h)
                    T.up(dve.tensor_copy(kcT[:, 4 * h:4 * h + 4, :], ps[:, 5 + h, :].rearrange("p (b c) -> p b c", c=P)),
                         "kv_tok")

            def row_max(n):
                dve.wait_ge(sem("s_ps"), n + 1)
                if n == 0:
                    dve.wait_ge(sem("ld_const"), 16)
                if n >= 2:
                    dve.wait_ge(sem("pt_ps"), 2 * (n - 1))
                w = 256 if n < 8 else 192
                Sn = Sb[:, n % 2, 0:4 * w].rearrange("p (g w) -> p g w", g=4)
                st = att_st[:, n % 2]
                if n < 8:
                    nb, kv = n // 2, n % 2
                    m = C("band")[:, 256 * (nb > 0):256 * (nb > 0) + 256].unsqueeze(1).to_broadcast([P, 4, 256])
                    T.link(TT(Sn, ps[:, 3:5, :].rearrange("p a (g w) -> p (a g) w", g=2), m, ALU.add), "s_read")
                    sink = par[:, SINK + 4 * kv:SINK + 4 * kv + 4]
                else:
                    dm = C("bandd").rearrange("p (b w) -> p b w", w=192)
                    for kv in range(2):
                        ins = TT(Sn[:, 2 * kv:2 * kv + 2, :],
                                 ps[:, 3 + kv, 0:384].rearrange("p (b w) -> p b w", w=192), dm, ALU.add)
                    T.link(ins, "s_read")
                    sink = par[:, SINKD:SINKD + 2].unsqueeze(2).to_broadcast([P, 2, 2])
                T.link(dve.tensor_reduce(st[:, 0, :], Sn, AX, ALU.max), "dve_step")
                f = (lambda a: a) if n < 8 else (lambda a: a.rearrange("p (k b) -> p k b", k=2))
                T.link(TT(f(st[:, 0, :]), f(st[:, 0, :]), sink, ALU.max), "dve_step")
                T.link(TSc(st[:, 1, :], st[:, 0, :], -1.0, None, ALU.mult), "dve_step")
                T.up(TT(f(st[:, 2, :]), sink, f(st[:, 1, :]), ALU.add), "s_max")

            def normalise(n):
                dve.wait_ge(sem("exp_done"), n + 1)
                w = 256 if n < 8 else 192
                Sn = Sb[:, n % 2, 0:4 * w].rearrange("p (g w) -> p g w", g=4)
                st = att_st[:, n % 2]
                T.link(TT(st[:, 5, :], st[:, 3, :], st[:, 4, :], ALU.add), "dve_step")
                T.link(dve.reciprocal(st[:, 6, :], st[:, 5, :]), "dve_step")
                T.up(TT(Sn, Sn, st[:, 6, :].unsqueeze(2).to_broadcast([P, 4, w]), ALU.mult), "p_ready")

            def pt_copy(n):
                dve.wait_ge(sem("pt_ps"), 2 * n + 2)
                if n >= 1:
                    dve.wait_ge(sem("pv_ps"), n)
                r = P if n < 8 else NS
                T.up(dve.tensor_copy(PT[0:r, 1, :], ps[0:r, 6, :]), "pt_dve")

            def pcol(o, j):
                return par[:, o + j:o + j + 1]

            def prep_a(j):
                if j == 0:
                    dve.wait_ge(sem("lora_evac"), 12)
                if j >= 2:
                    dve.wait_ge(sem("prep"), j - 1)
                T.up(TSc(A4[:, j, :], K4[:, j, :], pcol(KK_, j), None, ALU.mult), "kraw")
                T.link(dve.tensor_tensor_scan(PM[:, j % 2, :], C("reset"), SG4[:, j, :], 0.0, ALU.mult, ALU.add), "cum")
                T.up(TT(SG4[:, j, :], PM[:, j % 2, :], SG4[:, j, :], ALU.subtract), "cum")
                if j >= 1:
                    dve.wait_ge(sem("hsum_ps"), 2 * j)
                s = SQ[:, 1, :]
                T.link(TSc(s, B4[:, j, :], -1.0, pcol(KA, j), ALU.add, ALU.mult), "dve_step")
                T.link(STT(K4[:, j, :], s, 1.0, K4[:, j, :], ALU.add, ALU.mult), "dve_step")
                T.up(STT(s, R4[:, j, :], pcol(RK, j), K4[:, j, :], ALU.mult, ALU.mult), "hsum_in_b")

            def prep_b(j, parts=range(5)):
                s = SQ[:, 0, :]
                if 0 in parts:
                    dve.wait_ge(sem("norm_read"), j + 1)
                    T.link(TSc(s, s, 1e-12, None, ALU.max), "dve_step")
                    T.link(dve.reciprocal(s, s), "dve_step")
                if 1 in parts:
                    T.link(TT(A4[:, j, :], A4[:, j, :], s, ALU.mult), "dve_step")
                    T.link(TT(B4[:, j, :], B4[:, j, :], A4[:, j, :], ALU.mult), "dve_step")
                if 2 in parts:
                    dve.wait_ge(sem("pexp"), 2 * j + 2)
                    TT(R4[:, j, :], R4[:, j, :], PM[:, j % 2, :], ALU.mult)
                    TT(K4[:, j, :], K4[:, j, :], PI[:, j % 2, :], ALU.mult)
                if 3 in parts:
                    TT(B4[:, j, :], B4[:, j, :], PI[:, j % 2, :], ALU.mult)
                    dve.tensor_copy(PL[:, j, 0:8], PM[:, j % 2, CHUNK - 1:NP_:CHUNK])
                    dve.tensor_copy(PL[:, j, 8:16], PM[:, j % 2, NP_ + TS - 1:NT:TS])
                if 4 in parts:
                    T.link(STT(A4[:, j, :], A4[:, j, :], -1.0, SG4[:, j, :], ALU.mult, ALU.mult), "prep")

            def prep_c(j):
                dve.wait_ge(sem("hsum_ps"), 2 * j + 2)
                d = SG4[:, j, :] if j < 3 else SQ[:, 1, :]
                TT(d[:, 0:NP_], ps[:, 7, :], V4[:, j, 0:NP_], ALU.mult)
                T.up(TT(d[:, NP_:NT], ps[:, hsum_bank(j), 0:NS], V4[:, j, NP_:NT], ALU.mult), "bonus_read")

            for ct in range(COLT):
                if ct < 2:
                    mix(ct)
                elif ct < 8:
                    if ct == 7:
                        kv_tok()
                else:
                    k = ct - RW0
                    mix(ct)
                    if 1 <= k < 10:
                        normalise(k - 1)
                    if 2 <= k < 11:
                        pt_copy(k - 2)
                    if k < 9:
                        row_max(k)
                    if k % 3 == 2:
                        prep_a(k // 3)
                    if k >= 3 and k % 3 == 0:
                        prep_b(k // 3 - 1, range(2))
                    if k >= 4 and k % 3 == 1:
                        prep_b(k // 3 - 1, range(2, 5))
                        prep_c(k // 3 - 1)
            T.up(dve.memset(gn_eps, GN_EPS), "zeroed")

            def wy(q):
                R, L = rows(q), levels(q)
                tag = "" if q < 4 else "_s"
                if q == 0:
                    dve.wait_ge(sem("kv_out"), 64)
                    dve.wait_ge(sem("pv_ps"), 9)
                up4 = C("upper" + tag)[0:R]
                lev = C("level").rearrange("p (l c) -> p l c", l=6)

                def b4(a):
                    return a[0:R, 0:4 * R].rearrange("p (u c) -> p u c", u=4)

                def lv(l):
                    return lev[0:R, l, 0:R].unsqueeze(1).to_broadcast([R, 4, R])

                for n in range(2, 4):
                    dve.wait_ge(sem("tok_ps"), 4 * q + n + 1)
                    T.up(dve.tensor_copy(TOK[n][0:R], ps[0:R, n, :].rearrange("p (u c) -> p u c", u=4)), "tok_dve")
                for p in range(2):
                    dve.wait_ge(sem("n_ps"), 2 * q + p + 1)
                    T.link(TT(b4(X[p]), b4(ps[:, 4 + p, :]), lv(0), ALU.mult), "dve_step")
                    T.up(TT(b4(X[p]), b4(X[p]), ident[0:R, 0:R].unsqueeze(1).to_broadcast([R, 4, R]), ALU.add),
                         "x_ready")
                if q == 1:
                    prep_c(3)
                for G, pn, en in ((BG, "bg_ps", "bg_ev"), (KG, "kg_ps", "kg_ev")):
                    for p in range(2):
                        dve.wait_ge(sem(pn), 2 * q + p + 1)
                        T.up(TT(G[p][0:R, 0:8 * R].rearrange("p (a b) -> p a b", a=2),
                                ps[0:R, 2 * p:2 * p + 2, 0:4 * R],
                                up4.unsqueeze(1).to_broadcast([R, 2, 4 * R]), ALU.mult), en)
                for l in range(1, L + 1):
                    for p in range(2):
                        dve.wait_ge(sem("w1_ps"), 10 * q + 2 * (l - 1) + p + 1)
                        if l > 1:
                            dve.wait_ge(sem("xl_ps"), 10 * q + 2 * (l - 2) + p + 1)
                        T.up(TT(b4(W1[p]), b4(ps[:, 4 + p, :]), lv(l), ALU.mult), "w1_ev")
                    if q == 1:
                        prep_b(3, (l - 1, ))
                        if l == 5:
                            dve.wait_ge(sem("bonus_read"), 4)
                            T.link(dve.tensor_copy(SG4[:, 3, :], SQ[:, 1, :]), "prep")
                    for p in range(2):
                        dve.wait_ge(sem("xl_ps"), 10 * q + 2 * (l - 1) + p + 1)
                        if l < L:
                            T.up(TT(b4(X[p]), b4(ps[:, 6 + p, :]), b4(X[p]), ALU.add), "x_ready")
                        else:
                            T.up(TT(b4(XT[p]), b4(ps[:, 6 + p, :]), b4(XT[p]), ALU.add), "t_ready")
                dve.wait_ge(sem("post_ps"), 4 * q + 1)
                T.up(TT(units(R4, q), ps[:, 2, 0:4 * R].rearrange("p (u c) -> p u c", u=4), units(R4, q), ALU.add),
                     "post_dve")
                if q == 4:
                    return
                dve.wait_ge(sem("post_ps"), 4 * q + 3)
                for cp in range(2):
                    T.up(TT(A4[:, q, 0:NP_].rearrange("p (u c k) -> p u c k", u=4, c=2)[:, :, cp, :],
                            ps[:, 6 + cp, 0:256].rearrange("p (u k) -> p u k", u=4),
                            C("ident2").unsqueeze(1).to_broadcast([P, 4, HD]), ALU.add), "post_dve")
                dve.wait_ge(sem("post_ps"), 4 * q + 4)
                for cp in range(2):
                    T.up(TT(B4[:, q, 0:NP_].rearrange("p (u c k) -> p u c k", u=4, c=2)[:, :, cp, :],
                            ps[:, 4 + cp, 0:256].rearrange("p (u k) -> p u k", u=4),
                            PL[:, q, cp:8:2].unsqueeze(2).to_broadcast([P, 4, HD]), ALU.mult), "post_dve")

            for q in range(5):
                wy(q)

            batch = C("batch")[0:NS].unsqueeze(2).to_broadcast([NS, NB, HD])

            def bv(a):
                return a[0:NS, :].rearrange("p (b v) -> p b v", b=NB)

            def z1_copy(u):
                dve.wait_ge(sem("z1_ps"), 2 * u + 2)
                Zu = Z0[:, u]
                T.link(TT(Zu, ps[:, 6 + u % 2, :].rearrange("p (b v) -> p b v", b=NB), Zu, ALU.add), "dve_step")
                T.up(TT(Zu, Zu, PL[:, u, 8:16].unsqueeze(2).to_broadcast([P, NB, HD]), ALU.mult), "z1_ev")

            def z_step(c):
                dve.wait_ge(sem("z_ps"), c)
                T.link(TT(Zp[:, c], ps[:, 1, 0:256].rearrange("p (j v) -> p j v", j=4),
                          PL[:, :, c:c + 1].to_broadcast([P, 4, HD]), ALU.mult), "dve_step")
                T.up(TT(Zp[:, c], Zp[:, c], B4[:, :, c * HD:(c + 1) * HD], ALU.add), "z_ready")

            for n in range(8):
                u, p = n // 2, n % 2
                dve.wait_ge(sem("u_ps"), n + 1)
                if n >= 2:
                    dve.wait_ge(sem("z1_ps"), n - 1)
                H = GH[p][0:NS, u * P + HD:(u + 1) * P].unsqueeze(1).to_broadcast([NS, NB, HD])
                T.link(TT(bv(W1[p]), bv(ps[:, 4 + p, :]), H, ALU.add), "dve_step")
                TT(bv(NM[p]), TOK[3][0:NS, u, par_rows(p)].unsqueeze(1).to_broadcast([NS, NB, HD]), batch, ALU.mult)
                T.up(TT(bv(W1[p]), bv(W1[p]), batch, ALU.mult), "um_ev")
                if n >= 1:
                    z_step(n)
                if p == 0 and u >= 1:
                    z1_copy(u - 1)
            z1_copy(3)

            for j in range(4):
                dve.wait_ge(sem("y_ps"), j + 1)
                T.up(TT(V4[:, j, CHUNK:NP_], ps[:, (4, 5, 2, 3)[j], CHUNK:NP_], V4[:, j, CHUNK:NP_], ALU.add), "y_ev")

            dve.wait_ge(sem("ys_ps"), 1)
            dve.wait_ge(sem("post_act"), 5)
            T.up(TT(V4[:, :, NP_:NT], ps[:, 0, 0:256].rearrange("p (u t) -> p u t", u=4), V4[:, :, NP_:NT], ALU.add),
                 "ys_ev")

            def centre(j):
                y = V4[:, j, :]
                dve.wait_ge(sem("hm_ps"), j + 1)
                T.up(STT(y, ps[:, 0:2, :].rearrange("p a b -> p (a b)")[:, 0:NT], -1.0 / HD, y, ALU.mult, ALU.add),
                     "centred")

            def scale_heads(j):
                y, s = V4[:, j, :], SD[j % 2]
                dve.wait_ge(sem("centred"), j + 1)
                dve.wait_ge(sem("var_read"), j + 1)
                T.link(dve.reciprocal(s, s), "dve_step")
                T.up(STT(y, y, pcol(GNG, j), s, ALU.mult, ALU.mult), "gn_y")

            dve.wait_ge(sem("y_ev"), 4)
            centre(0)
            for j in range(1, 4):
                centre(j)
                scale_heads(j - 1)
            scale_heads(3)

            T.up(dve.memset(ln_eps, LN_EPS), "zeroed")
            T.up(dve.memset(rt[:, :, :], 0.0), "zeroed")
            dve.wait_ge(sem("zeroed"), 6)

            def norm(i, n, lnp):
                r = trows(i)
                x, st = x1[0:r, i, :], lnst[0:r, i % 2]
                for h in range(2):
                    ins = dve.bn_stats(st[:, 6 * h:6 * h + 6], x[:, h * 512:(h + 1) * 512])
                T.link(ins, "dve_step")
                T.up(dve.bn_aggr(st[:, 12:14], st[:, 0:12]), n + "_var")
                dve.wait_ge(sem("ln1_sd"), i + 1)
                T.link(dve.reciprocal(st[:, 15:16], st[:, 14:15]), "dve_step")
                T.link(TSc(x, x, st[:, 12:13], st[:, 15:16], ALU.subtract, ALU.mult), "dve_step")
                T.link(TT(x, x, lnp[0:r, 0, :], ALU.mult), "dve_step")
                T.up(TT(x, x, lnp[0:r, 1, :], ALU.add), "x1_ready")

            def x1t_copy(i):
                r = trows(i)
                dve.wait_ge(sem("x1t_ps"), 2 * i + 2)
                if i:
                    dve.wait_ge(sem("logit_ps"), i)
                T.up(dve.tensor_copy(x1T[:, 4:8, 0:r], ps[:, 3, :].rearrange("p (k c) -> p k c", c=P)[:, :, 0:r]),
                     "x1t_dve")

            def lg_copy(i):
                r = trows(i)
                dve.wait_ge(sem("logit_ps"), i + 1)
                T.up(dve.tensor_copy(rt[0:r, i, :], ps[0:r, 0, 0:E]), "lg_ev")

            dve.wait_ge(sem("ld_norm"), 32)
            for i in range(5):
                r = trows(i)
                dve.wait_ge(sem("op_ps"), i + 1)
                dve.wait_ge(sem(f"ld_rows{i % 2}"), 16 * ((2, 1)[i % 2] + i // 2 + 1))
                T.link(STT(x1[0:r, i, :], xres[0:r, i % 2, :], ALPHA,
                           ps[0:r, 4 + 2 * (i % 2):6 + 2 * (i % 2), :].rearrange("p a b -> p (a b)"), ALU.mult, ALU.add),
                       "pre_ln")
                norm(i, "ln1", ln1)
                if i >= 1:
                    x1t_copy(i - 1)
                if i >= 2:
                    lg_copy(i - 2)
            lg_copy(3)
            x1t_copy(4)
            lg_copy(4)

            R_ = CAP

            def xg_copy(e, s, first=False):
                dve.wait_ge(sem("xg_turn"), e + 1)
                if not first:
                    dve.wait_ge(sem("up_ps"), e - 1)
                T.up(dve.tensor_copy(xgT[s][:, 4:8, 0:R_], ps[:, 1, :].rearrange("p (k c) -> p k c", c=P)[:, :, 0:R_]),
                     "xgT_dve")

            L = lambda ins: T.link(ins, "dve_step")
            def bE(a):
                return a.unsqueeze(2).to_broadcast([P, 5, E])
            def q4(a):
                return a.rearrange("p i (g e) -> p (i g) e", g=4)
            def f20(a):
                return a.rearrange("p i g -> p (i g)")
            def b4_(a):
                return f20(a).unsqueeze(2).to_broadcast([P, 20, 4])
            iota20 = C("iota4").unsqueeze(1).to_broadcast([P, 20, 4])
            iota5 = C("iota4").unsqueeze(1).to_broadcast([P, 5, 4])
            dve.wait_ge(sem("lg_ev"), 5)
            L(dve.tensor_reduce(S5[:, 0, :], rt[:, :, :], AX, ALU.max))
            T.up(TT(PR, rt[:, :, :], bE(S5[:, 0, :]), ALU.subtract), "lg_max")
            dve.tensor_copy(BEF, C("before"))
            dve.tensor_copy(ONE, C("ones"))
            L(dve.memset(CH[:, 5, :], 0.0))
            dve.wait_ge(sem("lg_exp"), 1)
            L(dve.tensor_reduce(S5[:, 1, :], PR, AX, ALU.add))
            L(dve.reciprocal(S5[:, 2, :], S5[:, 1, :]))
            L(TT(PR, PR, bE(S5[:, 2, :]), ALU.mult))
            L(TT(SEL, PR, par[:, RB:RB + E].unsqueeze(1).to_broadcast([P, 5, E]), ALU.add))

            def first_max(v, m, c, hot, bm, io):
                L(dve.tensor_reduce(m, v, AX, ALU.max))
                L(TT(c, v, bm(m), ALU.is_equal))
                L(STT(c, c, -8.0, io, ALU.mult, ALU.add))
                L(dve.tensor_reduce(f20(C1) if hot is not BGR else S5[:, 4, :], c, AX, ALU.min))
                return c

            b20 = lambda m: m.unsqueeze(2).to_broadcast([P, 20, 4])
            first_max(q4(SEL), f20(G1), q4(CN), O1, b20, iota20)
            L(TT(q4(O1), q4(CN), b4_(C1), ALU.is_equal))
            L(STT(SEL, O1, NEG, SEL, ALU.mult, ALU.add))
            first_max(q4(SEL), f20(G2), q4(CN), O2, b20, iota20)
            L(TT(q4(O2), q4(CN), b4_(C1), ALU.is_equal))
            L(TT(SC, G1, G2, ALU.add))
            b5 = lambda m: m.unsqueeze(2).to_broadcast([P, 5, 4])
            first_max(SC, S5[:, 3, :], CNB, BGR, b5, iota5)
            L(TT(BGR, CNB, b5(S5[:, 4, :]), ALU.is_equal))
            L(TT(BGR, BGR, C("valid").unsqueeze(2).to_broadcast([P, 5, 4]), ALU.mult))
            L(TT(q4(M1), q4(O1), b4_(BGR), ALU.mult))
            L(TT(q4(M2), q4(O2), b4_(BGR), ALU.mult))
            T.up(TT(CH[:, 0:5, :], M1, M2, ALU.add), "chosen")
            for n, M in ((0, M1), (1, M2)):
                for h, part in enumerate(("tok_high", "tok_low")):
                    L(TT(TI[n][:, :, h, :], M, C(part).unsqueeze(2).to_broadcast([P, 5, E]), ALU.mult))
            dve.wait_ge(sem("route_ps"), 1)
            L(dve.tensor_copy(CN, ps[:, RANKB, 0:5 * E].rearrange("p (i e) -> p i e", e=E)))
            for n, M in ((0, M1), (1, M2)):
                L(TT(EQ, M, CN, ALU.mult))
                L(dve.tensor_reduce(S5[:, n, :], EQ, AX, ALU.add))
                T.up(TT(OH[n], C("rank").unsqueeze(1).to_broadcast([P, 5, P]),
                        S5[:, n, :].unsqueeze(2).to_broadcast([P, 5, P]), ALU.is_equal), "chosen")
            L(dve.tensor_copy(CT, ps[:, RANKB, 5 * E:6 * E]))
            dve.wait_ge(sem("route_ps"), 2)
            T.up(dve.tensor_copy(idx_i[0:CAP, 0:E], ps[0:CAP, 2, 0:E]), "slots")
            for n, M in ((0, M1), (1, M2)):
                L(TT(EQ, M, PR, ALU.mult))
                L(dve.tensor_reduce(S5[:, 6 + n, :], EQ, AX, ALU.add))
            L(TT(S5[:, 5, :], S5[:, 6, :], S5[:, 7, :], ALU.add))
            L(TT(S5[:, 5, :], S5[:, 5, :], C("spare"), ALU.add))
            L(dve.reciprocal(S5[:, 8, :], S5[:, 5, :]))
            for n in range(2):
                L(TT(S5[:, 9 + n, :], S5[:, 6 + n, :], S5[:, 8, :], ALU.mult))
            L(TSc(NV, CT, float(CAP), None, ALU.is_gt))
            for n in range(2, (NT + CAP - 1) // CAP):
                L(STT(NV, CT, float(n * CAP), NV, ALU.is_gt, ALU.add))
            L(TT(TR, C("tri").rearrange("p (a b) -> p a b", b=E), NV.unsqueeze(1).to_broadcast([P, E, E]), ALU.mult))
            L(dve.tensor_reduce(ST, TR, AX, ALU.add))
            L(TSc(B2, ST, float(CAP), float((E - 1) * CAP), ALU.mult, ALU.add))
            L(TT(B2, B2, C("slot0"), ALU.subtract))
            bi = lambda a: a.unsqueeze(1).to_broadcast([P, 5, E])
            xg_copy(0, 0, True)
            L(TSc(PO, CN, float(CAP), None, ALU.is_ge))
            L(TT(PO, PO, bi(B2), ALU.mult))
            L(TT(PO, PO, CN, ALU.add))
            L(TT(PO, PO, bi(C("slot0")), ALU.add))
            for n, M in ((0, M1), (1, M2)):
                L(TT(EQ, M, PO, ALU.mult))
                L(dve.tensor_reduce(S5[:, n, :], EQ, AX, ALU.add))
                L(dve.tensor_copy(slot_i[:, :, n], S5[:, n, :]))
            L(dve.tensor_reduce(S5[:, 11, 0:1], NV, AX, ALU.add))
            L(dve.tensor_copy(flag_i, S5[:, 11, 0:1]))
            L(TT(IT, ST.unsqueeze(1).to_broadcast([P, OVER, E]), C("item").unsqueeze(2).to_broadcast([P, OVER, E]),
                 ALU.is_le))
            L(dve.tensor_reduce(IV[:, 0, 0:OVER], IT, AX, ALU.add))
            L(TSc(IV[:, 1, 0:OVER], IV[:, 0, 0:OVER], -1.0, None, ALU.add))
            T.link(dve.tensor_copy(eid_i, IV[:, 1, 0:OVER]), "slots")

            def h_mul(e, s, first=False):
                dve.wait_ge(sem("silu"), e + 1)
                dve.wait_ge(sem("up_ps"), e + 1)
                if not first:
                    dve.wait_ge(sem("ht_ps"), e - 1)
                T.up(TT(hh[0:R_, s, :], sg[0:R_, s, :], ps[0:R_, 3, :], ALU.mult), "h_ready")

            def y_copy(e, s, first=False):
                dve.wait_ge(sem("down_ps"), e + 1)
                if not first:
                    dve.wait_ge(sem(f"y_st{s}"), e * 8 - 8 * s)
                T.up(dve.tensor_copy(yst[0:R_, s, 512:D], ps[0:R_, 6, :]), "y_dve")

            dve.wait_ge(sem("x1_st"), 80)
            for i in range(5):
                r = trows(i)
                T.up(TSc(x1[0:r, i, :], x1[0:r, i, :], ALPHA, None, ALU.mult), "dve_step")
            scaled = T.n["dve_step"]
            h_mul(0, 0, True)
            xg_copy(1, 1, True)
            h_mul(1, 1, True)
            xg_copy(2, 0)
            y_copy(0, 0, True)
            h_mul(2, 0)
            xg_copy(3, 1)
            y_copy(1, 1, True)
            h_mul(3, 1)
            xg_copy(4, 0)
            y_copy(2, 0)
            with dve.Fori(2, E // 2 - 1) as it:
                for s in range(2):
                    e = 2 * it + s
                    h_mul(e, s)
                    xg_copy(e + 1, 1 - s)
                    y_copy(e - 1, 1 - s)
            h_mul(E - 2, 0)
            xg_copy(E - 1, 1)
            y_copy(E - 3, 1)
            h_mul(E - 1, 1)
            y_copy(E - 2, 0)
            y_copy(E - 1, 1)
            more = dve.value_load(flag_i[0:1, :], min_val=0, max_val=OVER)
            with dve.If(more > 0):
                with dve.Fori(0, OVER) as it:
                    dve.wait_ge(sem("over_act"), 4 * it + 2)
                    TT(hh[0:R_, 0, :], sg[0:R_, 0, :], ps[0:R_, 3, :], ALU.mult).then_inc(sem("o_h"), 1)
            dve.wait_ge(sem("dve_step"), scaled)
            for i in range(6):
                if i < 5:
                    r = trows(i)
                    x, st = x1[0:r, i, :], lnst[0:r, i % 2]
                    dve.wait_ge(sem(f"yab{min(i, 2)}"), 32 if i < 2 else 96)
                    T.link(STT(x, yab[0:r, i, 0, :], S5[0:r, 9, i:i + 1], x, ALU.mult, ALU.add), "dve_step")
                    T.link(STT(x, yab[0:r, i, 1, :], S5[0:r, 10, i:i + 1], x, ALU.mult, ALU.add), "dve_step")
                    if i >= 2:
                        dve.wait_ge(sem("ln2_nrm"), i - 1)
                    for h in range(2):
                        ins = dve.bn_stats(st[:, 6 * h:6 * h + 6], x[:, h * 512:(h + 1) * 512])
                    T.link(ins, "dve_step")
                    T.up(dve.bn_aggr(st[:, 12:14], st[:, 0:12]), "ln2_var")
                if i >= 1:
                    st = lnst[0:trows(i - 1), (i - 1) % 2]
                    dve.wait_ge(sem("ln2_sd"), i)
                    T.link(dve.reciprocal(st[:, 15:16], st[:, 14:15]), "dve_step")
                    T.up(STT(st[:, 16:17], st[:, 12:13], -1.0, st[:, 15:16], ALU.mult, ALU.mult), "ln2_rs")
            dve.wait_ge(sem("ld_norm"), 64)
            for i in range(3, 5):
                x, r = x1[0:trows(i), i, :], trows(i)
                dve.wait_ge(sem("ln2_nrm"), i + 1)
                T.link(TT(x, x, ln2[0:r, 0, :], ALU.mult), "dve_step")
                T.up(TT(x, x, ln2[0:r, 1, :], ALU.add), "y_last")


def kernel(**inputs):
    import concourse.bacc as _bacc
    from concourse.bass_utils import run_bass_kernel_spmd as _run

    a = {k: np.asarray(v) for k, v in inputs.items()}
    q = [np.r_[j * 64:j * 64 + 64, 256 + j * 64:256 + j * 64 + 64] for j in range(4)]
    rw = 768
    wa = np.r_[rw + 512:rw + 576, rw + 1600:rw + 1664]
    gl = np.arange(rw + 1664, rw + 1792)
    rwkv = [rw + o + j * 128 + np.arange(128) for j in range(4) for o in (0, 576, 1088)]
    tiles = [wa, gl] + q + [np.arange(512, 640), np.arange(640, 768)] + rwkv
    perm = np.concatenate(tiles)
    win = a["w_in"][0][:, perm].reshape(KT, P, COLT, P).transpose(2, 1, 0, 3).reshape(COLT, P, KT * P)
    mu = a["mu_rwkv"][0][np.concatenate([wa, gl] + rwkv) - rw].reshape(14, P).T
    vec = [a[n].reshape(4, P).T for n in ("decay_w0", "aaa_a0", "k_k", "k_a", "r_k", "gn_g", "gn_b")]
    sinks = a["sinks"][0]
    sd = np.stack([np.tile(np.repeat(sinks[kv * 4:kv * 4 + 4], 8), 4) for kv in range(2)], 1)
    params = np.concatenate([mu, np.zeros_like(mu)] + vec + [np.tile(sinks[None], (P, 1)), sd,
                             np.tile(a["router_bias"][None], (P, 1))], 1)
    table = constant_table()
    arrays = {
        "consts": np.concatenate([table[k] for k in CAT], 1),
        "params": params, "win": win,
        "xs9": np.concatenate([a["state_shift"][0][:, None], a["x_sample"]], 1).reshape(72, D),
    }
    wo = a["w_o"][0]
    rows_ = np.concatenate(q + [512 + np.arange(512)])
    arrays["wo"] = wo[rows_].reshape(KT, P, D).transpose(1, 0, 2).reshape(P, KT * D)
    arrays["tokid"] = (np.arange(5)[None] * P + np.arange(P)[:, None]).astype(np.int32)
    for n in ("x_prompt", "x_sample", "state_wkv", "w_router", "w_gate", "w_up", "w_down", "ln1_g", "ln1_b",
              "ln2_g", "ln2_b", "cache_k", "cache_v", "decay_w2", "aaa_a2", "gate_g2"):
        arrays[n] = a[n]
    nc = _bacc.Bacc("TRN2", target_bir_lowering=False, num_devices=1)
    arrays = {f"in_{k}": np.ascontiguousarray(v) for k, v in arrays.items()}
    i_ = {k[3:]: nc.dram_tensor(k, v.shape, mybir.dt.from_np(v.dtype), kind="ExternalInput").ap()
          for k, v in arrays.items()}
    o_ = {n: nc.dram_tensor("out_" + n, s, F32, kind="ExternalOutput").ap() for n, s in OUTS}
    hymba_step(nc, i_, o_)
    r = _run(nc, [arrays], core_ids=[0])
    return tuple(r.results[0]["out_" + n] for n, _ in OUTS)
```
